# Optimizing a Trainium2 kernel written in Bass

```python
import math
import jax
import jax.numpy as jnp
from jax import lax
import numpy as np

D_MODEL = 1024
BATCH = 1
SEQ = 512
DEPTH = 2

N_META = 16
BLOCK_Q = 128
MIX_WIDTH = D_MODEL // 2
V_HEAD_DIM = 64
MLA_HEADS = MIX_WIDTH // V_HEAD_DIM
QK_NOPE_DIM = 64
QK_ROPE_DIM = 32
QK_HEAD_DIM = QK_NOPE_DIM + QK_ROPE_DIM
Q_LORA_RANK = 3 * D_MODEL // 8
KV_LORA_RANK = D_MODEL // 4
ROPE_BASE = 10000.0
CONV_WIDTH = MIX_WIDTH
CONV_K = 3
S5_WIDTH = MIX_WIDTH
S5_GROUP = 16
S5_GROUPS = S5_WIDTH // S5_GROUP
S5_STATE = 64
N_BRANCH = 3
D_FF = 128 * ((8 * D_MODEL // 3 + 127) // 128)
ALPHA = (2.0 * DEPTH) ** 0.25
BETA = (8.0 * DEPTH) ** -0.25
LN_EPS = 1e-5
RMS_EPS = 1e-6
IN_SPLITS = (Q_LORA_RANK, KV_LORA_RANK, QK_ROPE_DIM, CONV_WIDTH, CONV_WIDTH, CONV_WIDTH, S5_WIDTH, N_BRANCH * D_MODEL)
D_IN = sum(IN_SPLITS)

kernel_name = "hybrid_mla_shortconv_s5_deepnorm_macaron"

def layer_norm(x, g, b):
    xf = x.astype(jnp.float32)
    mu = jnp.mean(xf, axis=-1, keepdims=True)
    var = jnp.mean(jnp.square(xf - mu), axis=-1, keepdims=True)
    y = (xf - mu) * lax.rsqrt(var + LN_EPS) * g.astype(jnp.float32) + b.astype(jnp.float32)
    return y.astype(x.dtype)

def rms_norm(x, g):
    xf = x.astype(jnp.float32)
    y = xf * lax.rsqrt(jnp.mean(jnp.square(xf), axis=-1, keepdims=True) + RMS_EPS) * g.astype(jnp.float32)
    return y.astype(x.dtype)

def swiglu(x, w_gate, w_up, w_down):
    return (jax.nn.silu(x @ w_gate) * (x @ w_up)) @ w_down

def rope(x, pos):
    d = x.shape[-1]
    inv_freq = ROPE_BASE ** (-jnp.arange(0, d, 2, dtype=jnp.float32) / d)
    ang = pos.astype(jnp.float32)[:, None] * inv_freq[None, :]
    cos = jnp.cos(ang)[None, :, None, :]
    sin = jnp.sin(ang)[None, :, None, :]
    xf = x.astype(jnp.float32)
    x1, x2 = xf[..., : d // 2], xf[..., d // 2:]
    return jnp.concatenate([x1 * cos - x2 * sin, x2 * cos + x1 * sin], axis=-1).astype(x.dtype)

def mla_branch(c_q_raw, c_kv_raw, k_rope_raw, q_norm_g, w_uq, kv_norm_g, w_ukv, w_out):
    B, L, _ = c_q_raw.shape
    pos = jnp.arange(L)
    q = (rms_norm(c_q_raw, q_norm_g) @ w_uq).reshape(B, L, MLA_HEADS, QK_HEAD_DIM)
    kv = (rms_norm(c_kv_raw, kv_norm_g) @ w_ukv).reshape(B, L, MLA_HEADS, QK_NOPE_DIM + V_HEAD_DIM)
    q = jnp.concatenate([q[..., :QK_NOPE_DIM], rope(q[..., QK_NOPE_DIM:], pos)], axis=-1)
    k_rope = rope(k_rope_raw[:, :, None, :], pos)
    k = jnp.concatenate([kv[..., :QK_NOPE_DIM], jnp.broadcast_to(k_rope, (B, L, MLA_HEADS, QK_ROPE_DIM))], axis=-1)
    v = kv[..., QK_NOPE_DIM:]
    pad = (-L) % BLOCK_Q
    padw = ((0, 0), (pad, 0), (0, 0), (0, 0))
    q, k, v = jnp.pad(q, padw), jnp.pad(k, padw), jnp.pad(v, padw)
    n_blocks = (L + pad) // BLOCK_Q
    scale = QK_HEAD_DIM ** -0.5
    outs = []
    for i in range(n_blocks):
        kend = (i + 1) * BLOCK_Q
        qs = q[:, i * BLOCK_Q: kend]
        s = jnp.einsum('bqhd,bkhd->bhqk', qs, k[:, :kend]).astype(jnp.float32) * scale
        qi = i * BLOCK_Q + jnp.arange(BLOCK_Q)
        ki = jnp.arange(kend)
        mask = (ki[None, :] <= qi[:, None]) & (ki[None, :] >= pad)
        s = jnp.where(mask[None, None], s, -1e30)
        p = jax.nn.softmax(s, axis=-1).astype(v.dtype)
        outs.append(jnp.einsum('bhqk,bkhd->bqhd', p, v[:, :kend]))
    o = jnp.concatenate(outs, axis=1)[:, pad:]
    return o.reshape(B, L, MLA_HEADS * V_HEAD_DIM) @ w_out

def short_conv_branch(xbar, b_gate, c_gate, conv_w, conv_b, w_out):
    L = xbar.shape[1]
    u = c_gate * xbar
    up = jnp.pad(u, ((0, 0), (CONV_K - 1, 0), (0, 0)))
    y = conv_b + sum(conv_w[j] * up[:, j: j + L] for j in range(CONV_K))
    return (b_gate * y) @ w_out

def _ssm_combine(e1, e2):
    a1r, a1i, b1r, b1i = e1
    a2r, a2i, b2r, b2i = e2
    ar = a2r * a1r - a2i * a1i
    ai = a2r * a1i + a2i * a1r
    br = a2r * b1r - a2i * b1i + b2r
    bi = a2r * b1i + a2i * b1r + b2i
    return (ar, ai, br, bi)

def s5_branch(u, a_re, a_im, log_dt, b_re, b_im, c_re, c_im, d, w_glu, b_glu, w_out):
    B, L, _ = u.shape
    f32 = jnp.float32
    uf = u.astype(f32).reshape(B, L, S5_GROUPS, S5_GROUP)
    a_re, a_im = a_re.astype(f32), a_im.astype(f32)
    dt = jnp.exp(log_dt.astype(f32))[:, None]
    mag = jnp.exp(dt * a_re)
    ab_re, ab_im = mag * jnp.cos(dt * a_im), mag * jnp.sin(dt * a_im)
    den = a_re * a_re + a_im * a_im
    nr, ni = ab_re - 1.0, ab_im
    coef_re = (nr * a_re + ni * a_im) / den
    coef_im = (ni * a_re - nr * a_im) / den
    b_re, b_im = b_re.astype(f32), b_im.astype(f32)
    bb_re = coef_re[..., None] * b_re - coef_im[..., None] * b_im
    bb_im = coef_re[..., None] * b_im + coef_im[..., None] * b_re
    bu_re = jnp.einsum('gnh,blgh->blgn', bb_re, uf)
    bu_im = jnp.einsum('gnh,blgh->blgn', bb_im, uf)
    shp = (1, L, S5_GROUPS, S5_STATE)
    elems = (jnp.broadcast_to(ab_re[None, None], shp), jnp.broadcast_to(ab_im[None, None], shp), bu_re, bu_im)
    _, _, xr, xi = lax.associative_scan(_ssm_combine, elems, axis=1)
    y = (jnp.einsum('ghn,blgn->blgh', c_re.astype(f32), xr)
         - jnp.einsum('ghn,blgn->blgh', c_im.astype(f32), xi)
         + d.astype(f32) * uf)
    y = jax.nn.gelu(y.reshape(B, L, S5_WIDTH).astype(u.dtype))
    y = y * jax.nn.sigmoid(y @ w_glu + b_glu)
    return y @ w_out

def hybrid_layer(x, ffn1_w_gate, ffn1_w_up, ffn1_w_down, ln1_g, ln1_b, w_in,
                 mla_q_norm_g, mla_w_uq, mla_kv_norm_g, mla_w_ukv, mla_w_o,
                 conv_w, conv_b, conv_w_out,
                 s5_a_re, s5_a_im, s5_log_dt, s5_b_re, s5_b_im, s5_c_re, s5_c_im, s5_d, s5_w_glu, s5_b_glu, s5_w_out,
                 w_o, ln2_g, ln2_b, ffn2_w_gate, ffn2_w_up, ffn2_w_down, ln3_g, ln3_b):
    B, L, _ = x.shape
    x = layer_norm(ALPHA * x + 0.5 * swiglu(x, ffn1_w_gate, ffn1_w_up, ffn1_w_down), ln1_g, ln1_b)
    proj = x @ w_in
    c_q, c_kv, k_rope, xbar, b_gate, c_gate, u_s5, gates = jnp.split(proj, np.cumsum(IN_SPLITS)[:-1].tolist(), axis=-1)
    y_a = mla_branch(c_q, c_kv, k_rope, mla_q_norm_g, mla_w_uq, mla_kv_norm_g, mla_w_ukv, mla_w_o)
    y_b = short_conv_branch(xbar, b_gate, c_gate, conv_w, conv_b, conv_w_out)
    y_c = s5_branch(u_s5, s5_a_re, s5_a_im, s5_log_dt, s5_b_re, s5_b_im, s5_c_re, s5_c_im, s5_d, s5_w_glu, s5_b_glu, s5_w_out)
    g = jax.nn.sigmoid(gates.reshape(B, L, N_BRANCH, D_MODEL))
    mixed = g[:, :, 0] * y_a + g[:, :, 1] * y_b + g[:, :, 2] * y_c
    x = layer_norm(ALPHA * x + mixed @ w_o, ln2_g, ln2_b)
    x = layer_norm(ALPHA * x + 0.5 * swiglu(x, ffn2_w_gate, ffn2_w_up, ffn2_w_down), ln3_g, ln3_b)
    return x

def setup_inputs(seed: int = 0) -> dict:
    key = jax.random.key(seed)
    keys = iter(jax.random.split(key, 48))
    f32 = jnp.float32

    def nrm(shape, scale):
        return jax.random.normal(next(keys), shape, f32) * scale

    def gain(shape):
        return 1.0 + nrm(shape, 0.01)

    Dp = DEPTH
    n_idx = jnp.arange(S5_STATE, dtype=f32)
    inp = {}
    inp["x"] = nrm((BATCH, SEQ, D_MODEL), 1.0)
    inp["meta"] = nrm((N_META, D_MODEL), 1.0)
    inp["ffn1_w_gate"] = nrm((Dp, D_MODEL, D_FF), D_MODEL ** -0.5)
    inp["ffn1_w_up"] = nrm((Dp, D_MODEL, D_FF), D_MODEL ** -0.5)
    inp["ffn1_w_down"] = nrm((Dp, D_FF, D_MODEL), BETA * D_FF ** -0.5)
    inp["ln1_g"] = gain((Dp, D_MODEL))
    inp["ln1_b"] = nrm((Dp, D_MODEL), 0.01)
    inp["w_in"] = nrm((Dp, D_MODEL, D_IN), D_MODEL ** -0.5)
    inp["mla_q_norm_g"] = gain((Dp, Q_LORA_RANK))
    inp["mla_w_uq"] = nrm((Dp, Q_LORA_RANK, MLA_HEADS * QK_HEAD_DIM), Q_LORA_RANK ** -0.5)
    inp["mla_kv_norm_g"] = gain((Dp, KV_LORA_RANK))
    inp["mla_w_ukv"] = nrm((Dp, KV_LORA_RANK, MLA_HEADS * (QK_NOPE_DIM + V_HEAD_DIM)), KV_LORA_RANK ** -0.5)
    inp["mla_w_o"] = nrm((Dp, MLA_HEADS * V_HEAD_DIM, D_MODEL), (MLA_HEADS * V_HEAD_DIM) ** -0.5)
    inp["conv_w"] = nrm((Dp, CONV_K, CONV_WIDTH), CONV_K ** -0.5)
    inp["conv_b"] = nrm((Dp, CONV_WIDTH), 0.01)
    inp["conv_w_out"] = nrm((Dp, CONV_WIDTH, D_MODEL), CONV_WIDTH ** -0.5)
    inp["s5_a_re"] = -0.5 * jnp.exp(nrm((Dp, S5_GROUPS, S5_STATE), 0.01))
    inp["s5_a_im"] = math.pi * n_idx + nrm((Dp, S5_GROUPS, S5_STATE), 0.01)
    inp["s5_log_dt"] = jax.random.uniform(next(keys), (Dp, S5_GROUPS), f32, math.log(1e-3), math.log(1e-1))
    inp["s5_b_re"] = nrm((Dp, S5_GROUPS, S5_STATE, S5_GROUP), (2 * S5_GROUP) ** -0.5)
    inp["s5_b_im"] = nrm((Dp, S5_GROUPS, S5_STATE, S5_GROUP), (2 * S5_GROUP) ** -0.5)
    inp["s5_c_re"] = nrm((Dp, S5_GROUPS, S5_GROUP, S5_STATE), (2 * S5_STATE) ** -0.5)
    inp["s5_c_im"] = nrm((Dp, S5_GROUPS, S5_GROUP, S5_STATE), (2 * S5_STATE) ** -0.5)
    inp["s5_d"] = nrm((Dp, S5_GROUPS, S5_GROUP), 1.0)
    inp["s5_w_glu"] = nrm((Dp, S5_WIDTH, S5_WIDTH), S5_WIDTH ** -0.5)
    inp["s5_b_glu"] = nrm((Dp, S5_WIDTH), 0.01)
    inp["s5_w_out"] = nrm((Dp, S5_WIDTH, D_MODEL), S5_WIDTH ** -0.5)
    inp["w_o"] = nrm((Dp, D_MODEL, D_MODEL), BETA * D_MODEL ** -0.5)
    inp["ln2_g"] = gain((Dp, D_MODEL))
    inp["ln2_b"] = nrm((Dp, D_MODEL), 0.01)
    inp["ffn2_w_gate"] = nrm((Dp, D_MODEL, D_FF), D_MODEL ** -0.5)
    inp["ffn2_w_up"] = nrm((Dp, D_MODEL, D_FF), D_MODEL ** -0.5)
    inp["ffn2_w_down"] = nrm((Dp, D_FF, D_MODEL), BETA * D_FF ** -0.5)
    inp["ln3_g"] = gain((Dp, D_MODEL))
    inp["ln3_b"] = nrm((Dp, D_MODEL), 0.01)
    return inp

def reference(x, meta, ffn1_w_gate, ffn1_w_up, ffn1_w_down, ln1_g, ln1_b, w_in,
              mla_q_norm_g, mla_w_uq, mla_kv_norm_g, mla_w_ukv, mla_w_o,
              conv_w, conv_b, conv_w_out,
              s5_a_re, s5_a_im, s5_log_dt, s5_b_re, s5_b_im, s5_c_re, s5_c_im, s5_d, s5_w_glu, s5_b_glu, s5_w_out,
              w_o, ln2_g, ln2_b, ffn2_w_gate, ffn2_w_up, ffn2_w_down, ln3_g, ln3_b):
    B = x.shape[0]
    h = jnp.concatenate([jnp.broadcast_to(meta[None].astype(x.dtype), (B, N_META, D_MODEL)), x], axis=1)
    for i in range(DEPTH):
        h = hybrid_layer(h, ffn1_w_gate[i], ffn1_w_up[i], ffn1_w_down[i], ln1_g[i], ln1_b[i], w_in[i],
                         mla_q_norm_g[i], mla_w_uq[i], mla_kv_norm_g[i], mla_w_ukv[i], mla_w_o[i],
                         conv_w[i], conv_b[i], conv_w_out[i],
                         s5_a_re[i], s5_a_im[i], s5_log_dt[i], s5_b_re[i], s5_b_im[i], s5_c_re[i], s5_c_im[i],
                         s5_d[i], s5_w_glu[i], s5_b_glu[i], s5_w_out[i],
                         w_o[i], ln2_g[i], ln2_b[i], ffn2_w_gate[i], ffn2_w_up[i], ffn2_w_down[i], ln3_g[i], ln3_b[i])
    return h[:, N_META:]


_drawn_inputs = setup_inputs


def setup_inputs(seed=0):
    import zlib

    import numpy as np

    out = dict(_drawn_inputs(seed))
    spreads = {}
    factors = {'ln1_g': 3.591,
     'ln1_b': 3.65,
     'mla_q_norm_g': 8.0,
     'mla_kv_norm_g': 8.0,
     'conv_b': 24.942,
     's5_a_re': 64.0,
     's5_a_im': 64.0,
     's5_log_dt': 64.0,
     's5_b_re': 64.0,
     's5_b_im': 64.0,
     's5_c_re': 64.0,
     's5_c_im': 64.0,
     's5_b_glu': 200.0,
     'ln2_g': 3.77,
     'ln2_b': 3.752,
     'ln3_g': 3.909,
     'ln3_b': 3.876}
    for name, (base, spread) in spreads.items():
        noise = np.random.default_rng([zlib.crc32(name.encode()), seed]).standard_normal(out[name].shape)
        drawn = base * np.exp(spread * noise) if base else spread * noise
        out[name] = jnp.asarray(drawn.astype(out[name].dtype))
    for name, factor in factors.items():
        out[name] = (out[name] * factor).astype(out[name].dtype)
    return out
```

```python
import numpy as np
import concourse.bass as bass
from concourse import mybir
from contextlib import ExitStack

P = 128
D_MODEL, SEQ, DEPTH, N_META = 1024, 512, 2, 16
L = SEQ + N_META
HALF = L // 2
MIX = D_MODEL // 2
HEADS, NOPE, ROPE, VDIM = 8, 64, 32, 64
QKD = NOPE + ROPE
QR, KVR = 3 * D_MODEL // 8, D_MODEL // 4
CONV_K = 3
GROUP, GROUPS, STATE = 16, 32, 64
D_FF = P * ((8 * D_MODEL // 3 + P - 1) // P)
ALPHA = (2.0 * DEPTH) ** 0.25
LN_EPS, RMS_EPS = 1e-5, 1e-6
KD, NF, MT = D_MODEL // P, D_FF // P, MIX // P
TC = 8
NC = L // TC
HC = NC // 2
PAIRS = GROUPS // 2
QT = [(i * P, min(P, L - i * P)) for i in range((L + P - 1) // P)]
NQ = len(QT)
VREG = (NQ - 1) * P

C_CKV = QR
C_KR = QR + KVR
C_XBAR = C_KR + ROPE
C_B = C_XBAR + MIX
C_C = C_B + MIX
C_U = C_C + MIX
C_G = C_U + MIX
KR_AT = 64

SLOTS = 4
RAW = 2
AHEAD = SLOTS - 1
DOWN_CUT = [(0, 6), (6, 6), (12, 5), (17, 5)]
FFN_CH = 2 * NF + 4 * KD
B_FFN1 = 0
B_M1 = B_FFN1 + FFN_CH
N_M1 = 10
B_CONV = B_M1 + N_M1
B_GLU = B_CONV + 3 * MT
B_V = B_GLU + MT
B_HEAD = B_V + 2
B_MERGE = B_HEAD + 2 * HEADS
B_WO = B_MERGE + 6 * KD
B_FFN2 = B_WO + KD
CH = B_FFN2 + FFN_CH
assert CH % SLOTS == 0 and not (B_M1 | B_HEAD | B_MERGE | B_WO | B_FFN2) % SLOTS

ARENA_WORDS = 53100

PC_LN = 0
PC_QG, PC_KG = 48, 51
PC_CW, PC_CB = 53, 65
PC_GB, PC_D = 69, 73
PC_N = 77

SC = MT * STATE + PAIRS
TWO_PI_INV = float(np.float32(1 / (2 * np.pi)))
PI_A = 6.28125
PI_B = float(np.float32(np.round((2 * np.pi - PI_A) * 2 ** 20) / 2 ** 20))
PI_C = float(np.float32(2 * np.pi - PI_A - PI_B))
ROUND = 12582912.0
SIN_MAX = 3.1415925


class Steps:

    def __init__(self, eng, sem, layer, per_layer):
        self.eng, self.sem, self.base, self.per_layer = eng, sem, layer * per_layer, per_layer
        self.n, self.it, self.size, self.start = 0, None, 0, 0

    def done(self, ins):
        ins.then_inc(self.sem, 1)
        self.n += 1
        self.wait()

    def wait(self):
        at = self.base + self.n
        if self.it is not None:
            at = at + self.it * self.size
        self.eng.wait_ge(self.sem, at)

    def enter(self, it, size):
        self.it, self.size, self.start = it, size, self.n

    def leave(self, times):
        assert self.n - self.start == self.size, (self.n, self.start, self.size)
        self.n = self.start + self.size * times
        self.it = None

    def close(self):
        assert self.n == self.per_layer, (self.n, self.per_layer)


def build(nc, t):
    f32, f32r = mybir.dt.float32, mybir.dt.float32r
    ALU, ACT, AX = mybir.AluOpType, mybir.ActivationFunctionType, mybir.AxisListType
    ds = bass.ds

    ctx = ExitStack()
    with ctx:
        UNIT = L * 4
        base = (nc.sbuf_base + 31) // 32 * 32
        ctx.enter_context(nc.sbuf_tensor("arena", [P, ARENA_WORDS], f32))
        top = [base]

        def at(name, shape, dt, offset):
            return nc.alloc_sbuf_tensor_at(name, shape, dt, offset=offset)

        def new(name, shape, dt=f32):
            n = 4
            for s in shape[1:]:
                n *= s
            off = top[0]
            top[0] += (n + 31) // 32 * 32
            return at(name, shape, dt, off), off

        xh, _ = new("x_hi", [P, KD, L], f32r)
        xhf = xh.bitcast(f32)
        xl, o = new("x_lo", [P, KD, L], f32r)
        xlf = xl.bitcast(f32)
        w_raw, _ = new("w_raw", [P, RAW, 8 * P])
        w_hi, _ = new("w_hi", [P, SLOTS, 8 * P], f32r)
        w_lo, _ = new("w_lo", [P, SLOTS, 8 * P], f32r)
        M, m0 = new("mixer_region", [P, 52, L])
        U = lambda k: m0 + k * UNIT
        stat, stat_off = new("stat", [P, 5, L])
        ident, _ = new("ident", [P, P])
        ones, _ = new("ones", [P, P])
        mask, _ = new("mask", [P, P])
        rope_cos, _ = new("rope_cos", [P, L])
        rope_sin, _ = new("rope_sin", [P, L])
        swap, _ = new("swap", [P, ROPE])
        par, _ = new("par", [P, PC_N])
        s5lam, _ = new("s5_lambda", [P, 2, SC])
        s5cf, _ = new("s5_coef", [P, 2, SC])
        bS, _ = new("s5_bbar_states", [P, 2, PAIRS * 2 * GROUP])
        step_r, _ = new("s5_step_re", [P, 2, PAIRS])
        step_i, _ = new("s5_step_im", [P, 2, PAIRS])
        kr, _ = new("k_rope", [P, L])
        small, _ = new("softmax_cols", [P, 4, 2 * NQ])
        assert top[0] <= base + ARENA_WORDS * 4, top[0]

        gh = at("hid_hi", [P, NF, L], f32r, U(0))
        gl = at("hid_lo", [P, NF, L], f32r, U(NF))
        glf = at("hid_rest", [P, NF, L], f32, U(NF))
        silu = at("silu", [P, 2, L], f32, U(44))
        z = at("ln_in", [P, KD, L], f32, U(44))
        cqh = at("cq_hi", [P, 3, L], f32r, U(0))
        cql = at("cq_lo", [P, 3, L], f32r, U(3))
        cqf = at("cq_raw", [P, 3, L], f32, U(3))
        kvh = at("ckv_hi", [P, 2 * L + P], f32r, U(6))
        kvo = U(6) + (2 * L + P) * 4
        kvl = at("ckv_lo", [P, 2 * L + P], f32r, kvo)
        kvf = at("ckv_raw", [P, 2, L], f32, kvo)
        lf = at("s5_in", [P, 2, TC, 512], f32, U(11))
        cl = at("s5_out", [P, 2, TC, 512], f32, U(36))
        braw = at("s5_b_raw", [P, 4, 512], f32, U(27))
        ug = at("s5_u", [P, MT, L], f32, U(27))
        X = at("s5_state", [P, NC + 1, 2, PAIRS], f32, U(31))
        K = at("s5_toeplitz", [P, MT, TC, P], f32, U(19))
        yh = at("s5_y_hi", [P, MT, L], f32r, U(36))
        yl = at("s5_y_lo", [P, MT, L], f32r, U(40))
        zh = at("conv_hi", [P, MT, L], f32r, U(11))
        zl = at("conv_lo", [P, MT, L], f32r, U(15))
        zlf = at("conv_rest", [P, MT, L], f32, U(15))
        sh = at("s5_hi", [P, MT, L], f32r, U(19))
        sl = at("s5_lo", [P, MT, L], f32r, U(23))
        slf = at("s5_rest", [P, MT, L], f32, U(23))
        oh = at("att_hi", [P, MT, L], f32r, U(27))
        ol = at("att_lo", [P, MT, L], f32r, U(31))
        V = at("v", [P, NQ, HEADS * VDIM], f32, U(35))
        PT = at("probs_T", [P, NQ, L], f32, U(40))
        pr = at("probs", [P, 2, L], f32, U(45))
        qT = at("q", [P, 2, L], f32, U(47))
        kT = at("k", [P, 2, L], f32, U(49))
        vb = at("v_head", [P, 2, NQ, VDIM], f32, stat_off + 3 * UNIT)
        conv_u = at("conv_u", [P, L + 2], f32, stat_off + UNIT)
        mh = at("mix_hi", [P, KD, L], f32r, U(0))
        ml = at("mix_lo", [P, KD, L], f32r, U(36))
        mlf = at("mix_rest", [P, KD, L], f32, U(36))
        s5p = at("s5_params", [P, 9, SC], f32, stat_off)
        tmp = at("s5_tmp", [P, 4, 512], f32, stat_off)

        ghf, yhf, ohf, mhf = (v.bitcast(f32) for v in (gh, yh, oh, mh))
        kvh3, kvl3 = (v[:, 0:2 * L].rearrange("p (k t) -> p k t", k=2) for v in (kvh, kvl))

        ps = ctx.enter_context(nc.psum_tensor("ps", [P, 8, 512], f32))
        pair = lambda k: ps[:, 2 * k:2 * k + 2, 0:HALF]
        two = lambda ap: ap.rearrange("p (h t) -> p h t", h=2)

        def sem(name):
            return ctx.enter_context(nc.semaphore(name))

        w_loaded = [sem(f"w_loaded{s}") for s in range(RAW)]
        w_rounded, w_split, chunk_done = sem("w_rounded"), sem("w_split"), sem("chunk_done")
        const_in, x_in, x_ready = sem("const_in"), sem("x_in"), sem("x_ready")
        par_in, s5p_in, b_in, c_in = sem("par_in"), sem("s5p_in"), sem("b_in"), sem("c_in")
        dve_step, act_step, passed = sem("dve_step"), sem("act_step"), sem("passed")
        silu_done, hid_done = sem("silu_done"), sem("hid_done")
        z_taken, ln_sums, ln_stat = sem("z_taken"), sem("ln_sums"), sem("ln_stat")
        ln_var, ln_sd, ln_scaled, ln_hi = sem("ln_var"), sem("ln_sd"), sem("ln_scaled"), sem("ln_hi")
        dt_done, trig_in, trig_done, s5_half = sem("dt_done"), sem("trig_in"), sem("trig_done"), sem("s5_half")
        m1_taken, b_used, lf_ready, cl_ready, f_ready = (sem("m1_taken"), sem("b_used"), sem("lf_ready"),
                                                         sem("cl_ready"), sem("f_ready"))
        f_taken, scan_done, conv_taken, conv_hi, conv_done = (sem("f_taken"), sem("scan_done"), sem("conv_taken"),
                                                              sem("conv_hi_done"), sem("conv_done"))
        rms_sums, rms_stat, rms_var, rms_sd, rms_scaled, rms_hi, lat_ready = (
            sem("rms_sums"), sem("rms_stat"), sem("rms_var"), sem("rms_sd"), sem("rms_scaled"), sem("rms_hi"),
            sem("lat_ready"))
        k_zero, k_ready, k_taken, y_ready, y_taken, gelu_done, yh_done, y_split = (
            sem("k_zero"), sem("k_ready"), sem("k_taken"), sem("y_ready"), sem("y_taken"), sem("gelu_done"),
            sem("yh_done"), sem("y_split"))
        glu_sig, glu_out, glu_hi, glu_done = sem("glu_sig"), sem("glu_out"), sem("glu_hi"), sem("glu_done")
        kr_swap, kr_done, kr_set, v_taken = sem("kr_swap"), sem("kr_done"), sem("kr_set"), sem("v_taken")
        q_copied, k_copied, q_swap, q_ready, vb_done = (sem("q_copied"), sem("k_copied"), sem("q_swap"),
                                                        sem("q_ready"), sem("vb_done"))
        s_done, nb_ready, p_exp, p_ready, t_done, pt_done, pv_done, oh_done, o_done = (
            sem("s_done"), sem("nb_ready"), sem("p_exp"), sem("p_ready"), sem("t_done"), sem("pt_done"),
            sem("pv_done"), sem("oh_done"), sem("o_done"))
        gate_sig, merge_mul, mix_rest, mix_hi_done, mix_done = (sem("gate_sig"), sem("merge_mul"), sem("mix_rest_done"),
                                                                sem("mix_hi_done"), sem("mix_done"))
        ones_set, first_hi = sem("ones_set"), sem("first_hi")

        block = ctx.enter_context(nc.Block())

        def wait_apart(eng, s, value):
            eng.wait_ge(s, value)
            eng.sem_inc(passed, 1)

        def loop(eng, start, end):
            eng.sem_inc(passed, 1)
            return eng.Fori(start, end)

        def done_at(l, c):
            return l * CH + (c + 1 + SLOTS)

        @block.sync
        def _(sp):
            def load(l, c, it_chunks, ncols, src, k):
                sp.wait_ge(w_split, l * CH + it_chunks + (c + 1))
                dst = w_raw[:, c % RAW, 0:ncols].rearrange("p (k m) -> p k m", k=k)
                sp.dma_start(dst, src).then_inc(w_loaded[c % RAW], 16)

            def rows(w, l, r0, nk, c0, nm):
                return w[ds(l, 1), r0:r0 + nk * P, ds(c0, nm)].rearrange("a (k p) m -> p (a k) m", p=P)

            def ffn(l, b0, wg, wu, wd):
                with sp.Fori(0, NF // 2) as i:
                    for j in range(2):
                        for n, w in enumerate((wg, wu)):
                            load(l, b0 + 2 * j + n, i * 4, 8 * P, rows(w, l, 0, KD, (i * 2 + j) * P, P), KD)
                with sp.Fori(0, KD) as d:
                    for n, (r, nk) in enumerate(DOWN_CUT):
                        load(l, b0 + 2 * NF + n, d * 4, nk * P, rows(wd, l, r * P, nk, d * P, P), nk)

            sp.dma_start(z[:], t["x_T"].rearrange("(k p) t -> p k t", p=P)).then_inc(x_in, 16)
            with sp.Fori(0, DEPTH) as l:
                ffn(l, B_FFN1, t["ffn1_w_gate"], t["ffn1_w_up"], t["ffn1_w_down"])
                w_in = t["w_in"]
                cols = [P * k for k in range(5)] + [C_KR - KR_AT] + [C_U + P * k for k in range(MT)]
                for m in range(MT):
                    cols += [C_XBAR + P * m, C_C + P * m, C_B + P * m]
                for n, c0 in enumerate(cols):
                    load(l, B_M1 + n, 0, 8 * P, rows(w_in, l, 0, KD, c0, P), KD)
                for m in range(MT):
                    load(l, B_GLU + m, 0, MT * P, rows(t["s5_w_glu"], l, 0, MT, m * P, P), MT)
                w_v = t["mla_w_ukv"].rearrange("l r (h s d) -> l r h s d", h=HEADS, s=2)
                for k in range(2):
                    src = w_v[ds(l, 1), k * P:(k + 1) * P, :, 1, :].rearrange("a p h d -> (a p) h d")
                    load(l, B_V + k, 0, HEADS * VDIM, src, HEADS)
                with sp.Fori(0, HEADS // 2) as i:
                    for b in range(2):
                        h = i * 2 + b
                        load(l, B_HEAD + 2 * b, i * 4, 3 * QKD, rows(t["mla_w_uq"], l, 0, 3, h * QKD, QKD), 3)
                        load(l, B_HEAD + 2 * b + 1, i * 4, 2 * P, rows(t["mla_w_ukv"], l, 0, 2, h * P, P), 2)
                with sp.Fori(0, KD // 2) as i:
                    for b in range(2):
                        for r, w in enumerate(("mla_w_o", "conv_w_out", "s5_w_out")):
                            n = 6 * b + 2 * r
                            load(l, B_MERGE + n, i * 12, 8 * P,
                                 rows(w_in, l, 0, KD, (i * 2 + b) * P + (C_G + r * D_MODEL), P), KD)
                            load(l, B_MERGE + n + 1, i * 12, MT * P, rows(t[w], l, 0, MT, (i * 2 + b) * P, P), MT)
                with sp.Fori(0, KD // 4) as i:
                    for n in range(4):
                        load(l, B_WO + n, i * 4, 8 * P, rows(t["w_o"], l, 0, KD, (i * 4 + n) * P, P), KD)
                ffn(l, B_FFN2, t["ffn2_w_gate"], t["ffn2_w_up"], t["ffn2_w_down"])
            for k in range(KD):
                sp.wait_ge(x_ready, 3 * KD * DEPTH + k + 1)
                sp.dma_start(t["out"][k * P:(k + 1) * P, :], z[:, k, N_META:L]).then_inc(x_in, 16)
            sp.wait_ge(x_in, 16 * (1 + KD))

        @block.gpsimd
        def _(pool):
            pool.sem_inc(w_split, RAW)
            with pool.Fori(0, DEPTH * CH // SLOTS) as i:
                for s in range(SLOTS):
                    pool.wait_ge(w_rounded, i * SLOTS + (s + 1))
                    pool.tensor_tensor(w_lo[:, s], w_raw[:, s % RAW], w_hi[:, s].bitcast(f32),
                                       ALU.subtract).then_inc(w_split, 1)

        @block.tensor
        def _(pe):
            pe.sem_inc(chunk_done, SLOTS)
            pe.sem_inc(t_done, 2)

            def split_ready(l, c, it_chunks=0):
                pe.wait_ge(w_split, l * CH + it_chunks + (c + 1 + RAW))

            def product(out, c, k0, hi, lo, n_tiles, first, last, m=P, kp=P, x_wait=None):
                s = c % SLOTS
                for k in range(n_tiles):
                    if x_wait is not None:
                        pe.wait_ge(x_ready, x_wait + (k + 1))
                    cols = slice(k * m, (k + 1) * m)
                    parts = ((w_hi, hi), (w_hi, lo), (w_lo, hi))
                    for n, (w, x) in enumerate(parts):
                        for h in range(2):
                            ins = nc.tensor.matmul(out[0:m, h], w[:, s, cols], x[:, k0 + k, h * HALF:(h + 1) * HALF],
                                                   start=first and k == 0 and n == 0,
                                                   stop=last and k == n_tiles - 1 and n == 2)
                return ins

            def sum_over_features(src, out):
                for h in range(2):
                    ins = nc.tensor.matmul(out[:, h], ones[:], src[:, h * HALF:(h + 1) * HALF], start=True, stop=True)
                return ins

            def layer_norm_middle(l, which):
                pe.wait_ge(ln_sums, (l * 3 + which) * KD + KD // 2)
                sum_over_features(stat[:, 1], pair(2)).then_inc(ln_stat, 1)

            def layer_norm_end(l, which):
                pe.wait_ge(ln_sums, (l * 3 + which) * KD + KD)
                sum_over_features(stat[:, 1], pair(2))
                sum_over_features(stat[:, 2], pair(3)).then_inc(ln_stat, 1)

            def ffn(l, b0, w):
                x0 = l * 24 + w * 16
                with loop(pe, 0, NF // 2) as i:
                    n0 = (l * 2 + w) * NF + i * 2
                    for j in range(2):
                        c = b0 + 2 * j
                        split_ready(l, c, i * 4)
                        pe.wait_ge(silu_done, n0 + (j + 1))
                        product(pair(2 * j), c, 0, xh, xl, KD, True, True,
                                x_wait=x0 if j == 0 else None).then_inc(chunk_done, 1)
                        split_ready(l, c + 1, i * 4)
                        pe.wait_ge(hid_done, n0 + (j + 1))
                        product(pair(2 * j + 1), c + 1, 0, xh, xl, KD, True, True).then_inc(chunk_done, 1)
                pe.wait_ge(hid_done, (l * 2 + w) * NF + (NF + 2))
                for part in range(2):
                    with loop(pe, 0, 2) as i:
                        for b in range(2):
                            dd = part * 4 + b
                            pe.wait_ge(z_taken, (l * 3 + 2 * w) * KD + i * 2 + (dd + 1))
                            for n, (r, nk) in enumerate(DOWN_CUT):
                                c = b0 + 2 * NF + 4 * dd + n
                                split_ready(l, c, i * 8)
                                product(pair(b), c, r, gh, gl, nk, n == 0, n == 3).then_inc(chunk_done, 1)
                    (layer_norm_middle, layer_norm_end)[part](l, 2 * w)

            def m1(l):
                def one(c, k, it):
                    split_ready(l, c, it)
                    pe.wait_ge(m1_taken, l * N_M1 + it + (c - B_M1 + 1))
                    product(pair(k), c, 0, xh, xl, KD, True, True,
                            x_wait=l * 24 + 8 if k == 0 else None).then_inc(chunk_done, 1)
                with loop(pe, 0, 2) as i:
                    for k in range(4):
                        one(B_M1 + k, k, i * 4)
                for k in range(2):
                    one(B_M1 + 8 + k, k, 0)

            def s5_states_in(l):
                pe.wait_ge(lf_ready, l + 1)
                pe.wait_ge(m1_taken, l * N_M1 + (N_M1 + 4))
                for m in range(MT):
                    b0 = 4 * (m % 2)
                    if m >= 2:
                        pe.wait_ge(f_taken, l * PAIRS + (4 * (m - 1)))
                    for ri in range(2):
                        for s in range(TC):
                            for q in range(4):
                                rows = slice(32 * q, 32 * q + 32)
                                ins = nc.tensor.matmul(ps[:, b0 + q, ri * NC:(ri + 1) * NC],
                                                       lf[rows, ri, TC - 1 - s, m * P:(m + 1) * P],
                                                       ug[rows, m, s * NC:(s + 1) * NC],
                                                       start=s == 0, stop=s == TC - 1)
                    ins.then_inc(f_ready, 1)

            def conv(l):
                pe.wait_ge(f_taken, l * PAIRS + PAIRS)
                with loop(pe, 0, 3) as i:
                    for k in range(4):
                        split_ready(l, B_CONV + k, i * 4)
                        pe.wait_ge(conv_taken, l * 12 + i * 4 + (k + 1))
                        product(pair(k), B_CONV + k, 0, xh, xl, KD, True, True).then_inc(chunk_done, 1)

            def s5_toeplitz(l):
                pe.wait_ge(conv_taken, l * 12 + (12 + 4))
                pe.wait_ge(cl_ready, l + 1)
                for m in range(MT):
                    for q in range(4):
                        p = 4 * m + q
                        for ri in range(2):
                            ins = nc.tensor.matmul(ps[32 * q:32 * q + 32, m, 0:TC * 32],
                                                   bS[:, ri, p * 32:(p + 1) * 32],
                                                   cl[:, ri, :, p * 32:(p + 1) * 32],
                                                   start=ri == 0, stop=ri == 1)
                    ins.then_inc(k_ready, 1)

            def latents(l):
                for n in range(2):
                    pe.wait_ge(rms_sums, l * 2 + (n + 1))
                    sum_over_features(stat[:, 2 + n], pair(2 + n)).then_inc(rms_stat, 1)
                wait_apart(pe, k_taken, l * PAIRS + PAIRS)
                for h in range(2):
                    ins = nc.tensor.matmul(ps[64:96, h, 0:HALF], swap[64:96, :], kr[64:96, h * HALF:(h + 1) * HALF],
                                           start=True, stop=True)
                ins.then_inc(kr_swap, 1)

            def s5_outputs(l):
                pe.wait_ge(k_taken, l * PAIRS + PAIRS)
                pe.wait_ge(scan_done, l + 1)
                pe.wait_ge(kr_done, l + 1)
                for m in range(MT):
                    a = 2 * (m % 2)
                    if m >= 2:
                        pe.wait_ge(y_taken, l * MT + (m - 1))
                    for j in range(TC):
                        for bank, (lo, up) in enumerate(((0, 4), (4, 8))):
                            s0 = max(j, lo)
                            if s0 >= up:
                                continue
                            nc.tensor.matmul(ps[:, a + bank, (s0 - lo) * NC:4 * NC], K[:, m, j, :],
                                             ug[:, m, (s0 - j) * NC:(up - j) * NC], start=j == 0, stop=False,
                                             skip_group_check=True)
                    for s in range(TC):
                        for ri in range(2):
                            for q in range(4):
                                p = 4 * m + q
                                ins = nc.tensor.matmul(
                                    ps[32 * q:32 * q + 32, a + s // 4, (s % 4) * NC:(s % 4 + 1) * NC],
                                    cl[:, ri, s, p * 32:(p + 1) * 32], X[:, 0:NC, ri, p],
                                    start=False, stop=ri == 1, skip_group_check=True)
                    ins.then_inc(y_ready, 1)

            def glu(l):
                pe.wait_ge(y_split, l * MT + MT)
                for m in range(MT):
                    c = B_GLU + m
                    split_ready(l, c)
                    product(pair(m), c, 0, yh, yl, MT, True, True).then_inc(chunk_done, 1)

            def values(l):
                pe.wait_ge(lat_ready, l * 5 + 5)
                pe.wait_ge(glu_sig, l * MT + MT)
                for k in range(2):
                    c = B_V + k
                    s = c % SLOTS
                    split_ready(l, c)
                    for i in range(NQ):
                        tok = slice(k * L + i * P, k * L + (i + 1) * P)
                        for n, (x, w) in enumerate(((kvh, w_hi), (kvl, w_hi), (kvh, w_lo))):
                            ins = nc.tensor.matmul(ps[:, i, :], x[:, tok], w[:, s, 0:HEADS * VDIM],
                                                   start=k == 0 and n == 0, stop=k == 1 and n == 2)
                    ins.then_inc(chunk_done, 1)

            def heads(l):
                with loop(pe, 0, HEADS // 2) as i:
                    h0 = l * HEADS + i * 2
                    pe.wait_ge(v_taken, l * NQ + NQ)
                    pe.wait_ge(o_done, h0 + 2)
                    for b in range(2):
                        c = B_HEAD + 2 * b
                        split_ready(l, c, i * 4)
                        product(pair(b), c, 0, cqh, cql, 3, True, True, m=QKD).then_inc(chunk_done, 1)
                        split_ready(l, c + 1, i * 4)
                        product(pair(3 - b), c + 1, 0, kvh3, kvl3, 2, True, True).then_inc(chunk_done, 1)
                    for b in range(2):
                        wait_apart(pe, q_copied, h0 + (b + 1))
                        for h in range(2):
                            ins = nc.tensor.matmul(ps[64:96, 2 * b + h, 0:HALF], swap[64:96, :],
                                                   qT[64:96, b, h * HALF:(h + 1) * HALF], start=True, stop=True)
                        ins.then_inc(q_swap, 1)
                    pe.wait_ge(q_ready, h0 + 2)
                    pe.wait_ge(k_copied, h0 + 2)
                    pe.wait_ge(kr_set, l + 1)

                    def scores(b, j):
                        q0, nq = QT[j]
                        if j < NQ - 1:
                            ins = nc.tensor.matmul(ps[:, j, 0:q0 + P], qT[0:QKD, b, q0:q0 + nq],
                                                   kT[0:QKD, b, 0:q0 + P], start=True, stop=True)
                        else:
                            for h in range(2):
                                ins = nc.tensor.matmul(ps[0:nq, h, 0:HALF], qT[0:QKD, b, q0:q0 + nq],
                                                       kT[0:QKD, b, h * HALF:(h + 1) * HALF], start=True, stop=True)
                        ins.then_inc(s_done, 1)

                    def transposes(b, j):
                        q0, nq = QT[j]
                        buf = (NQ * b + j) % 2
                        wait_apart(pe, p_ready, (h0 + b) * NQ + (j + 1))
                        wait_apart(pe, pt_done, (h0 + b) * NQ + (j + 1))
                        for k in range(j + 1):
                            k0, nk = QT[k]
                            if nk == P:
                                ins = nc.tensor.transpose(ps[:, 4 + buf, k * nq:(k + 1) * nq],
                                                          pr[0:nq, buf, k0:k0 + P], ident[0:nq, 0:nq])
                            else:
                                ins = nc.tensor.matmul(ps[0:nk, 4 + buf, k * nq:(k + 1) * nq],
                                                       pr[0:nq, buf, k0:k0 + nk], ident[0:nq, 0:nq],
                                                       start=True, stop=True)
                        ins.then_inc(t_done, 1)

                    def values_sum(b):
                        wait_apart(pe, pt_done, (h0 + b) * NQ + (NQ + 2))
                        wait_apart(pe, vb_done, h0 + (b + 1))
                        for half in range(2):
                            todo = [k for k in range(NQ) if QT[k][0] < (half + 1) * HALF]
                            for k in todo:
                                k0, nk = QT[k]
                                q0 = max(k0, half * HALF)
                                ins = nc.tensor.matmul(
                                    ps[64 * b:64 * b + 64, 6 + half, q0 - half * HALF:HALF],
                                    vb[0:nk, b, k, :], PT[0:nk, k, q0:(half + 1) * HALF],
                                    start=k == 0, stop=k == todo[-1], skip_group_check=True)
                        ins.then_inc(pv_done, 1)

                    for j in range(4):
                        scores(0, j)
                    transposes(0, 0)
                    transposes(0, 1)
                    scores(0, 4)
                    transposes(0, 2)
                    transposes(0, 3)
                    transposes(0, 4)
                    for j in range(4):
                        scores(1, j)
                    values_sum(0)
                    transposes(1, 0)
                    transposes(1, 1)
                    scores(1, 4)
                    transposes(1, 2)
                    transposes(1, 3)
                    transposes(1, 4)
                    values_sum(1)

            def merge(l):
                pe.wait_ge(o_done, l * HEADS + (HEADS + 2))
                with loop(pe, 0, KD // 2) as i:
                    for b in range(2):
                        for r, (yhi, ylo) in enumerate(((oh, ol), (zh, zl), (sh, sl))):
                            n = 3 * b + r
                            c = B_MERGE + 2 * n
                            split_ready(l, c, i * 12)
                            pe.wait_ge(gate_sig, l * 24 + i * 6 + (n + 1))
                            product(pair(2 * (n % 2)), c, 0, xh, xl, KD, True, True).then_inc(chunk_done, 1)
                            split_ready(l, c + 1, i * 12)
                            pe.wait_ge(merge_mul, l * 24 + i * 6 + (n + 1))
                            product(pair(2 * (n % 2) + 1), c + 1, 0, yhi, ylo, MT, True, True).then_inc(chunk_done, 1)

            def w_o(l):
                pe.wait_ge(mix_done, l * KD + KD)
                for part in range(2):
                    for b in range(4):
                        c = B_WO + part * 4 + b
                        split_ready(l, c)
                        pe.wait_ge(z_taken, (l * 3 + 1) * KD + (part * 4 + b + 1))
                        product(pair(b % 2), c, 0, mh, ml, KD, True, True).then_inc(chunk_done, 1)
                    (layer_norm_middle, layer_norm_end)[part](l, 1)

            pe.wait_ge(const_in, 16 * 5)
            pe.wait_ge(ones_set, 1)
            with loop(pe, 0, DEPTH) as l:
                ffn(l, B_FFN1, 0)
                m1(l)
                s5_states_in(l)
                conv(l)
                s5_toeplitz(l)
                latents(l)
                s5_outputs(l)
                glu(l)
                values(l)
                heads(l)
                merge(l)
                w_o(l)
                ffn(l, B_FFN2, 1)

        @block.scalar
        def _(act):
            def ACTV(out, in_, f=ACT.Copy, **kw):
                return nc.scalar.activation(out, in_, f, **kw)

            def round_ahead(l, c, per4=0, i=None):
                c += AHEAD
                v, free = l * (CH // RAW) + (c // RAW + 1), l * CH + (c + 1)
                if i is not None:
                    v, free = v + i * (per4 * SLOTS // RAW), free + i * (per4 * SLOTS)
                act.wait_ge(chunk_done, free)
                act.wait_ge(w_loaded[c % RAW], v * 16)
                ACTV(w_hi[:, c % SLOTS], w_raw[:, c % RAW]).then_inc(w_rounded, 1)

            def layer_norm_end(l, which, st):
                n = l * 3 + which
                act.wait_ge(ln_var, n + 1)
                ACTV(stat[:, 2], stat[:, 2], ACT.Sqrt).then_inc(ln_sd, 1)
                for k in range(KD):
                    act.wait_ge(ln_scaled, n * KD + (k + 1))
                    col = PC_LN + which * 16 + k
                    st.done(ACTV(z[:, k], z[:, k], ACT.Identity, scale=par[:, col:col + 1],
                                 bias=par[:, col + 8:col + 9]))
                    ACTV(xh[:, k], z[:, k]).then_inc(ln_hi, 1)

            def ffn(l, b0, w, st):
                with act.Fori(0, NF // 2) as i:
                    n0 = (l * 2 + w) * NF + i * 2
                    for j in range(2):
                        c = b0 + 2 * j
                        round_ahead(l, c, 1, i)
                        act.wait_ge(chunk_done, done_at(l, c) + i * 4)
                        act.wait_ge(hid_done, n0 + (j + 1))
                        ACTV(two(silu[:, j]), pair(2 * j), ACT.Silu).then_inc(silu_done, 1)
                        round_ahead(l, c + 1, 1, i)
                b1 = b0 + 2 * NF
                last = b0 == B_FFN2
                with act.Fori(0, KD - last) as d:
                    for n in range(4):
                        round_ahead(l, b1 + n, 1, d)
                if last:
                    round_ahead(l, b1 + 4 * (KD - 1))
                layer_norm_end(l, 2 * w, st)

            act.sem_inc(silu_done, 2)
            act.sem_inc(gate_sig, 2)
            act.sem_inc(m1_taken, 4)
            act.sem_inc(pt_done, 2)
            for dst, name in ((ident[:], "c_ident"), (mask[:], "c_mask"), (rope_cos[64:96, :], "c_cos"),
                              (rope_sin[64:96, :], "c_sin"), (swap[64:96, :], "c_swap")):
                act.dma_start(dst, t[name]).then_inc(const_in, 16)

            with act.Fori(0, DEPTH) as l:
                st = Steps(act, act_step, l, ACT_STEPS)
                for c in range(AHEAD):
                    round_ahead(l, c - AHEAD)
                act.wait_ge(x_ready, l * 24 + 8)
                act.dma_start(par[:], t["par"][ds(l, 1)].rearrange("a p c -> (a p) c")).then_inc(par_in, 16)
                act.dma_start(s5p[:, 0:3], t["s5_par"][ds(l, 1)].rearrange("a p k c -> (a p) k c")).then_inc(s5p_in, 16)
                act.wait_ge(s5p_in, l * 16 + 16)
                ACTV(s5p[:, 2], s5p[:, 2], ACT.Exp).then_inc(dt_done, 1)
                act.wait_ge(trig_in, l + 1)
                ACTV(s5p[:, 3], s5p[:, 3], ACT.Exp)
                ACTV(s5p[:, 6], s5p[:, 4], ACT.Sin)
                ACTV(s5p[:, 7], s5p[:, 4], ACT.Sin, scale=0.5).then_inc(trig_done, 1)
                act.wait_ge(par_in, l * 16 + 16)
                ffn(l, B_FFN1, 0, st)

                act.wait_ge(x_ready, l * 24 + 16)
                act.dma_start(braw[:], t["s5_b"][ds(l, 1)].rearrange("a p k c -> (a p) k c")).then_inc(b_in, 16)
                act.dma_start(cl[:, :, 0], t["s5_c"][ds(l, 1)].rearrange("a p k c -> (a p) k c")).then_inc(c_in, 16)
                for n in range(N_M1):
                    c = B_M1 + n
                    round_ahead(l, c)
                    act.wait_ge(chunk_done, done_at(l, c))
                    src = pair(n % 4)
                    if n < 3:
                        ACTV(two(cqf[:, n]), src).then_inc(m1_taken, 1)
                    elif n < 5:
                        ACTV(two(kvf[:, n - 3]), src).then_inc(m1_taken, 1)
                    elif n == 5:
                        ACTV(two(kr[64:96]), src[64:96]).then_inc(m1_taken, 1)
                    else:
                        if n == 6:
                            wait_apart(act, b_used, l + 1)
                            act.wait_ge(chunk_done, done_at(l, c))
                        for h in range(2):
                            out = ug[:, n - 6].rearrange("p (s c) -> p s c", s=TC)[:, :, h * HC:(h + 1) * HC]
                            ins = ACTV(out, src[:, h].rearrange("p (c s) -> p s c", s=TC))
                        ins.then_inc(m1_taken, 1)
                for m in range(MT):
                    act.wait_ge(f_ready, l * MT + (m + 1))
                    for q in range(4):
                        ACTV(X[:, 1:NC + 1, :, 4 * m + q],
                             ps[:, 4 * (m % 2) + q, 0:2 * NC].rearrange("p (r c) -> p c r", r=2)).then_inc(f_taken, 1)
                for n in range(3 * MT):
                    round_ahead(l, B_CONV + n)
                wait_apart(act, k_zero, l + 1)
                for m in range(MT):
                    act.wait_ge(k_ready, l * MT + (m + 1))
                    for q in range(4):
                        r = slice(32 * q, 32 * q + 32)
                        ACTV(K[r, m, :, r], ps[r, m, 0:TC * 32].rearrange("p (j o) -> p j o", j=TC)).then_inc(k_taken, 1)
                act.wait_ge(rms_var, l + 1)
                ACTV(stat[:, 2:4], stat[:, 2:4], ACT.Sqrt).then_inc(rms_sd, 1)
                for m in range(MT):
                    act.wait_ge(y_taken, l * MT + (m + 1))
                    ACTV(ug[:, m].rearrange("p (c s) -> p c s", s=TC), stat[:, m % 2].rearrange("p (s c) -> p c s", s=TC),
                         ACT.Gelu_apprx_tanh).then_inc(gelu_done, 1)
                for b in range(2):
                    ins = ACTV(kT[64:96, b], kr[64:96])
                ins.then_inc(kr_set, 1)
                for m in range(MT):
                    round_ahead(l, B_GLU + m)
                    act.wait_ge(chunk_done, done_at(l, B_GLU + m))
                    if m >= 2:
                        act.wait_ge(glu_out, l * MT + (m - 1))
                    ACTV(two(stat[:, 2 + m % 2]), pair(m), ACT.Sigmoid,
                         bias=par[:, PC_GB + m:PC_GB + m + 1]).then_inc(glu_sig, 1)
                for k in range(2):
                    round_ahead(l, B_V + k)
                act.wait_ge(chunk_done, done_at(l, B_V + 1))
                for k in range(NQ):
                    ACTV(V[:, k], ps[:, k, :]).then_inc(v_taken, 1)
                wait_apart(act, glu_done, l * MT + MT)

                with act.Fori(0, HEADS // 2) as i:
                    h0 = l * HEADS + i * 2

                    def take_qkv(b):
                        c = B_HEAD + 2 * b
                        round_ahead(l, c, 1, i)
                        act.wait_ge(chunk_done, done_at(l, c) + i * 4)
                        ACTV(two(qT[0:QKD, b]), pair(b)[0:QKD]).then_inc(q_copied, 1)
                        round_ahead(l, c + 1, 1, i)
                        act.wait_ge(chunk_done, done_at(l, c + 1) + i * 4)
                        ACTV(two(kT[0:NOPE, b]), pair(3 - b)[0:NOPE]).then_inc(k_copied, 1)
                        if b == 0:
                            wait_apart(act, v_taken, l * NQ + NQ)
                        ACTV(vb[:, b], V[:, :, ds((i * 2 + b) * VDIM, VDIM)]).then_inc(vb_done, 1)

                    def exps(b, j):
                        n, buf = (h0 + b) * NQ + (j + 1), (NQ * b + j) % 2
                        q0, nq = QT[j]
                        act.wait_ge(nb_ready, n)
                        act.wait_ge(t_done, n)
                        col = NQ * b + j
                        src, dst = (ps[:, j, 0:q0 + P], pr[:, buf, 0:q0 + P]) if nq == P else (
                            pair(0)[0:nq], two(pr[0:nq, buf]))
                        ACTV(dst, src, ACT.Exp, scale=QKD ** -0.5, bias=small[0:nq, 1, col:col + 1],
                             accum_out=small[0:nq, 2, col:col + 1]).then_inc(p_exp, 1)

                    def copy_t(b, j):
                        n, bank = (h0 + b) * NQ + (j + 3), 4 + (NQ * b + j) % 2
                        q0, nq = QT[j]
                        act.wait_ge(t_done, n)
                        if nq == P:
                            ins = ACTV(PT[:, 0:j + 1, q0:q0 + P],
                                       ps[:, bank, 0:(j + 1) * P].rearrange("p (k q) -> p k q", q=P))
                        else:
                            ACTV(PT[:, 0:j, q0:q0 + nq], ps[:, bank, 0:j * nq].rearrange("p (k q) -> p k q", q=nq))
                            ins = ACTV(PT[0:nq, j, q0:q0 + nq], ps[0:nq, bank, j * nq:(j + 1) * nq])
                        ins.then_inc(pt_done, 1)

                    def take_o(b):
                        wait_apart(act, pv_done, h0 + (b + 1))
                        ACTV(oh[64 * b:64 * b + 64, ds(i, 1)].rearrange("p a (h t) -> p (a h) t", h=2),
                             pair(3)[64 * b:64 * b + 64]).then_inc(oh_done, 1)

                    take_qkv(0)
                    take_qkv(1)
                    for b in range(2):
                        exps(b, 0)
                        exps(b, 1)
                        if b == 1:
                            take_o(0)
                        copy_t(b, 0)
                        exps(b, 2)
                        copy_t(b, 1)
                        exps(b, 3)
                        copy_t(b, 2)
                        exps(b, 4)
                        copy_t(b, 3)
                        copy_t(b, 4)
                    take_o(1)

                with act.Fori(0, KD // 2) as i:
                    for n in range(6):
                        c = B_MERGE + 2 * n
                        round_ahead(l, c, 3, i)
                        act.wait_ge(chunk_done, done_at(l, c) + i * 12)
                        act.wait_ge(merge_mul, l * 24 + i * 6 + (n + 1))
                        ACTV(two(stat[:, n % 2]), pair(2 * (n % 2)), ACT.Sigmoid).then_inc(gate_sig, 1)
                        round_ahead(l, c + 1, 3, i)
                for n in range(KD):
                    round_ahead(l, B_WO + n)
                layer_norm_end(l, 1, st)
                ffn(l, B_FFN2, 1, st)
                st.close()

        @block.vector
        def _(dve):
            tt, ts, stt = nc.vector.tensor_tensor, nc.vector.tensor_scalar, nc.vector.scalar_tensor_tensor
            MUL, ADD, SUB = ALU.mult, ALU.add, ALU.subtract

            def follow(ins, s, value):
                ins.then_inc(s, 1)
                dve.wait_ge(s, value)

            def split_tile(st, hi, lo, rest, after=None):
                st.done(ts(hi, rest, 1.0, None, MUL))
                return tt(lo, rest, hi.bitcast(f32), SUB)

            def take_z(l, which, st, scale, i, k, c, deviate):
                kk = ds(i * 2 + k, 1)
                one = lambda ap: ap[:, kk].rearrange("p a (h t) -> p (a h) t", h=2)
                flat = lambda ap: ap[:, kk].rearrange("p a t -> p (a t)")
                dve.wait_ge(chunk_done, c)
                ins = stt(one(z), pair(k % 2), scale, one(xhf), MUL, ADD)
                follow(ins, z_taken, (l * 3 + which) * KD + i * 2 + (k + 3))
                st.done(tt(flat(z), flat(z), flat(xlf), ADD))
                if not deviate:
                    follow(tt(stat[:, 1], stat[:, 1], flat(z), ADD), ln_sums, (l * 3 + which) * KD + i * 2 + (k + 1))
                else:
                    st.done(tt(flat(z), flat(z), stat[:, 0], SUB))
                    tt(stat[:, 1], stat[:, 1], flat(z), ADD)
                    st.done(tt(stat[:, 3], flat(z), flat(z), MUL))
                    follow(tt(stat[:, 2], stat[:, 2], stat[:, 3], ADD), ln_sums,
                           (l * 3 + which) * KD + i * 2 + (k + 1))

            def layer_norm(l, which, st, scale, eps, chunk_of, per_tile):
                n = l * 3 + which
                dve.memset(stat[:, 1], 0.0)
                st.done(dve.memset(stat[:, 2], 0.0))
                with loop(dve, 0, 2) as i:
                    st.enter(i, 2)
                    for k in range(2):
                        take_z(l, which, st, scale, i, k, done_at(l, chunk_of(k)) + i * 2 * per_tile, False)
                    st.leave(2)
                dve.wait_ge(ln_stat, 2 * n + 1)
                st.done(ts(two(stat[:, 0]), pair(2), 1.0 / (D_MODEL // 2), None, MUL))
                for k in range(KD // 2):
                    tt(z[:, k], z[:, k], stat[:, 0], SUB)
                st.done(stt(stat[:, 1], stat[:, 0], -float(KD // 2), stat[:, 1], MUL, ADD))
                for k in range(KD // 2):
                    st.done(tt(stat[:, 3], z[:, k], z[:, k], MUL))
                    st.done(tt(stat[:, 2], stat[:, 2], stat[:, 3], ADD))
                with loop(dve, 2, 4) as i:
                    st.enter(i - 2, 6)
                    for k in range(2):
                        take_z(l, which, st, scale, i, k, done_at(l, chunk_of(k)) + i * 2 * per_tile, True)
                    st.leave(2)
                dve.wait_ge(ln_stat, 2 * n + 2)
                st.done(ts(two(stat[:, 0]), pair(2), 1.0 / D_MODEL, None, MUL))
                ts(two(stat[:, 2]), pair(3), 1.0 / D_MODEL, eps, MUL, ADD)
                st.done(tt(stat[:, 3], stat[:, 0], stat[:, 0], MUL))
                tt(stat[:, 2], stat[:, 2], stat[:, 3], SUB).then_inc(ln_var, 1)
                dve.wait_ge(ln_sd, n + 1)
                st.done(nc.vector.reciprocal(stat[:, 1], stat[:, 2]))
                st.done(tt(stat[:, 3], stat[:, 0], stat[:, 1], MUL))
                for k in range(KD + 1):
                    if k < KD:
                        st.done(tt(z[:, k], z[:, k], stat[:, 1], MUL))
                        tt(z[:, k], z[:, k], stat[:, 3], SUB).then_inc(ln_scaled, 1)
                    if k:
                        dve.wait_ge(ln_hi, n * KD + k)
                        tt(xl[:, k - 1], z[:, k - 1], xhf[:, k - 1], SUB).then_inc(x_ready, 1)

            def ffn(l, b0, w, st):
                with loop(dve, 0, NF // 2) as i:
                    st.enter(i, 4)
                    n0 = (l * 2 + w) * NF + i * 2
                    for j in range(2):
                        f = ds(i * 2 + j, 1)
                        flat = lambda ap: ap[:, f].rearrange("p a t -> p (a t)")
                        dve.wait_ge(silu_done, n0 + (j + 3))
                        dve.wait_ge(chunk_done, done_at(l, b0 + 2 * j + 1) + i * 4)
                        st.done(tt(glf[:, f].rearrange("p a (h t) -> p (a h) t", h=2), two(silu[:, j]),
                                   pair(2 * j + 1), MUL))
                        st.done(ts(flat(gh), flat(glf), 1.0, None, MUL))
                        tt(flat(gl), flat(glf), flat(ghf), SUB).then_inc(hid_done, 1)
                    st.leave(NF // 2)
                layer_norm(l, 2 * w, st, 0.5 / ALPHA, LN_EPS / ALPHA ** 2,
                           lambda k: b0 + 2 * NF + 4 * k + 3, 4)

            def s5_parameters(l, st):
                q = lambda k: s5p[:, k]
                dve.wait_ge(dt_done, l + 1)
                tt(q(3), q(2), q(0), MUL)
                st.done(tt(q(4), q(2), q(1), MUL))
                st.done(ts(q(5), q(4), TWO_PI_INV, ROUND, MUL, ADD))
                st.done(ts(q(5), q(5), ROUND, None, SUB))
                for c in (PI_A, PI_B, PI_C):
                    st.done(stt(q(4), q(5), -c, q(4), MUL, ADD))
                ts(q(4), q(4), SIN_MAX, -SIN_MAX, ALU.min, ALU.max).then_inc(trig_in, 1)
                dve.wait_ge(trig_done, l + 1)
                st.done(tt(q(7), q(7), q(7), MUL))
                st.done(ts(q(7), q(7), -2.0, 1.0, MUL, ADD))
                tt(s5lam[:, 0], q(3), q(7), MUL)
                tt(s5lam[:, 1], q(3), q(6), MUL)
                tt(q(5), q(0), q(0), MUL)
                st.done(tt(q(8), q(1), q(1), MUL))
                st.done(tt(q(5), q(5), q(8), ADD))
                nc.vector.reciprocal(q(5), q(5))
                st.done(ts(q(8), s5lam[:, 0], -1.0, None, ADD))
                tt(q(3), q(8), q(0), MUL)
                tt(q(4), s5lam[:, 1], q(1), MUL)
                tt(q(6), s5lam[:, 1], q(0), MUL)
                st.done(tt(q(7), q(8), q(1), MUL))
                tt(q(3), q(3), q(4), ADD)
                st.done(tt(q(6), q(6), q(7), SUB))
                tt(s5cf[:, 0], q(3), q(5), MUL)
                tt(s5cf[:, 1], q(6), q(5), MUL)
                c = slice(MT * STATE, SC)
                re, im = s5lam[:, 0, c], s5lam[:, 1, c]
                w = PAIRS
                for k in range(3):
                    rr, ii, ri = (s5p[:, 8, n * w:(n + 1) * w] for n in range(3))
                    tt(rr, re, re, MUL)
                    tt(ii, im, im, MUL)
                    st.done(tt(ri, re, im, MUL))
                    re, im = (s5p[:, 7, (2 * k + n) * w:(2 * k + n + 1) * w] for n in range(2))
                    tt(re, rr, ii, SUB)
                    st.done(ts(im, ri, 2.0, None, MUL))
                for n in range(2):
                    ts(step_r[:, n], re, 1.0, None, MUL)
                    ins = ts(step_i[:, n], im, (1.0, -1.0)[n], None, MUL)
                st.done(ins)

            def s5_tables(l, st):
                def cmul(out_r, out_i, ar, ai, br, bi, op_r, op_i, like):
                    p4 = [tmp[:, n].rearrange(like[0], **like[1]) for n in range(4)]
                    tt(p4[0], ar, br, MUL)
                    tt(p4[1], ai, bi, MUL)
                    tt(p4[2], ar, bi, MUL)
                    st.done(tt(p4[3], ai, br, MUL))
                    tt(out_r, tmp[:, 0], tmp[:, 1], op_r)
                    st.done(tt(out_i, tmp[:, 2], tmp[:, 3], op_i))

                chan = ("p (t s n) -> p t s n", dict(t=MT, s=2))
                stat_ = ("p (q h) -> p q h", dict(q=PAIRS))

                def on_channels(ap):
                    return ap[:, 0:MT * STATE].rearrange("p (t n) -> p t n", t=MT).unsqueeze(2).to_broadcast(
                        [P, MT, 2, STATE])

                def on_states(ap):
                    return ap[:, MT * STATE:SC].unsqueeze(2).to_broadcast([P, PAIRS, 32])

                as_ = lambda ap, like: ap.rearrange(like[0], **like[1])
                dve.wait_ge(b_in, l * 16 + 16)
                for src, dst, like, on in ((0, (braw[:, 0], braw[:, 1]), chan, on_channels),
                                           (2, (bS[:, 0], bS[:, 1]), stat_, on_states)):
                    cmul(dst[0], dst[1], on(s5cf[:, 0]), on(s5cf[:, 1]), as_(braw[:, src], like),
                         as_(braw[:, src + 1], like), SUB, ADD, like)
                lr, li = on_channels(s5lam[:, 0]), on_channels(s5lam[:, 1])
                for j in range(TC):
                    br, bi = (braw[:, 0], braw[:, 1]) if j == 0 else (lf[:, 0, j - 1], lf[:, 1, j - 1])
                    cmul(lf[:, 0, j], lf[:, 1, j], lr, li, as_(br, chan), as_(bi, chan), SUB, ADD, chan)
                    if j == 0:
                        dve.sem_inc(b_used, 1)
                dve.sem_inc(lf_ready, 1)
                dve.wait_ge(c_in, l * 16 + 16)
                st.done(ts(cl[:, 1, 0], cl[:, 1, 0], -1.0, None, MUL))
                lr, li = on_states(s5lam[:, 0]), on_states(s5lam[:, 1])
                for j in range(1, TC):
                    cmul(cl[:, 0, j], cl[:, 1, j], lr, li, as_(cl[:, 0, j - 1], stat_), as_(cl[:, 1, j - 1], stat_),
                         ADD, SUB, stat_)
                st.done(dve.memset(X[:, 0], 0.0))
                dve.sem_inc(cl_ready, 1)

            def conv_tile(l, m, st):
                n0 = 3 * m

                def there(n):
                    dve.wait_ge(chunk_done, done_at(l, B_CONV + n0 + n))
                    return pair((n0 + n) % 4)

                def taken(ins, n):
                    follow(ins, conv_taken, l * 12 + (n0 + n + 5))

                taken(ts(two(stat[:, 4]), there(0), 1.0, None, MUL), 0)
                taken(tt(two(conv_u[:, 2:]), two(stat[:, 4]), there(1), MUL), 1)
                tap = lambda j: par[:, PC_CW + 4 * j + m:PC_CW + 4 * j + m + 1]
                st.done(ts(stat[:, 3], conv_u[:, 2:], tap(2), par[:, PC_CB + m:PC_CB + m + 1], MUL, ADD))
                for j in (1, 0):
                    st.done(stt(stat[:, 3], conv_u[:, j:j + L], tap(j), stat[:, 3], MUL, ADD))
                taken(tt(two(zlf[:, m]), two(stat[:, 3]), there(2), MUL), 2)
                split_tile(st, zh[:, m], zl[:, m], zlf[:, m]).then_inc(conv_done, 1)

            def scan(l, c0, c1, st):
                a, b = (stat[:, 0, n * 32:(n + 1) * 32].rearrange("p (r q) -> p r q", r=2) for n in range(2))
                with loop(dve, c0, c1) as c:
                    st.enter(c - c0, 3)
                    now, nxt = (X[:, ds(c + n, 1)].rearrange("p a r q -> p (a r) q") for n in range(2))
                    tt(a, now, step_r[:], MUL)
                    st.done(tt(b[:, ::-1], now, step_i[:], MUL))
                    st.done(tt(a, a, b, ADD))
                    st.done(tt(nxt, nxt, a, ADD))
                    st.leave(c1 - c0)

            def latents(l, st):
                for n, (src, k1, width) in enumerate(((cqf, 3, QR), (kvf, 2, KVR))):
                    for k in range(k1):
                        dst = stat[:, 2 + n] if k == 0 else stat[:, 0]
                        ins = tt(dst, src[:, k], src[:, k], MUL)
                        if k:
                            st.done(ins)
                            ins = tt(stat[:, 2 + n], stat[:, 2 + n], stat[:, 0], ADD)
                        if k < k1 - 1:
                            st.done(ins)
                    ins.then_inc(rms_sums, 1)
                for v in (kvh, kvl):
                    dve.memset(v[:, 2 * L:2 * L + P].bitcast(f32), 0.0)
                dve.wait_ge(rms_stat, l * 2 + 2)
                for n, width in enumerate((QR, KVR)):
                    ins = ts(two(stat[:, 2 + n]), pair(2 + n), 1.0 / width, RMS_EPS, MUL, ADD)
                ins.then_inc(rms_var, 1)
                dve.wait_ge(kr_swap, l + 1)
                tt(two(stat[64:96, 4]), ps[64:96, 0:2, 0:HALF], two(rope_sin[64:96]), MUL)
                st.done(tt(kr[64:96], kr[64:96], rope_cos[64:96], MUL))
                tt(kr[64:96], kr[64:96], stat[64:96, 4], ADD).then_inc(kr_done, 1)
                dve.wait_ge(rms_sd, l + 1)
                for n in range(2):
                    ins = nc.vector.reciprocal(stat[:, 2 + n], stat[:, 2 + n])
                st.done(ins)
                for n, (src, hi, lo, k1, col) in enumerate(((cqf, cqh, cql, 3, PC_QG), (kvf, kvh3, kvl3, 2, PC_KG))):
                    for k in range(k1):
                        g = par[:, col + k:col + k + 1]
                        st.done(tt(src[:, k], src[:, k], stat[:, 2 + n], MUL))
                        st.done(ts(hi[:, k], src[:, k], g, None, MUL))
                        stt(lo[:, k], src[:, k], g, hi[:, k].bitcast(f32), MUL, SUB).then_inc(lat_ready, 1)

            def s5_outputs(l, st):
                for m in range(MT):
                    dve.wait_ge(y_ready, l * MT + (m + 1))
                    if m >= 2:
                        dve.wait_ge(gelu_done, l * MT + (m - 1))
                    stt(two(stat[:, m % 2]), two(ug[:, m]), par[:, PC_D + m:PC_D + m + 1],
                        ps[:, 2 * (m % 2):2 * (m % 2) + 2, 0:HALF], MUL, ADD).then_inc(y_taken, 1)
                for m in range(MT):
                    dve.wait_ge(gelu_done, l * MT + (m + 1))
                    st.done(ts(yh[:, m], ug[:, m], 1.0, None, MUL))
                    tt(yl[:, m], ug[:, m], yhf[:, m], SUB).then_inc(y_split, 1)
                for m in range(MT):
                    dve.wait_ge(glu_sig, l * MT + (m + 1))
                    follow(tt(slf[:, m], ug[:, m], stat[:, 2 + m % 2], MUL), glu_out, l * MT + (m + 1))
                    split_tile(st, sh[:, m], sl[:, m], slf[:, m]).then_inc(glu_done, 1)

            def heads(l, st):
                with loop(dve, 0, HEADS // 2) as i:
                    st.enter(i, 32)
                    h0 = l * HEADS + i * 2
                    scale = QKD ** -0.5
                    for b in range(2):
                        dve.wait_ge(q_swap, h0 + (b + 1))
                        tt(two(stat[64:96, 1 + b]), ps[64:96, 2 * b:2 * b + 2, 0:HALF], two(rope_sin[64:96]), MUL)
                        st.done(tt(qT[64:96, b], qT[64:96, b], rope_cos[64:96], MUL))
                        tt(qT[64:96, b], qT[64:96, b], stat[64:96, 1 + b], ADD).then_inc(q_ready, 1)

                    def row_max(b, j):
                        q0, nq = QT[j]
                        col = NQ * b + j
                        dve.wait_ge(s_done, (h0 + b) * NQ + (j + 1))
                        if nq == P:
                            diag, row, ax = ps[:, j, q0:q0 + P], ps[:, j, 0:q0 + P], AX.X
                        else:
                            diag, row, ax = ps[0:nq, 1, q0 - HALF:L - HALF], pair(0)[0:nq], AX.XY
                        st.done(tt(diag, diag, mask[0:nq, 0:nq], ADD))
                        st.done(nc.vector.tensor_reduce(small[0:nq, 0, col:col + 1], row, ax, ALU.max))
                        ts(small[0:nq, 1, col:col + 1], small[0:nq, 0, col:col + 1], -scale, None,
                           MUL).then_inc(nb_ready, 1)

                    def normalise(b, j):
                        q0, nq = QT[j]
                        col, buf = NQ * b + j, (NQ * b + j) % 2
                        dve.wait_ge(p_exp, (h0 + b) * NQ + (j + 1))
                        st.done(nc.vector.reciprocal(small[0:nq, 3, col:col + 1], small[0:nq, 2, col:col + 1]))
                        n = q0 + nq
                        ts(pr[0:nq, buf, 0:n], pr[0:nq, buf, 0:n], small[0:nq, 3, col:col + 1], None,
                           MUL).then_inc(p_ready, 1)

                    def take_o(b):
                        dve.wait_ge(oh_done, h0 + (b + 1))
                        rows = slice(64 * b, 64 * b + 64)
                        view = lambda ap: ap[rows, ds(i, 1)].rearrange("p a (h t) -> p (a h) t", h=2)
                        tt(view(ol), pair(3)[rows], view(ohf), SUB).then_inc(o_done, 1)

                    for b in range(2):
                        row_max(b, 0)
                        row_max(b, 1)
                        if b == 1:
                            take_o(0)
                        normalise(b, 0)
                        row_max(b, 2)
                        normalise(b, 1)
                        row_max(b, 3)
                        normalise(b, 2)
                        row_max(b, 4)
                        normalise(b, 3)
                        normalise(b, 4)
                    take_o(1)
                    st.leave(HEADS // 2)

            def merge(l, st):
                with loop(dve, 0, KD // 2) as i:
                    st.enter(i, 6)
                    for b in range(2):
                        k = ds(i * 2 + b, 1)
                        flat = lambda ap: ap[:, k].rearrange("p a t -> p (a t)")
                        for r in range(3):
                            n = 3 * b + r
                            dve.wait_ge(gate_sig, l * 24 + i * 6 + (n + 3))
                            dve.wait_ge(chunk_done, done_at(l, B_MERGE + 2 * n + 1) + i * 12)
                            dst = mlf[:, k].rearrange("p a (h t) -> p (a h) t", h=2) if r == 0 else two(stat[:, 2])
                            ins = tt(dst, two(stat[:, n % 2]), pair(2 * (n % 2) + 1), MUL)
                            follow(ins, merge_mul, l * 24 + i * 6 + (n + 3))
                            if r:
                                st.done(tt(flat(mlf), flat(mlf), stat[:, 2], ADD))
                        st.done(ts(flat(mh), flat(mlf), 1.0, None, MUL))
                        tt(flat(ml), flat(mlf), flat(mhf), SUB).then_inc(mix_done, 1)
                    st.leave(KD // 2)

            dve.sem_inc(hid_done, 2)
            dve.sem_inc(z_taken, 2)
            dve.sem_inc(conv_taken, 4)
            dve.sem_inc(merge_mul, 2)
            dve.sem_inc(o_done, 2)
            dve.memset(ones[:], 1.0).then_inc(ones_set, 1)
            dve.wait_ge(x_in, 16)
            dve.wait_ge(const_in, 16 * 5)
            for k in range(KD):
                ts(xh[:, k], z[:, k], 1.0, None, MUL).then_inc(first_hi, 1)
                dve.wait_ge(first_hi, k + 1)
                tt(xl[:, k], z[:, k], xhf[:, k], SUB).then_inc(x_ready, 1)
            with loop(dve, 0, DEPTH) as l:
                st = Steps(dve, dve_step, l, DVE_STEPS)
                s5_parameters(l, st)
                ffn(l, B_FFN1, 0, st)
                s5_tables(l, st)
                wait_apart(dve, f_taken, l * PAIRS + PAIRS)
                dve.memset(K[:], 0.0).then_inc(k_zero, 1)
                st.done(dve.memset(conv_u[:, 0:2], 0.0))
                cuts = [1, 17, 33, 49, NC]
                for m in range(MT):
                    conv_tile(l, m, st)
                    scan(l, cuts[m], cuts[m + 1], st)
                dve.sem_inc(scan_done, 1)
                latents(l, st)
                s5_outputs(l, st)
                heads(l, st)
                merge(l, st)
                layer_norm(l, 1, st, 1.0 / ALPHA, LN_EPS / ALPHA ** 2, lambda k: B_WO + k, 1)
                ffn(l, B_FFN2, 1, st)
                st.close()


ACT_STEPS, DVE_STEPS = 24, 651


_WEIGHTS = ("ffn1_w_gate", "ffn1_w_up", "ffn1_w_down", "w_in", "mla_w_uq", "mla_w_ukv", "mla_w_o", "conv_w_out",
            "s5_w_glu", "s5_w_out", "w_o", "ffn2_w_gate", "ffn2_w_up", "ffn2_w_down")


def _layout(inp):
    a = {n: np.ascontiguousarray(inp[n]) for n in _WEIGHTS}
    a["x_T"] = np.ascontiguousarray(np.concatenate([inp["meta"], inp["x"][0]], 0).T)
    tiles = lambda v: v.reshape(DEPTH, -1, P).transpose(0, 2, 1)
    cols = []
    for n in ("ln1", "ln2", "ln3"):
        cols += [tiles(inp[n + "_g"]), tiles(inp[n + "_b"])]
    cols += [tiles(inp["mla_q_norm_g"]), tiles(inp["mla_kv_norm_g"])]
    cols += [tiles(inp["conv_w"][:, j]) for j in range(CONV_K)] + [tiles(inp["conv_b"])]
    cols += [tiles(inp["s5_b_glu"]), tiles(inp["s5_d"].reshape(DEPTH, MIX))]
    a["par"] = np.ascontiguousarray(np.concatenate(cols, 2))

    def channels(v):
        v = v.reshape(DEPTH, MT, GROUPS // MT, 1, STATE)
        v = np.broadcast_to(v, (DEPTH, MT, GROUPS // MT, GROUP, STATE))
        return v.transpose(0, 2, 3, 1, 4).reshape(DEPTH, P, MT * STATE)

    def states(v):
        return v.reshape(DEPTH, PAIRS, 2, STATE).transpose(0, 2, 3, 1).reshape(DEPTH, P, PAIRS)

    log_dt = np.broadcast_to(inp["s5_log_dt"][:, :, None], (DEPTH, GROUPS, STATE))
    a["s5_par"] = np.ascontiguousarray(np.stack([np.concatenate([channels(v), states(v)], 2) for v in
                                                 (inp["s5_a_re"], inp["s5_a_im"], log_dt)], 2))

    def b_channels(v):
        v = v.reshape(DEPTH, MT, 4, 2, STATE, GROUP)
        out = np.zeros((DEPTH, 4, 2, GROUP, MT, 2, STATE), v.dtype)
        for g in range(2):
            out[:, :, g, :, :, g] = v[:, :, :, g].transpose(0, 2, 4, 1, 3)
        return out.reshape(DEPTH, P, MT * 2 * STATE)

    def b_states(v):
        v = v.reshape(DEPTH, PAIRS, 2, STATE, GROUP)
        out = np.zeros((DEPTH, 2, STATE, PAIRS, 2, GROUP), v.dtype)
        for g in range(2):
            out[:, g, :, :, g] = v[:, :, g].transpose(0, 2, 1, 3)
        return out.reshape(DEPTH, P, PAIRS * 2 * GROUP)

    a["s5_b"] = np.ascontiguousarray(np.stack([b_channels(inp["s5_b_re"]), b_channels(inp["s5_b_im"]),
                                               b_states(inp["s5_b_re"]), b_states(inp["s5_b_im"])], 2))
    a["s5_c"] = np.ascontiguousarray(np.stack([b_states(inp[n].transpose(0, 1, 3, 2))
                                               for n in ("s5_c_re", "s5_c_im")], 2))
    a["c_ident"] = np.eye(P, dtype=np.float32)
    a["c_mask"] = np.triu(np.full((P, P), -1e30, np.float32), 1)
    inv_freq = np.float32(10000.0) ** (-np.arange(0, ROPE, 2, dtype=np.float32) / np.float32(ROPE))
    ang = inv_freq[:, None].astype(np.float32) * np.arange(L, dtype=np.float32)[None, :]
    a["c_cos"] = np.concatenate([np.cos(ang)] * 2, 0).astype(np.float32)
    a["c_sin"] = np.concatenate([-np.sin(ang), np.sin(ang)], 0).astype(np.float32)
    a["c_swap"] = np.roll(np.eye(ROPE, dtype=np.float32), ROPE // 2, 1)
    return a


def kernel(**inputs):
    import concourse.bacc as bacc
    from concourse.bass_utils import run_bass_kernel_spmd

    nc = bacc.Bacc("TRN2", target_bir_lowering=False, num_devices=1)
    arrays = _layout(inputs)
    t = {n: nc.dram_tensor(f"in_{n}", a.shape, mybir.dt.from_np(a.dtype), kind="ExternalInput").ap()
         for n, a in arrays.items()}
    t["out"] = nc.dram_tensor("out_T", (D_MODEL, SEQ), mybir.dt.float32, kind="ExternalOutput").ap()
    build(nc, t)
    r = run_bass_kernel_spmd(nc, [{f"in_{n}": a for n, a in arrays.items()}], core_ids=[0])
    return np.ascontiguousarray(r.results[0]["out_T"].T)[None]
```

```python
import numpy as np
import concourse.bass as bass
from concourse import mybir
from contextlib import ExitStack

P = 128
D_MODEL, SEQ, DEPTH, N_META = 1024, 512, 2, 16
L = SEQ + N_META
HALF = L // 2
MIX = D_MODEL // 2
HEADS, NOPE, ROPE, VDIM = 8, 64, 32, 64
QKD = NOPE + ROPE
QR, KVR = 3 * D_MODEL // 8, D_MODEL // 4
CONV_K = 3
GROUP, GROUPS, STATE = 16, 32, 64
D_FF = P * ((8 * D_MODEL // 3 + P - 1) // P)
ALPHA = (2.0 * DEPTH) ** 0.25
LN_EPS, RMS_EPS = 1e-5, 1e-6
KD, NF, MT = D_MODEL // P, D_FF // P, MIX // P
TC = 8
NC = L // TC
HC = NC // 2
PAIRS = GROUPS // 2
QT = [(i * P, min(P, L - i * P)) for i in range((L + P - 1) // P)]
NQ = len(QT)
VREG = (NQ - 1) * P

C_CKV = QR
C_KR = QR + KVR
C_XBAR = C_KR + ROPE
C_B = C_XBAR + MIX
C_C = C_B + MIX
C_U = C_C + MIX
C_G = C_U + MIX
KR_AT = 64

SLOTS = 4
RAW = 2
AHEAD = SLOTS - 1
DOWN_CUT = [(0, 6), (6, 6), (12, 5), (17, 5)]
FFN_CH = 2 * NF + 4 * KD
B_FFN1 = 0
B_M1 = B_FFN1 + FFN_CH
N_M1 = 10
B_CONV = B_M1 + N_M1
B_GLU = B_CONV + 3 * MT
B_V = B_GLU + MT
B_HEAD = B_V + 2
B_MERGE = B_HEAD + 2 * HEADS
B_WO = B_MERGE + 6 * KD
B_FFN2 = B_WO + KD
CH = B_FFN2 + FFN_CH
assert CH % SLOTS == 0 and not (B_M1 | B_HEAD | B_MERGE | B_WO | B_FFN2) % SLOTS

ARENA_WORDS = 53100

PC_LN = 0
PC_QG, PC_KG = 48, 51
PC_CW, PC_CB = 53, 65
PC_GB, PC_D = 69, 73
PC_N = 77

TWO_PI_INV = float(np.float32(1 / (2 * np.pi)))
PI_A = 6.28125
PI_B = float(np.float32(np.round((2 * np.pi - PI_A) * 2 ** 20) / 2 ** 20))
PI_C = float(np.float32(2 * np.pi - PI_A - PI_B))
ROUND = 12582912.0
SIN_MAX = 3.1415925


class Steps:

    def __init__(self, eng, sem, layer, per_layer):
        self.eng, self.sem, self.base, self.per_layer = eng, sem, layer * per_layer, per_layer
        self.n, self.it, self.size, self.start = 0, None, 0, 0

    def done(self, ins):
        ins.then_inc(self.sem, 1)
        self.n += 1
        self.wait()

    def wait(self):
        at = self.base + self.n
        if self.it is not None:
            at = at + self.it * self.size
        self.eng.wait_ge(self.sem, at)

    def enter(self, it, size):
        self.it, self.size, self.start = it, size, self.n

    def leave(self, times):
        assert self.n - self.start == self.size, (self.n, self.start, self.size)
        self.n = self.start + self.size * times
        self.it = None

    def close(self):
        assert self.n == self.per_layer, (self.n, self.per_layer)


def build(nc, t):
    f32, f32r = mybir.dt.float32, mybir.dt.float32r
    ALU, ACT, AX = mybir.AluOpType, mybir.ActivationFunctionType, mybir.AxisListType
    ds = bass.ds

    ctx = ExitStack()
    with ctx:
        UNIT = L * 4
        base = (nc.sbuf_base + 31) // 32 * 32
        ctx.enter_context(nc.sbuf_tensor("arena", [P, ARENA_WORDS], f32))
        top = [base]

        def at(name, shape, dt, offset):
            return nc.alloc_sbuf_tensor_at(name, shape, dt, offset=offset)

        def new(name, shape, dt=f32):
            n = 4
            for s in shape[1:]:
                n *= s
            off = top[0]
            top[0] += (n + 31) // 32 * 32
            return at(name, shape, dt, off), off

        xh, _ = new("x_hi", [P, KD, L], f32r)
        xhf = xh.bitcast(f32)
        xl, o = new("x_lo", [P, KD, L], f32r)
        xlf = xl.bitcast(f32)
        w_raw, _ = new("w_raw", [P, RAW, 8 * P])
        w_hi, _ = new("w_hi", [P, SLOTS, 8 * P], f32r)
        w_lo, _ = new("w_lo", [P, SLOTS, 8 * P], f32r)
        M, m0 = new("mixer_region", [P, 52, L])
        U = lambda k: m0 + k * UNIT
        stat, stat_off = new("stat", [P, 5, L])
        ident, _ = new("ident", [P, P])
        ones, _ = new("ones", [P, P])
        mask, _ = new("mask", [P, P])
        rope_cos, _ = new("rope_cos", [P, L])
        rope_sin, _ = new("rope_sin", [P, L])
        swap, _ = new("swap", [P, ROPE])
        par, _ = new("par", [P, PC_N])
        s5lam, _ = new("s5_lambda", [P, 2, PAIRS])
        s5cf, _ = new("s5_coef", [P, 2, PAIRS])
        turn, _ = new("s5_turn", [P, 2, PAIRS])
        decay, _ = new("s5_decay", [P, PAIRS])
        bS, _ = new("s5_bbar_states", [P, 2, PAIRS * 2 * GROUP])
        kr, _ = new("k_rope", [P, L])
        small, _ = new("softmax_cols", [P, 4, 2 * NQ])
        assert top[0] <= base + ARENA_WORDS * 4, top[0]

        gh = at("hid_hi", [P, NF, L], f32r, U(0))
        gl = at("hid_lo", [P, NF, L], f32r, U(NF))
        glf = at("hid_rest", [P, NF, L], f32, U(NF))
        silu = at("silu", [P, 2, L], f32, U(44))
        z = at("ln_in", [P, KD, L], f32, U(44))
        cqh = at("cq_hi", [P, 3, L], f32r, U(0))
        cql = at("cq_lo", [P, 3, L], f32r, U(3))
        cqf = at("cq_raw", [P, 3, L], f32, U(3))
        kvh = at("ckv_hi", [P, 2 * L + P], f32r, U(6))
        kvo = U(6) + (2 * L + P) * 4
        kvl = at("ckv_lo", [P, 2 * L + P], f32r, kvo)
        kvf = at("ckv_raw", [P, 2, L], f32, kvo)
        lfS = at("s5_in_states", [P, 2, PAIRS, GROUP, TC], f32, U(44))
        lfT = at("s5_in", [P, 2, PAIRS, P], f32, U(11))
        u8 = at("s5_u_stacked", [P, 8, MT, NC], f32, U(19))
        decays = at("s5_decays", [P, PAIRS, NC], f32, U(23))
        turns = [at(n, [P, PAIRS, NC], f32, U(k)) for n, k in (("s5_turns_re", 0), ("s5_turns_im", 6))]
        cl = at("s5_out", [P, TC, 2, 512], f32, U(36))
        braw = at("s5_b_raw", [P, 2, 512], f32, U(31))
        bcomp = at("s5_b_own", [P, 2, PAIRS * GROUP], f32, U(33))
        craw = at("s5_c_raw", [P, 2, 512], f32, U(34))
        ug = at("s5_u", [P, TC, MT, NC], f32, U(27))
        X = at("s5_state", [P, 2, PAIRS, NC], f32, U(31))
        K = at("s5_toeplitz", [P, MT, TC, P], f32, U(19))
        yh = at("s5_y_hi", [P, MT, L], f32r, U(36))
        yl = at("s5_y_lo", [P, MT, L], f32r, U(40))
        zh = at("conv_hi", [P, MT, L], f32r, U(11))
        zl = at("conv_lo", [P, MT, L], f32r, U(15))
        zlf = at("conv_rest", [P, MT, L], f32, U(15))
        sh = at("s5_hi", [P, MT, L], f32r, U(19))
        sl = at("s5_lo", [P, MT, L], f32r, U(23))
        slf = at("s5_rest", [P, MT, L], f32, U(23))
        oh = at("att_hi", [P, MT, L], f32r, U(27))
        ol = at("att_lo", [P, MT, L], f32r, U(31))
        V = at("v", [P, NQ, HEADS * VDIM], f32, U(35))
        PT = at("probs_T", [P, NQ, L], f32, U(40))
        pr = at("probs", [P, 2, L], f32, U(45))
        qT = at("q", [P, 2, L], f32, U(47))
        kT = at("k", [P, 2, L], f32, U(49))
        vb = at("v_head", [P, 2, NQ, VDIM], f32, stat_off + 3 * UNIT)
        conv_u = at("conv_u", [P, L + 2], f32, stat_off + UNIT)
        mh = at("mix_hi", [P, KD, L], f32r, U(0))
        ml = at("mix_lo", [P, KD, L], f32r, U(36))
        mlf = at("mix_rest", [P, KD, L], f32, U(36))
        s5p = at("s5_params", [P, 12, PAIRS], f32, stat_off)
        tmp = at("s5_tmp", [P, 4, 512], f32, stat_off)

        ghf, yhf, ohf, mhf = (v.bitcast(f32) for v in (gh, yh, oh, mh))
        kvh3, kvl3 = (v[:, 0:2 * L].rearrange("p (k t) -> p k t", k=2) for v in (kvh, kvl))

        ps = ctx.enter_context(nc.psum_tensor("ps", [P, 8, 512], f32))
        pair = lambda k: ps[:, 2 * k:2 * k + 2, 0:HALF]
        two = lambda ap: ap.rearrange("p (h t) -> p h t", h=2)

        def sem(name):
            return ctx.enter_context(nc.semaphore(name))

        w_loaded = [sem(f"w_loaded{s}") for s in range(RAW)]
        w_rounded, w_split, chunk_done = sem("w_rounded"), sem("w_split"), sem("chunk_done")
        const_in, x_in, x_ready = sem("const_in"), sem("x_in"), sem("x_ready")
        par_in, s5p_in, b_in, c_in = sem("par_in"), sem("s5p_in"), sem("b_in"), sem("c_in")
        dve_step, act_step, passed = sem("dve_step"), sem("act_step"), sem("passed")
        silu_done, hid_done = sem("silu_done"), sem("hid_done")
        z_taken, ln_sums, ln_stat = sem("z_taken"), sem("ln_sums"), sem("ln_stat")
        ln_var, ln_sd, ln_scaled, ln_hi = sem("ln_var"), sem("ln_sd"), sem("ln_scaled"), sem("ln_hi")
        dt_done, trig_in, trig_done, s5_half = sem("dt_done"), sem("trig_in"), sem("trig_done"), sem("s5_half")
        m1_taken, lf_ready, lf_turned, lf_taken, cl_ready, f_ready = (
            sem("m1_taken"), sem("lf_ready"), sem("lf_turned"), sem("lf_taken"), sem("cl_ready"), sem("f_ready"))
        u_stacked, rms_taken = sem("u_stacked"), sem("rms_taken")
        f_taken, scan_done, conv_taken, conv_hi, conv_done = (sem("f_taken"), sem("scan_done"), sem("conv_taken"),
                                                              sem("conv_hi_done"), sem("conv_done"))
        rms_sums, rms_stat, rms_sd, rms_scaled, rms_hi, lat_ready = (
            sem("rms_sums"), sem("rms_stat"), sem("rms_sd"), sem("rms_scaled"), sem("rms_hi"),
            sem("lat_ready"))
        k_zero, k_ready, k_taken, y_ready, y_taken, gelu_done, yh_done, y_split = (
            sem("k_zero"), sem("k_ready"), sem("k_taken"), sem("y_ready"), sem("y_taken"), sem("gelu_done"),
            sem("yh_done"), sem("y_split"))
        glu_sig, glu_out, glu_hi, glu_done = sem("glu_sig"), sem("glu_out"), sem("glu_hi"), sem("glu_done")
        kr_swap, kr_done, kr_set, v_taken = sem("kr_swap"), sem("kr_done"), sem("kr_set"), sem("v_taken")
        q_copied, k_copied, q_swap, q_ready, vb_done = (sem("q_copied"), sem("k_copied"), sem("q_swap"),
                                                        sem("q_ready"), sem("vb_done"))
        s_done, nb_ready, p_exp, p_ready, t_done, pt_done, pv_done, oh_done, o_done = (
            sem("s_done"), sem("nb_ready"), sem("p_exp"), sem("p_ready"), sem("t_done"), sem("pt_done"),
            sem("pv_done"), sem("oh_done"), sem("o_done"))
        gate_sig, merge_mul, mix_rest, mix_hi_done, mix_done = (sem("gate_sig"), sem("merge_mul"), sem("mix_rest_done"),
                                                                sem("mix_hi_done"), sem("mix_done"))
        ones_set, first_hi = sem("ones_set"), sem("first_hi")

        block = ctx.enter_context(nc.Block())

        def wait_apart(eng, s, value):
            eng.wait_ge(s, value)
            eng.sem_inc(passed, 1)

        def loop(eng, start, end):
            eng.sem_inc(passed, 1)
            return eng.Fori(start, end)

        def done_at(l, c):
            return l * CH + (c + 1 + SLOTS)

        @block.sync
        def _(sp):
            def load(l, c, it_chunks, ncols, src, k):
                wait_apart(sp, w_split, l * CH + it_chunks + (c + 1))
                dst = w_raw[:, c % RAW, 0:ncols].rearrange("p (k m) -> p k m", k=k)
                sp.dma_start(dst, src).then_inc(w_loaded[c % RAW], 16)

            def rows(w, l, r0, nk, c0, nm):
                return w[ds(l, 1), r0:r0 + nk * P, ds(c0, nm)].rearrange("a (k p) m -> p (a k) m", p=P)

            def ffn(l, b0, wg, wu, wd):
                with sp.Fori(0, NF // 2) as i:
                    for j in range(2):
                        for n, w in enumerate((wg, wu)):
                            load(l, b0 + 2 * j + n, i * 4, 8 * P, rows(w, l, 0, KD, (i * 2 + j) * P, P), KD)
                with sp.Fori(0, KD) as d:
                    for n, (r, nk) in enumerate(DOWN_CUT):
                        load(l, b0 + 2 * NF + n, d * 4, nk * P, rows(wd, l, r * P, nk, d * P, P), nk)

            sp.dma_start(z[:], t["x_T"].rearrange("(k p) t -> p k t", p=P)).then_inc(x_in, 16)
            with sp.Fori(0, DEPTH) as l:
                ffn(l, B_FFN1, t["ffn1_w_gate"], t["ffn1_w_up"], t["ffn1_w_down"])
                w_in = t["w_in"]
                cols = [C_U + P * k for k in range(MT)] + [P * k for k in range(5)] + [C_KR - KR_AT]
                for m in range(MT):
                    cols += [C_XBAR + P * m, C_C + P * m, C_B + P * m]
                for n, c0 in enumerate(cols):
                    load(l, B_M1 + n, 0, 8 * P, rows(w_in, l, 0, KD, c0, P), KD)
                for m in range(MT):
                    load(l, B_GLU + m, 0, MT * P, rows(t["s5_w_glu"], l, 0, MT, m * P, P), MT)
                w_v = t["mla_w_ukv"].rearrange("l r (h s d) -> l r h s d", h=HEADS, s=2)
                for k in range(2):
                    src = w_v[ds(l, 1), k * P:(k + 1) * P, :, 1, :].rearrange("a p h d -> (a p) h d")
                    load(l, B_V + k, 0, HEADS * VDIM, src, HEADS)
                with sp.Fori(0, HEADS // 2) as i:
                    for b in range(2):
                        h = i * 2 + b
                        load(l, B_HEAD + 2 * b, i * 4, 3 * QKD, rows(t["mla_w_uq"], l, 0, 3, h * QKD, QKD), 3)
                        load(l, B_HEAD + 2 * b + 1, i * 4, 2 * P, rows(t["mla_w_ukv"], l, 0, 2, h * P, P), 2)
                with sp.Fori(0, KD // 2) as i:
                    for b in range(2):
                        for r, w in enumerate(("mla_w_o", "conv_w_out", "s5_w_out")):
                            n = 6 * b + 2 * r
                            load(l, B_MERGE + n, i * 12, 8 * P,
                                 rows(w_in, l, 0, KD, (i * 2 + b) * P + (C_G + r * D_MODEL), P), KD)
                            load(l, B_MERGE + n + 1, i * 12, MT * P, rows(t[w], l, 0, MT, (i * 2 + b) * P, P), MT)
                with sp.Fori(0, KD // 4) as i:
                    for n in range(4):
                        load(l, B_WO + n, i * 4, 8 * P, rows(t["w_o"], l, 0, KD, (i * 4 + n) * P, P), KD)
                ffn(l, B_FFN2, t["ffn2_w_gate"], t["ffn2_w_up"], t["ffn2_w_down"])
            for k in range(KD):
                sp.wait_ge(x_ready, 3 * KD * DEPTH + k + 1)
                sp.dma_start(t["out"][k * P:(k + 1) * P, :], z[:, k, N_META:L]).then_inc(x_in, 16)
            sp.wait_ge(x_in, 16 * (1 + KD))

        @block.gpsimd
        def _(pool):
            pool.sem_inc(w_split, RAW)
            with pool.Fori(0, DEPTH * CH // SLOTS) as i:
                for s in range(SLOTS):
                    pool.wait_ge(w_rounded, i * SLOTS + (s + 1))
                    pool.tensor_tensor(w_lo[:, s], w_raw[:, s % RAW], w_hi[:, s].bitcast(f32),
                                       ALU.subtract).then_inc(w_split, 1)

        @block.tensor
        def _(pe):
            pe.sem_inc(chunk_done, SLOTS)
            pe.sem_inc(t_done, 2)

            def split_ready(l, c, it_chunks=0):
                pe.wait_ge(w_split, l * CH + it_chunks + (c + 1 + RAW))

            def product(out, c, k0, hi, lo, n_tiles, first, last, m=P, kp=P, x_wait=None):
                s = c % SLOTS
                for k in range(n_tiles):
                    if x_wait is not None:
                        pe.wait_ge(x_ready, x_wait + (k + 1))
                    cols = slice(k * m, (k + 1) * m)
                    parts = ((w_hi, hi), (w_hi, lo), (w_lo, hi))
                    for n, (w, x) in enumerate(parts):
                        for h in range(2):
                            ins = nc.tensor.matmul(out[0:m, h], w[:, s, cols], x[:, k0 + k, h * HALF:(h + 1) * HALF],
                                                   start=first and k == 0 and n == 0,
                                                   stop=last and k == n_tiles - 1 and n == 2)
                return ins

            def sum_over_features(src, out):
                for h in range(2):
                    ins = nc.tensor.matmul(out[:, h], ones[:], src[:, h * HALF:(h + 1) * HALF], start=True, stop=True)
                return ins

            def layer_norm_middle(l, which):
                pe.wait_ge(ln_sums, (l * 3 + which) * KD + KD // 2)
                sum_over_features(stat[:, 1], pair(2)).then_inc(ln_stat, 1)

            def layer_norm_end(l, which):
                pe.wait_ge(ln_sums, (l * 3 + which) * KD + KD)
                sum_over_features(stat[:, 1], pair(2))
                sum_over_features(stat[:, 2], pair(3)).then_inc(ln_stat, 1)

            def ffn(l, b0, w):
                x0 = l * 24 + w * 16
                with loop(pe, 0, NF // 2) as i:
                    n0 = (l * 2 + w) * NF + i * 2
                    for j in range(2):
                        c = b0 + 2 * j
                        split_ready(l, c, i * 4)
                        pe.wait_ge(silu_done, n0 + (j + 1))
                        product(pair(2 * j), c, 0, xh, xl, KD, True, True,
                                x_wait=x0 if j == 0 else None).then_inc(chunk_done, 1)
                        split_ready(l, c + 1, i * 4)
                        pe.wait_ge(hid_done, n0 + (j + 1))
                        product(pair(2 * j + 1), c + 1, 0, xh, xl, KD, True, True).then_inc(chunk_done, 1)
                pe.wait_ge(hid_done, (l * 2 + w) * NF + (NF + 2))
                for part in range(2):
                    with loop(pe, 0, 2) as i:
                        for b in range(2):
                            dd = part * 4 + b
                            pe.wait_ge(z_taken, (l * 3 + 2 * w) * KD + i * 2 + (dd + 1))
                            for n, (r, nk) in enumerate(DOWN_CUT):
                                c = b0 + 2 * NF + 4 * dd + n
                                split_ready(l, c, i * 8)
                                product(pair(b), c, r, gh, gl, nk, n == 0, n == 3).then_inc(chunk_done, 1)
                    (layer_norm_middle, layer_norm_end)[part](l, 2 * w)

            def m1(l):
                for n in range(N_M1):
                    c = B_M1 + n
                    if n == MT:
                        turn_inputs(l)
                    split_ready(l, c)
                    pe.wait_ge(m1_taken, l * N_M1 + (n + 1))
                    if n >= MT:
                        pe.wait_ge(lf_taken, l * 8 + (2 * min(n - MT, MT - 1) + 2))
                    product(pair(n % 4), c, 0, xh, xl, KD, True, True,
                            x_wait=l * 24 + 8 if n == 0 else None).then_inc(chunk_done, 1)

            def turn_inputs(l):
                pe.wait_ge(lf_ready, l + 1)
                for n in range(8):
                    if n % 2 == 0:
                        pe.wait_ge(m1_taken, l * N_M1 + (n // 2 + 5))
                    for k in range(4):
                        p = 4 * (n // 2) + k
                        ins = nc.tensor.transpose(ps[:, n, k * P:(k + 1) * P],
                                                  lfS[:, n % 2, p].rearrange("p h s -> p (h s)"), ident[:])
                    ins.then_inc(lf_turned, 1)

            def latent_sums(l):
                for n in range(2):
                    pe.wait_ge(rms_sums, l * 2 + (n + 1))
                    pe.wait_ge(m1_taken, l * N_M1 + (N_M1 + 2 + n))
                    sum_over_features(stat[:, 3 + n], pair(2 + n)).then_inc(rms_stat, 1)
                wait_apart(pe, m1_taken, l * N_M1 + (N_M1 + 4))
                for h in range(2):
                    ins = nc.tensor.matmul(ps[64:96, 2 + h, 0:HALF], swap[64:96, :], kr[64:96, h * HALF:(h + 1) * HALF],
                                           start=True, stop=True)
                ins.then_inc(kr_swap, 1)

            def s5_states_in(l):
                pe.wait_ge(u_stacked, l * 128 + 128)
                for m in range(MT):
                    if m == 1:
                        pe.wait_ge(kr_done, l + 1)
                    if m == 2:
                        pe.wait_ge(rms_taken, l + 1)
                    for ri in range(2):
                        for q in range(4):
                            for g in range(2):
                                p = 4 * m + q
                                ins = nc.tensor.matmul(ps[64 * g:64 * g + 64, 2 * m + ri, q * NC:(q + 1) * NC],
                                                       lfT[:, ri, p, 64 * g:64 * g + 64], u8[:, 2 * q + g, m],
                                                       start=True, stop=True)
                    ins.then_inc(f_ready, 1)

            def conv(l):
                pe.wait_ge(f_taken, l * MT + MT)
                with loop(pe, 0, 3) as i:
                    for k in range(4):
                        split_ready(l, B_CONV + k, i * 4)
                        pe.wait_ge(conv_taken, l * 12 + i * 4 + (k + 1))
                        product(pair(k), B_CONV + k, 0, xh, xl, KD, True, True).then_inc(chunk_done, 1)

            def s5_toeplitz(l):
                pe.wait_ge(conv_taken, l * 12 + (12 + 4))
                pe.wait_ge(cl_ready, l + 1)
                for m in range(MT):
                    for q in range(4):
                        p = 4 * m + q
                        for ri in range(2):
                            ins = nc.tensor.matmul(ps[32 * q:32 * q + 32, m, 0:TC * 32],
                                                   bS[:, ri, p * 32:(p + 1) * 32],
                                                   cl[:, :, ri, p * 32:(p + 1) * 32],
                                                   start=ri == 0, stop=ri == 1)
                    ins.then_inc(k_ready, 1)

            def s5_outputs(l):
                pe.wait_ge(k_taken, l * PAIRS + PAIRS)
                pe.wait_ge(scan_done, l + 1)
                for m in range(MT):
                    a = 2 * (m % 2)
                    if m >= 2:
                        pe.wait_ge(y_taken, l * MT + (m - 1))
                    for j in range(TC):
                        for bank, (lo, up) in enumerate(((0, 4), (4, 8))):
                            s0 = max(j, lo)
                            if s0 >= up:
                                continue
                            nc.tensor.matmul(ps[:, a + bank, (s0 - lo) * NC:4 * NC], K[:, m, j, :],
                                             ug[:, s0 - j:up - j, m, :], start=j == 0, stop=False,
                                             skip_group_check=True)
                    for s in range(TC):
                        for ri in range(2):
                            for q in range(4):
                                p = 4 * m + q
                                ins = nc.tensor.matmul(
                                    ps[32 * q:32 * q + 32, a + s // 4, (s % 4) * NC:(s % 4 + 1) * NC],
                                    cl[:, s, ri, p * 32:(p + 1) * 32], X[:, ri, p, :],
                                    start=False, stop=ri == 1, skip_group_check=True)
                    ins.then_inc(y_ready, 1)

            def glu(l):
                pe.wait_ge(y_split, l * MT + MT)
                for m in range(MT):
                    c = B_GLU + m
                    split_ready(l, c)
                    product(pair(m), c, 0, yh, yl, MT, True, True).then_inc(chunk_done, 1)

            def values(l):
                pe.wait_ge(lat_ready, l * 5 + 5)
                pe.wait_ge(glu_sig, l * MT + MT)
                for k in range(2):
                    c = B_V + k
                    s = c % SLOTS
                    split_ready(l, c)
                    for i in range(NQ):
                        tok = slice(k * L + i * P, k * L + (i + 1) * P)
                        for n, (x, w) in enumerate(((kvh, w_hi), (kvl, w_hi), (kvh, w_lo))):
                            ins = nc.tensor.matmul(ps[:, i, :], x[:, tok], w[:, s, 0:HEADS * VDIM],
                                                   start=k == 0 and n == 0, stop=k == 1 and n == 2)
                    ins.then_inc(chunk_done, 1)

            def heads(l):
                with loop(pe, 0, HEADS // 2) as i:
                    h0 = l * HEADS + i * 2
                    pe.wait_ge(v_taken, l * NQ + NQ)
                    pe.wait_ge(o_done, h0 + 2)
                    for b in range(2):
                        c = B_HEAD + 2 * b
                        split_ready(l, c, i * 4)
                        product(pair(b), c, 0, cqh, cql, 3, True, True, m=QKD).then_inc(chunk_done, 1)
                        split_ready(l, c + 1, i * 4)
                        product(pair(3 - b), c + 1, 0, kvh3, kvl3, 2, True, True).then_inc(chunk_done, 1)
                    for b in range(2):
                        wait_apart(pe, q_copied, h0 + (b + 1))
                        for h in range(2):
                            ins = nc.tensor.matmul(ps[64:96, 2 * b + h, 0:HALF], swap[64:96, :],
                                                   qT[64:96, b, h * HALF:(h + 1) * HALF], start=True, stop=True)
                        ins.then_inc(q_swap, 1)
                    pe.wait_ge(q_ready, h0 + 2)
                    pe.wait_ge(k_copied, h0 + 2)
                    pe.wait_ge(kr_set, l + 1)

                    def scores(b, j):
                        q0, nq = QT[j]
                        if j < NQ - 1:
                            ins = nc.tensor.matmul(ps[:, j, 0:q0 + P], qT[0:QKD, b, q0:q0 + nq],
                                                   kT[0:QKD, b, 0:q0 + P], start=True, stop=True)
                        else:
                            for h in range(2):
                                ins = nc.tensor.matmul(ps[0:nq, h, 0:HALF], qT[0:QKD, b, q0:q0 + nq],
                                                       kT[0:QKD, b, h * HALF:(h + 1) * HALF], start=True, stop=True)
                        ins.then_inc(s_done, 1)

                    def transposes(b, j):
                        q0, nq = QT[j]
                        buf = (NQ * b + j) % 2
                        wait_apart(pe, p_ready, (h0 + b) * NQ + (j + 1))
                        wait_apart(pe, pt_done, (h0 + b) * NQ + (j + 1))
                        for k in range(j + 1):
                            k0, nk = QT[k]
                            if nk == P:
                                ins = nc.tensor.transpose(ps[:, 4 + buf, k * nq:(k + 1) * nq],
                                                          pr[0:nq, buf, k0:k0 + P], ident[0:nq, 0:nq])
                            else:
                                ins = nc.tensor.matmul(ps[0:nk, 4 + buf, k * nq:(k + 1) * nq],
                                                       pr[0:nq, buf, k0:k0 + nk], ident[0:nq, 0:nq],
                                                       start=True, stop=True)
                        ins.then_inc(t_done, 1)

                    def values_sum(b):
                        wait_apart(pe, pt_done, (h0 + b) * NQ + (NQ + 2))
                        wait_apart(pe, vb_done, h0 + (b + 1))
                        for half in range(2):
                            todo = [k for k in range(NQ) if QT[k][0] < (half + 1) * HALF]
                            for k in todo:
                                k0, nk = QT[k]
                                q0 = max(k0, half * HALF)
                                ins = nc.tensor.matmul(
                                    ps[64 * b:64 * b + 64, 6 + half, q0 - half * HALF:HALF],
                                    vb[0:nk, b, k, :], PT[0:nk, k, q0:(half + 1) * HALF],
                                    start=k == 0, stop=k == todo[-1], skip_group_check=True)
                        ins.then_inc(pv_done, 1)

                    for j in range(4):
                        scores(0, j)
                    transposes(0, 0)
                    transposes(0, 1)
                    scores(0, 4)
                    transposes(0, 2)
                    transposes(0, 3)
                    transposes(0, 4)
                    for j in range(4):
                        scores(1, j)
                    values_sum(0)
                    transposes(1, 0)
                    transposes(1, 1)
                    scores(1, 4)
                    transposes(1, 2)
                    transposes(1, 3)
                    transposes(1, 4)
                    values_sum(1)

            def merge(l):
                pe.wait_ge(o_done, l * HEADS + (HEADS + 2))
                with loop(pe, 0, KD // 2) as i:
                    for b in range(2):
                        for r, (yhi, ylo) in enumerate(((oh, ol), (zh, zl), (sh, sl))):
                            n = 3 * b + r
                            c = B_MERGE + 2 * n
                            split_ready(l, c, i * 12)
                            pe.wait_ge(gate_sig, l * 24 + i * 6 + (n + 1))
                            product(pair(2 * (n % 2)), c, 0, xh, xl, KD, True, True).then_inc(chunk_done, 1)
                            split_ready(l, c + 1, i * 12)
                            pe.wait_ge(merge_mul, l * 24 + i * 6 + (n + 1))
                            product(pair(2 * (n % 2) + 1), c + 1, 0, yhi, ylo, MT, True, True).then_inc(chunk_done, 1)

            def w_o(l):
                pe.wait_ge(mix_done, l * KD + KD)
                for part in range(2):
                    for b in range(4):
                        c = B_WO + part * 4 + b
                        split_ready(l, c)
                        pe.wait_ge(z_taken, (l * 3 + 1) * KD + (part * 4 + b + 1))
                        product(pair(b % 2), c, 0, mh, ml, KD, True, True).then_inc(chunk_done, 1)
                    (layer_norm_middle, layer_norm_end)[part](l, 1)

            pe.wait_ge(const_in, 16 * 5)
            pe.wait_ge(ones_set, 1)
            with loop(pe, 0, DEPTH) as l:
                ffn(l, B_FFN1, 0)
                m1(l)
                latent_sums(l)
                s5_states_in(l)
                conv(l)
                s5_toeplitz(l)
                s5_outputs(l)
                glu(l)
                values(l)
                heads(l)
                merge(l)
                w_o(l)
                ffn(l, B_FFN2, 1)

        @block.scalar
        def _(act):
            def ACTV(out, in_, f=ACT.Copy, **kw):
                return nc.scalar.activation(out, in_, f, **kw)

            def round_ahead(l, c, per4=0, i=None):
                c += AHEAD
                v, free = l * (CH // RAW) + (c // RAW + 1), l * CH + (c + 1)
                if i is not None:
                    v, free = v + i * (per4 * SLOTS // RAW), free + i * (per4 * SLOTS)
                act.wait_ge(chunk_done, free)
                act.wait_ge(w_loaded[c % RAW], v * 16)
                ACTV(w_hi[:, c % SLOTS], w_raw[:, c % RAW]).then_inc(w_rounded, 1)

            def layer_norm_end(l, which, st):
                n = l * 3 + which
                act.wait_ge(ln_var, n + 1)
                ACTV(stat[:, 2], stat[:, 2], ACT.Sqrt).then_inc(ln_sd, 1)
                for k in range(KD):
                    act.wait_ge(ln_scaled, n * KD + (k + 1))
                    col = PC_LN + which * 16 + k
                    st.done(ACTV(z[:, k], z[:, k], ACT.Identity, scale=par[:, col:col + 1],
                                 bias=par[:, col + 8:col + 9]))
                    ACTV(xh[:, k], z[:, k]).then_inc(ln_hi, 1)

            def ffn(l, b0, w, st):
                with act.Fori(0, NF // 2) as i:
                    n0 = (l * 2 + w) * NF + i * 2
                    for j in range(2):
                        c = b0 + 2 * j
                        round_ahead(l, c, 1, i)
                        act.wait_ge(chunk_done, done_at(l, c) + i * 4)
                        act.wait_ge(hid_done, n0 + (j + 1))
                        ACTV(two(silu[:, j]), pair(2 * j), ACT.Silu).then_inc(silu_done, 1)
                        round_ahead(l, c + 1, 1, i)
                b1 = b0 + 2 * NF
                last = b0 == B_FFN2
                with act.Fori(0, KD - last) as d:
                    for n in range(4):
                        round_ahead(l, b1 + n, 1, d)
                if last:
                    round_ahead(l, b1 + 4 * (KD - 1))
                layer_norm_end(l, 2 * w, st)

            act.sem_inc(silu_done, 2)
            act.sem_inc(gate_sig, 2)
            act.sem_inc(m1_taken, 4)
            act.sem_inc(pt_done, 2)
            for dst, name in ((ident[:], "c_ident"), (mask[:], "c_mask"), (rope_cos[64:96, :], "c_cos"),
                              (rope_sin[64:96, :], "c_sin"), (swap[64:96, :], "c_swap")):
                act.dma_start(dst, t[name]).then_inc(const_in, 16)

            with act.Fori(0, DEPTH) as l:
                st = Steps(act, act_step, l, ACT_STEPS)
                for c in range(AHEAD):
                    round_ahead(l, c - AHEAD)
                act.wait_ge(x_ready, l * 24 + 8)
                act.dma_start(par[:], t["par"][ds(l, 1)].rearrange("a p c -> (a p) c")).then_inc(par_in, 16)
                act.dma_start(s5p[:, 0:3], t["s5_par"][ds(l, 1)].rearrange("a p k c -> (a p) k c")).then_inc(s5p_in, 16)
                act.wait_ge(s5p_in, l * 16 + 16)
                ACTV(s5p[:, 2], s5p[:, 2], ACT.Exp).then_inc(dt_done, 1)
                act.wait_ge(trig_in, l + 1)
                ACTV(s5p[:, 3], s5p[:, 3], ACT.Exp)
                ACTV(s5p[:, 6], s5p[:, 4], ACT.Sin)
                ACTV(s5p[:, 7], s5p[:, 4], ACT.Sin, scale=0.5).then_inc(trig_done, 1)
                act.wait_ge(par_in, l * 16 + 16)
                ffn(l, B_FFN1, 0, st)

                act.wait_ge(x_ready, l * 24 + 16)
                for dst, name, done in ((braw, "s5_b", b_in), (bcomp, "s5_b_own", b_in), (craw, "s5_c", c_in)):
                    act.dma_start(dst[:], t[name][ds(l, 1)].rearrange("a p k c -> (a p) k c")).then_inc(done, 16)
                for n in range(N_M1):
                    c = B_M1 + n
                    if n == MT:
                        wait_apart(act, m1_taken, l * N_M1 + (MT + 4))
                        for qg in range(8):
                            act.dma_start(u8[:, qg].rearrange("p m c -> p (m c)"),
                                          ug[GROUP * qg:GROUP * (qg + 1)].rearrange("h s m c -> h s (m c)")
                                          ).then_inc(u_stacked, 16)
                        for k in range(8):
                            act.wait_ge(lf_turned, l * 8 + (k + 1))
                            ACTV(lfT[:, k % 2, 4 * (k // 2):4 * (k // 2) + 4],
                                 ps[:, k, :].rearrange("p (q n) -> p q n", q=4)).then_inc(lf_taken, 1)
                    round_ahead(l, c)
                    act.wait_ge(chunk_done, done_at(l, c))
                    src = pair(n % 4)
                    if n < MT:
                        for h in range(2):
                            out = ug[:, :, n, h * HC:(h + 1) * HC]
                            ins = ACTV(out, src[:, h].rearrange("p (c s) -> p s c", s=TC))
                        ins.then_inc(m1_taken, 1)
                    elif n < MT + 3:
                        ACTV(two(cqf[:, n - MT]), src).then_inc(m1_taken, 1)
                    elif n < MT + 5:
                        ACTV(two(kvf[:, n - MT - 3]), src).then_inc(m1_taken, 1)
                    else:
                        ACTV(two(kr[64:96]), src[64:96]).then_inc(m1_taken, 1)
                for n in range(3 * MT):
                    round_ahead(l, B_CONV + n)
                wait_apart(act, k_zero, l + 1)
                for m in range(MT):
                    act.wait_ge(k_ready, l * MT + (m + 1))
                    for q in range(4):
                        r = slice(32 * q, 32 * q + 32)
                        ACTV(K[r, m, :, r], ps[r, m, 0:TC * 32].rearrange("p (j o) -> p j o", j=TC)).then_inc(k_taken, 1)
                act.wait_ge(rms_taken, l + 1)
                ACTV(stat[:, 3:5], stat[:, 3:5], ACT.Sqrt).then_inc(rms_sd, 1)
                for m in range(MT):
                    act.wait_ge(y_taken, l * MT + (m + 1))
                    ACTV(ug[:, :, m], ug[:, :, m], ACT.Gelu_apprx_tanh).then_inc(gelu_done, 1)
                for b in range(2):
                    ins = ACTV(kT[64:96, b], kr[64:96])
                ins.then_inc(kr_set, 1)
                for m in range(MT):
                    round_ahead(l, B_GLU + m)
                    act.wait_ge(chunk_done, done_at(l, B_GLU + m))
                    if m >= 2:
                        act.wait_ge(glu_out, l * MT + (m - 1))
                    ACTV(two(stat[:, 2 + m % 2]), pair(m), ACT.Sigmoid,
                         bias=par[:, PC_GB + m:PC_GB + m + 1]).then_inc(glu_sig, 1)
                for k in range(2):
                    round_ahead(l, B_V + k)
                act.wait_ge(chunk_done, done_at(l, B_V + 1))
                for k in range(NQ):
                    ACTV(V[:, k], ps[:, k, :]).then_inc(v_taken, 1)
                wait_apart(act, glu_done, l * MT + MT)

                with act.Fori(0, HEADS // 2) as i:
                    h0 = l * HEADS + i * 2

                    def take_qkv(b):
                        c = B_HEAD + 2 * b
                        round_ahead(l, c, 1, i)
                        act.wait_ge(chunk_done, done_at(l, c) + i * 4)
                        ACTV(two(qT[0:QKD, b]), pair(b)[0:QKD]).then_inc(q_copied, 1)
                        round_ahead(l, c + 1, 1, i)
                        act.wait_ge(chunk_done, done_at(l, c + 1) + i * 4)
                        ACTV(two(kT[0:NOPE, b]), pair(3 - b)[0:NOPE]).then_inc(k_copied, 1)
                        if b == 0:
                            wait_apart(act, v_taken, l * NQ + NQ)
                        ACTV(vb[:, b], V[:, :, ds((i * 2 + b) * VDIM, VDIM)]).then_inc(vb_done, 1)

                    def exps(b, j):
                        n, buf = (h0 + b) * NQ + (j + 1), (NQ * b + j) % 2
                        q0, nq = QT[j]
                        act.wait_ge(nb_ready, n)
                        act.wait_ge(t_done, n)
                        col = NQ * b + j
                        src, dst = (ps[:, j, 0:q0 + P], pr[:, buf, 0:q0 + P]) if nq == P else (
                            pair(0)[0:nq], two(pr[0:nq, buf]))
                        ACTV(dst, src, ACT.Exp, scale=QKD ** -0.5, bias=small[0:nq, 1, col:col + 1],
                             accum_out=small[0:nq, 2, col:col + 1]).then_inc(p_exp, 1)

                    def copy_t(b, j):
                        n, bank = (h0 + b) * NQ + (j + 3), 4 + (NQ * b + j) % 2
                        q0, nq = QT[j]
                        act.wait_ge(t_done, n)
                        if nq == P:
                            ins = ACTV(PT[:, 0:j + 1, q0:q0 + P],
                                       ps[:, bank, 0:(j + 1) * P].rearrange("p (k q) -> p k q", q=P))
                        else:
                            ACTV(PT[:, 0:j, q0:q0 + nq], ps[:, bank, 0:j * nq].rearrange("p (k q) -> p k q", q=nq))
                            ins = ACTV(PT[0:nq, j, q0:q0 + nq], ps[0:nq, bank, j * nq:(j + 1) * nq])
                        ins.then_inc(pt_done, 1)

                    def take_o(b):
                        wait_apart(act, pv_done, h0 + (b + 1))
                        ACTV(oh[64 * b:64 * b + 64, ds(i, 1)].rearrange("p a (h t) -> p (a h) t", h=2),
                             pair(3)[64 * b:64 * b + 64]).then_inc(oh_done, 1)

                    take_qkv(0)
                    take_qkv(1)
                    for b in range(2):
                        exps(b, 0)
                        exps(b, 1)
                        if b == 1:
                            take_o(0)
                        copy_t(b, 0)
                        exps(b, 2)
                        copy_t(b, 1)
                        exps(b, 3)
                        copy_t(b, 2)
                        exps(b, 4)
                        copy_t(b, 3)
                        copy_t(b, 4)
                    take_o(1)

                with act.Fori(0, KD // 2) as i:
                    for n in range(6):
                        c = B_MERGE + 2 * n
                        round_ahead(l, c, 3, i)
                        act.wait_ge(chunk_done, done_at(l, c) + i * 12)
                        act.wait_ge(merge_mul, l * 24 + i * 6 + (n + 1))
                        ACTV(two(stat[:, n % 2]), pair(2 * (n % 2)), ACT.Sigmoid).then_inc(gate_sig, 1)
                        round_ahead(l, c + 1, 3, i)
                for n in range(KD):
                    round_ahead(l, B_WO + n)
                layer_norm_end(l, 1, st)
                ffn(l, B_FFN2, 1, st)
                st.close()

        @block.vector
        def _(dve):
            tt, ts, stt = nc.vector.tensor_tensor, nc.vector.tensor_scalar, nc.vector.scalar_tensor_tensor
            MUL, ADD, SUB = ALU.mult, ALU.add, ALU.subtract

            def follow(ins, s, value):
                ins.then_inc(s, 1)
                dve.wait_ge(s, value)

            def split_tile(st, hi, lo, rest, after=None):
                st.done(ts(hi, rest, 1.0, None, MUL))
                return tt(lo, rest, hi.bitcast(f32), SUB)

            def take_z(l, which, st, scale, i, k, c, deviate):
                kk = ds(i * 2 + k, 1)
                one = lambda ap: ap[:, kk].rearrange("p a (h t) -> p (a h) t", h=2)
                flat = lambda ap: ap[:, kk].rearrange("p a t -> p (a t)")
                dve.wait_ge(chunk_done, c)
                ins = stt(one(z), pair(k % 2), scale, one(xhf), MUL, ADD)
                follow(ins, z_taken, (l * 3 + which) * KD + i * 2 + (k + 3))
                st.done(tt(flat(z), flat(z), flat(xlf), ADD))
                if not deviate:
                    follow(tt(stat[:, 1], stat[:, 1], flat(z), ADD), ln_sums, (l * 3 + which) * KD + i * 2 + (k + 1))
                else:
                    st.done(tt(flat(z), flat(z), stat[:, 0], SUB))
                    tt(stat[:, 1], stat[:, 1], flat(z), ADD)
                    st.done(tt(stat[:, 3], flat(z), flat(z), MUL))
                    follow(tt(stat[:, 2], stat[:, 2], stat[:, 3], ADD), ln_sums,
                           (l * 3 + which) * KD + i * 2 + (k + 1))

            def layer_norm(l, which, st, scale, eps, chunk_of, per_tile):
                n = l * 3 + which
                dve.memset(stat[:, 1], 0.0)
                st.done(dve.memset(stat[:, 2], 0.0))
                with loop(dve, 0, 2) as i:
                    st.enter(i, 2)
                    for k in range(2):
                        take_z(l, which, st, scale, i, k, done_at(l, chunk_of(k)) + i * 2 * per_tile, False)
                    st.leave(2)
                dve.wait_ge(ln_stat, 2 * n + 1)
                st.done(ts(two(stat[:, 0]), pair(2), 1.0 / (D_MODEL // 2), None, MUL))
                for k in range(KD // 2):
                    tt(z[:, k], z[:, k], stat[:, 0], SUB)
                st.done(stt(stat[:, 1], stat[:, 0], -float(KD // 2), stat[:, 1], MUL, ADD))
                for k in range(KD // 2):
                    st.done(tt(stat[:, 3], z[:, k], z[:, k], MUL))
                    st.done(tt(stat[:, 2], stat[:, 2], stat[:, 3], ADD))
                with loop(dve, 2, 4) as i:
                    st.enter(i - 2, 6)
                    for k in range(2):
                        take_z(l, which, st, scale, i, k, done_at(l, chunk_of(k)) + i * 2 * per_tile, True)
                    st.leave(2)
                dve.wait_ge(ln_stat, 2 * n + 2)
                st.done(ts(two(stat[:, 0]), pair(2), 1.0 / D_MODEL, None, MUL))
                ts(two(stat[:, 2]), pair(3), 1.0 / D_MODEL, eps, MUL, ADD)
                st.done(tt(stat[:, 3], stat[:, 0], stat[:, 0], MUL))
                tt(stat[:, 2], stat[:, 2], stat[:, 3], SUB).then_inc(ln_var, 1)
                dve.wait_ge(ln_sd, n + 1)
                st.done(nc.vector.reciprocal(stat[:, 1], stat[:, 2]))
                st.done(tt(stat[:, 3], stat[:, 0], stat[:, 1], MUL))
                for k in range(KD + 1):
                    if k < KD:
                        st.done(tt(z[:, k], z[:, k], stat[:, 1], MUL))
                        tt(z[:, k], z[:, k], stat[:, 3], SUB).then_inc(ln_scaled, 1)
                    if k:
                        dve.wait_ge(ln_hi, n * KD + k)
                        tt(xl[:, k - 1], z[:, k - 1], xhf[:, k - 1], SUB).then_inc(x_ready, 1)

            def ffn(l, b0, w, st):
                with loop(dve, 0, NF // 2) as i:
                    st.enter(i, 4)
                    n0 = (l * 2 + w) * NF + i * 2
                    for j in range(2):
                        f = ds(i * 2 + j, 1)
                        flat = lambda ap: ap[:, f].rearrange("p a t -> p (a t)")
                        dve.wait_ge(silu_done, n0 + (j + 3))
                        dve.wait_ge(chunk_done, done_at(l, b0 + 2 * j + 1) + i * 4)
                        st.done(tt(glf[:, f].rearrange("p a (h t) -> p (a h) t", h=2), two(silu[:, j]),
                                   pair(2 * j + 1), MUL))
                        st.done(ts(flat(gh), flat(glf), 1.0, None, MUL))
                        tt(flat(gl), flat(glf), flat(ghf), SUB).then_inc(hid_done, 1)
                    st.leave(NF // 2)
                layer_norm(l, 2 * w, st, 0.5 / ALPHA, LN_EPS / ALPHA ** 2,
                           lambda k: b0 + 2 * NF + 4 * k + 3, 4)

            def s5_parameters(l, st):
                q = lambda k: s5p[:, k]
                dve.wait_ge(dt_done, l + 1)
                tt(q(3), q(2), q(0), MUL)
                st.done(tt(q(4), q(2), q(1), MUL))
                st.done(ts(q(5), q(4), TWO_PI_INV, ROUND, MUL, ADD))
                st.done(ts(q(5), q(5), ROUND, None, SUB))
                for c in (PI_A, PI_B, PI_C):
                    st.done(stt(q(4), q(5), -c, q(4), MUL, ADD))
                ts(q(4), q(4), SIN_MAX, -SIN_MAX, ALU.min, ALU.max).then_inc(trig_in, 1)
                dve.wait_ge(trig_done, l + 1)
                st.done(tt(q(7), q(7), q(7), MUL))
                st.done(ts(q(7), q(7), -2.0, 1.0, MUL, ADD))
                tt(s5lam[:, 0], q(3), q(7), MUL)
                tt(s5lam[:, 1], q(3), q(6), MUL)
                mag, re, im = q(3), q(7), q(6)
                for k in range(3):
                    tt(q(8), re, re, MUL)
                    tt(q(9), im, im, MUL)
                    st.done(tt(q(10), re, im, MUL))
                    re, im, up = turn[:, 0], turn[:, 1], decay[:]
                    tt(up, mag, mag, MUL)
                    tt(re, q(8), q(9), SUB)
                    st.done(ts(im, q(10), 2.0, None, MUL))
                    mag = up
                tt(q(8), re, re, MUL)
                st.done(tt(q(9), im, im, MUL))
                st.done(tt(q(8), q(8), q(9), ADD))
                st.done(ts(q(8), q(8), -0.5, 1.5, MUL, ADD))
                tt(re, re, q(8), MUL)
                st.done(tt(im, im, q(8), MUL))
                tt(q(5), q(0), q(0), MUL)
                st.done(tt(q(8), q(1), q(1), MUL))
                st.done(tt(q(5), q(5), q(8), ADD))
                nc.vector.reciprocal(q(5), q(5))
                st.done(ts(q(8), s5lam[:, 0], -1.0, None, ADD))
                tt(q(3), q(8), q(0), MUL)
                tt(q(4), s5lam[:, 1], q(1), MUL)
                tt(q(6), s5lam[:, 1], q(0), MUL)
                st.done(tt(q(7), q(8), q(1), MUL))
                tt(q(3), q(3), q(4), ADD)
                st.done(tt(q(6), q(6), q(7), SUB))
                tt(s5cf[:, 0], q(3), q(5), MUL)
                tt(s5cf[:, 1], q(6), q(5), MUL)
                st.done(ts(q(11), q(8), 1.0, None, MUL))

            def s5_tables(l, st):
                def cmul(out, ar, ai, br, bi, op_r, op_i, n):
                    p4 = [tmp[:, k, 0:PAIRS * n].rearrange("p (q h) -> p q h", q=PAIRS) for k in range(4)]
                    tt(p4[0], ar, br, MUL)
                    tt(p4[1], ai, bi, MUL)
                    tt(p4[2], ar, bi, MUL)
                    st.done(tt(p4[3], ai, br, MUL))
                    flat = len(out[0].shape) == 2
                    f = (lambda ap: ap.rearrange("p q h -> p (q h)")) if flat else (lambda ap: ap)
                    tt(out[0], f(p4[0]), f(p4[1]), op_r)
                    st.done(tt(out[1], f(p4[2]), f(p4[3]), op_i))

                def each(ap, n):
                    return ap.unsqueeze(2).to_broadcast([P, PAIRS, n])

                block = ("p (q h) -> p q h", dict(q=PAIRS))
                as_ = lambda ap: ap.rearrange(block[0], **block[1])
                own = lambda ap: ap[:, 0:PAIRS * GROUP].rearrange("p (q h) -> p q h", q=PAIRS)
                dve.wait_ge(b_in, l * 32 + 32)
                cmul([bcomp[:, 0], bcomp[:, 1]], each(s5cf[:, 0], GROUP), each(s5cf[:, 1], GROUP), own(bcomp[:, 0]),
                     own(bcomp[:, 1]), SUB, ADD, GROUP)
                for j in range(TC):
                    br, bi = (own(bcomp[:, n]) if j == 0 else lfS[:, n, :, :, TC - j] for n in range(2))
                    cmul([lfS[:, n, :, :, TC - 1 - j] for n in range(2)], each(s5lam[:, 0], GROUP),
                         each(s5lam[:, 1], GROUP), br, bi, SUB, ADD, GROUP)
                dve.sem_inc(lf_ready, 1)
                cmul([bS[:, 0], bS[:, 1]], each(s5cf[:, 0], 32), each(s5cf[:, 1], 32), as_(braw[:, 0]),
                     as_(braw[:, 1]), SUB, ADD, 32)
                wr, wi = turns
                dve.memset(wr[:, :, 0:1], 1.0)
                dve.memset(wi[:, :, 0:1], 0.0)
                dve.memset(decays[:, :, 0:1], 0.0)
                ts(decays[:, :, 1:NC], decay[:].unsqueeze(2).to_broadcast([P, PAIRS, NC - 1]), 1.0, None, MUL)
                for n in range(2):
                    ins = ts(turns[n][:, :, 1], turn[:, n], 1.0, None, MUL)
                st.done(ins)
                k = 1
                while k < NC - 1:
                    w = min(k, NC - 1 - k)
                    wk = [v[:, :, k:k + 1].to_broadcast([P, PAIRS, w]) for v in turns]
                    cmul([v[:, :, k + 1:k + 1 + w] for v in turns], wk[0], wk[1], wr[:, :, 1:1 + w],
                         wi[:, :, 1:1 + w], SUB, ADD, w)
                    k += w
                dve.wait_ge(c_in, l * 16 + 16)
                dve.wait_ge(lf_turned, l * 8 + 8)
                ts(cl[:, 0, 0], craw[:, 0], 1.0, None, MUL)
                st.done(ts(cl[:, 0, 1], craw[:, 1], -1.0, None, MUL))
                for j in range(1, TC):
                    cmul([cl[:, j, 0], cl[:, j, 1]], each(s5lam[:, 0], 32), each(s5lam[:, 1], 32),
                         as_(cl[:, j - 1, 0]), as_(cl[:, j - 1, 1]), ADD, SUB, 32)
                dve.sem_inc(cl_ready, 1)

            def conv_tile(l, m, st):
                n0 = 3 * m

                def there(n):
                    dve.wait_ge(chunk_done, done_at(l, B_CONV + n0 + n))
                    return pair((n0 + n) % 4)

                def taken(ins, n):
                    follow(ins, conv_taken, l * 12 + (n0 + n + 5))

                taken(ts(two(stat[:, 0]), there(0), 1.0, None, MUL), 0)
                taken(tt(two(conv_u[:, 2:]), two(stat[:, 0]), there(1), MUL), 1)
                tap = lambda j: par[:, PC_CW + 4 * j + m:PC_CW + 4 * j + m + 1]
                st.done(ts(stat[:, 0], conv_u[:, 2:], tap(2), par[:, PC_CB + m:PC_CB + m + 1], MUL, ADD))
                for j in (1, 0):
                    st.done(stt(stat[:, 0], conv_u[:, j:j + L], tap(j), stat[:, 0], MUL, ADD))
                taken(tt(two(zlf[:, m]), two(stat[:, 0]), there(2), MUL), 2)
                split_tile(st, zh[:, m], zl[:, m], zlf[:, m]).then_inc(conv_done, 1)

            def scan(l, st):
                st.done(dve.memset(X[:, :, :, 0:1].rearrange("p r q c -> p (r q) c"), 0.0))
                N = NC - 1
                t2 = [stat[:, n, 0:4 * N].rearrange("p (q c) -> p q c", q=4) for n in range(2)]
                for m in range(MT):
                    dve.wait_ge(f_ready, l * MT + (m + 1))
                    fr, fi = (ps[:, 2 * m + n, 0:4 * NC].rearrange("p (q c) -> p q c", q=4)[:, :, 0:N] for n in range(2))
                    wr, wi = (v[:, 4 * m:4 * m + 4, 1:NC] for v in turns)
                    gr, gi = (X[:, n, 4 * m:4 * m + 4, 1:NC] for n in range(2))
                    tt(gr, fr, wr, MUL)
                    tt(t2[0], fi, wi, MUL)
                    tt(gi, fi, wr, MUL)
                    follow(tt(t2[1], fr, wi, MUL), f_taken, l * MT + (m + 1))
                    tt(gr, gr, t2[0], ADD)
                    ins = tt(gi, gi, t2[1], SUB)
                    st.done(ins)
                for n in range(2):
                    y = X[:, n].rearrange("p q c -> p (q c)")
                    ins = nc.vector.tensor_tensor_scan(y, decays[:].rearrange("p q c -> p (q c)"), y, 0.0, MUL, ADD)
                st.done(ins)
                for m in range(MT):
                    a, b, c, d = (stat[:, n // 2, n % 2 * HALF:(n % 2 + 1) * HALF] for n in range(4))
                    wr, wi = (v[:, 4 * m:4 * m + 4].rearrange("p q c -> p (q c)") for v in turns)
                    yr, yi = (X[:, n, 4 * m:4 * m + 4].rearrange("p q c -> p (q c)") for n in range(2))
                    tt(a, yr, wr, MUL)
                    tt(b, yi, wi, MUL)
                    tt(c, yr, wi, MUL)
                    st.done(tt(d, yi, wr, MUL))
                    tt(yr, a, b, SUB)
                    ins = tt(yi, c, d, ADD)
                    if m < MT - 1:
                        st.done(ins)
                follow(ins, scan_done, l + 1)
                dve.memset(K[:], 0.0).then_inc(k_zero, 1)

            def latent_sums(l, st):
                for n, (src, k1, m0_) in enumerate(((cqf, 3, MT), (kvf, 2, MT + 3))):
                    for k in range(k1):
                        dve.wait_ge(m1_taken, l * N_M1 + (m0_ + k + 5))
                        dst = stat[:, 3 + n] if k == 0 else stat[:, 0]
                        ins = tt(dst, src[:, k], src[:, k], MUL)
                        if k:
                            st.done(ins)
                            ins = tt(stat[:, 3 + n], stat[:, 3 + n], stat[:, 0], ADD)
                        if k < k1 - 1:
                            st.done(ins)
                    ins.then_inc(rms_sums, 1)
                dve.wait_ge(kr_swap, l + 1)
                tt(two(stat[64:96, 0]), ps[64:96, 2:4, 0:HALF], two(rope_sin[64:96]), MUL)
                st.done(tt(kr[64:96], kr[64:96], rope_cos[64:96], MUL))
                follow(tt(kr[64:96], kr[64:96], stat[64:96, 0], ADD), kr_done, l + 1)
                dve.wait_ge(rms_stat, l * 2 + 2)
                for n, width in enumerate((QR, KVR)):
                    ins = ts(two(stat[:, 3 + n]), pair(2 + n), 1.0 / width, RMS_EPS, MUL, ADD)
                ins.then_inc(rms_taken, 1)

            def latents(l, st):
                for v in (kvh, kvl):
                    dve.memset(v[:, 2 * L:2 * L + P].bitcast(f32), 0.0)
                dve.wait_ge(rms_sd, l + 1)
                for n in range(2):
                    ins = nc.vector.reciprocal(stat[:, 3 + n], stat[:, 3 + n])
                st.done(ins)
                for n, (src, hi, lo, k1, col) in enumerate(((cqf, cqh, cql, 3, PC_QG), (kvf, kvh3, kvl3, 2, PC_KG))):
                    for k in range(k1):
                        g = par[:, col + k:col + k + 1]
                        st.done(tt(src[:, k], src[:, k], stat[:, 3 + n], MUL))
                        st.done(ts(hi[:, k], src[:, k], g, None, MUL))
                        stt(lo[:, k], src[:, k], g, hi[:, k].bitcast(f32), MUL, SUB).then_inc(lat_ready, 1)

            def s5_outputs(l, st):
                for m in range(MT):
                    dve.wait_ge(y_ready, l * MT + (m + 1))
                    half = lambda ap: ap.rearrange("p (h s) c -> p h s c", h=2)
                    stt(half(ug[:, :, m]), half(ug[:, :, m]), par[:, PC_D + m:PC_D + m + 1],
                        ps[:, 2 * (m % 2):2 * (m % 2) + 2, 0:HALF].rearrange("p h (s c) -> p h s c", s=TC // 2),
                        MUL, ADD).then_inc(y_taken, 1)
                tok = lambda ap: ap.rearrange("p (c s) -> p c s", s=TC)
                for m in range(MT):
                    dve.wait_ge(gelu_done, l * MT + (m + 1))
                    gelu = ug[:, :, m].rearrange("p s c -> p c s")
                    st.done(ts(tok(yh[:, m]), gelu, 1.0, None, MUL))
                    tt(tok(yl[:, m]), gelu, tok(yhf[:, m]), SUB).then_inc(y_split, 1)
                for m in range(MT):
                    dve.wait_ge(glu_sig, l * MT + (m + 1))
                    gelu = ug[:, :, m].rearrange("p s c -> p c s")
                    follow(tt(tok(slf[:, m]), gelu, tok(stat[:, 2 + m % 2]), MUL), glu_out, l * MT + (m + 1))
                    split_tile(st, sh[:, m], sl[:, m], slf[:, m]).then_inc(glu_done, 1)

            def heads(l, st):
                with loop(dve, 0, HEADS // 2) as i:
                    st.enter(i, 32)
                    h0 = l * HEADS + i * 2
                    scale = QKD ** -0.5
                    for b in range(2):
                        dve.wait_ge(q_swap, h0 + (b + 1))
                        tt(two(stat[64:96, 1 + b]), ps[64:96, 2 * b:2 * b + 2, 0:HALF], two(rope_sin[64:96]), MUL)
                        st.done(tt(qT[64:96, b], qT[64:96, b], rope_cos[64:96], MUL))
                        tt(qT[64:96, b], qT[64:96, b], stat[64:96, 1 + b], ADD).then_inc(q_ready, 1)

                    def row_max(b, j):
                        q0, nq = QT[j]
                        col = NQ * b + j
                        dve.wait_ge(s_done, (h0 + b) * NQ + (j + 1))
                        if nq == P:
                            diag, row, ax = ps[:, j, q0:q0 + P], ps[:, j, 0:q0 + P], AX.X
                        else:
                            diag, row, ax = ps[0:nq, 1, q0 - HALF:L - HALF], pair(0)[0:nq], AX.XY
                        st.done(tt(diag, diag, mask[0:nq, 0:nq], ADD))
                        st.done(nc.vector.tensor_reduce(small[0:nq, 0, col:col + 1], row, ax, ALU.max))
                        ts(small[0:nq, 1, col:col + 1], small[0:nq, 0, col:col + 1], -scale, None,
                           MUL).then_inc(nb_ready, 1)

                    def normalise(b, j):
                        q0, nq = QT[j]
                        col, buf = NQ * b + j, (NQ * b + j) % 2
                        dve.wait_ge(p_exp, (h0 + b) * NQ + (j + 1))
                        st.done(nc.vector.reciprocal(small[0:nq, 3, col:col + 1], small[0:nq, 2, col:col + 1]))
                        n = q0 + nq
                        ts(pr[0:nq, buf, 0:n], pr[0:nq, buf, 0:n], small[0:nq, 3, col:col + 1], None,
                           MUL).then_inc(p_ready, 1)

                    def take_o(b):
                        dve.wait_ge(oh_done, h0 + (b + 1))
                        rows = slice(64 * b, 64 * b + 64)
                        view = lambda ap: ap[rows, ds(i, 1)].rearrange("p a (h t) -> p (a h) t", h=2)
                        tt(view(ol), pair(3)[rows], view(ohf), SUB).then_inc(o_done, 1)

                    for b in range(2):
                        row_max(b, 0)
                        row_max(b, 1)
                        if b == 1:
                            take_o(0)
                        normalise(b, 0)
                        row_max(b, 2)
                        normalise(b, 1)
                        row_max(b, 3)
                        normalise(b, 2)
                        row_max(b, 4)
                        normalise(b, 3)
                        normalise(b, 4)
                    take_o(1)
                    st.leave(HEADS // 2)

            def merge(l, st):
                with loop(dve, 0, KD // 2) as i:
                    st.enter(i, 6)
                    for b in range(2):
                        k = ds(i * 2 + b, 1)
                        flat = lambda ap: ap[:, k].rearrange("p a t -> p (a t)")
                        for r in range(3):
                            n = 3 * b + r
                            dve.wait_ge(gate_sig, l * 24 + i * 6 + (n + 3))
                            dve.wait_ge(chunk_done, done_at(l, B_MERGE + 2 * n + 1) + i * 12)
                            dst = mlf[:, k].rearrange("p a (h t) -> p (a h) t", h=2) if r == 0 else two(stat[:, 2])
                            ins = tt(dst, two(stat[:, n % 2]), pair(2 * (n % 2) + 1), MUL)
                            follow(ins, merge_mul, l * 24 + i * 6 + (n + 3))
                            if r:
                                st.done(tt(flat(mlf), flat(mlf), stat[:, 2], ADD))
                        st.done(ts(flat(mh), flat(mlf), 1.0, None, MUL))
                        tt(flat(ml), flat(mlf), flat(mhf), SUB).then_inc(mix_done, 1)
                    st.leave(KD // 2)

            dve.sem_inc(hid_done, 2)
            dve.sem_inc(z_taken, 2)
            dve.sem_inc(conv_taken, 4)
            dve.sem_inc(merge_mul, 2)
            dve.sem_inc(o_done, 2)
            dve.memset(ones[:], 1.0).then_inc(ones_set, 1)
            dve.wait_ge(x_in, 16)
            dve.wait_ge(const_in, 16 * 5)
            for k in range(KD):
                ts(xh[:, k], z[:, k], 1.0, None, MUL).then_inc(first_hi, 1)
                dve.wait_ge(first_hi, k + 1)
                tt(xl[:, k], z[:, k], xhf[:, k], SUB).then_inc(x_ready, 1)
            with loop(dve, 0, DEPTH) as l:
                st = Steps(dve, dve_step, l, DVE_STEPS)
                s5_parameters(l, st)
                ffn(l, B_FFN1, 0, st)
                s5_tables(l, st)
                latent_sums(l, st)
                scan(l, st)
                st.done(dve.memset(conv_u[:, 0:2], 0.0))
                for m in range(MT):
                    conv_tile(l, m, st)
                latents(l, st)
                s5_outputs(l, st)
                heads(l, st)
                merge(l, st)
                layer_norm(l, 1, st, 1.0 / ALPHA, LN_EPS / ALPHA ** 2, lambda k: B_WO + k, 1)
                ffn(l, B_FFN2, 1, st)
                st.close()


ACT_STEPS, DVE_STEPS = 24, 487


_WEIGHTS = ("ffn1_w_gate", "ffn1_w_up", "ffn1_w_down", "w_in", "mla_w_uq", "mla_w_ukv", "mla_w_o", "conv_w_out",
            "s5_w_glu", "s5_w_out", "w_o", "ffn2_w_gate", "ffn2_w_up", "ffn2_w_down")


def _layout(inp):
    a = {n: np.ascontiguousarray(inp[n]) for n in _WEIGHTS}
    a["x_T"] = np.ascontiguousarray(np.concatenate([inp["meta"], inp["x"][0]], 0).T)
    tiles = lambda v: v.reshape(DEPTH, -1, P).transpose(0, 2, 1)
    cols = []
    for n in ("ln1", "ln2", "ln3"):
        cols += [tiles(inp[n + "_g"]), tiles(inp[n + "_b"])]
    cols += [tiles(inp["mla_q_norm_g"]), tiles(inp["mla_kv_norm_g"])]
    cols += [tiles(inp["conv_w"][:, j]) for j in range(CONV_K)] + [tiles(inp["conv_b"])]
    cols += [tiles(inp["s5_b_glu"]), tiles(inp["s5_d"].reshape(DEPTH, MIX))]
    a["par"] = np.ascontiguousarray(np.concatenate(cols, 2))

    def states(v):
        return v.reshape(DEPTH, PAIRS, 2, STATE).transpose(0, 2, 3, 1).reshape(DEPTH, P, PAIRS)

    log_dt = np.broadcast_to(inp["s5_log_dt"][:, :, None], (DEPTH, GROUPS, STATE))
    a["s5_par"] = np.ascontiguousarray(np.stack([states(v) for v in
                                                 (inp["s5_a_re"], inp["s5_a_im"], log_dt)], 2))

    def b_states(v):
        v = v.reshape(DEPTH, PAIRS, 2, STATE, GROUP)
        out = np.zeros((DEPTH, 2, STATE, PAIRS, 2, GROUP), v.dtype)
        for g in range(2):
            out[:, g, :, :, g] = v[:, :, g].transpose(0, 2, 1, 3)
        return out.reshape(DEPTH, P, PAIRS * 2 * GROUP)

    def b_own(v):
        return v.reshape(DEPTH, PAIRS, 2, STATE, GROUP).transpose(0, 2, 3, 1, 4).reshape(DEPTH, P, PAIRS * GROUP)

    for name, lay in (("s5_b", b_states), ("s5_b_own", b_own)):
        a[name] = np.ascontiguousarray(np.stack([lay(inp["s5_b_re"]), lay(inp["s5_b_im"])], 2))
    a["s5_c"] = np.ascontiguousarray(np.stack([b_states(inp[n].transpose(0, 1, 3, 2))
                                               for n in ("s5_c_re", "s5_c_im")], 2))
    a["c_ident"] = np.eye(P, dtype=np.float32)
    a["c_mask"] = np.triu(np.full((P, P), -1e30, np.float32), 1)
    inv_freq = np.float32(10000.0) ** (-np.arange(0, ROPE, 2, dtype=np.float32) / np.float32(ROPE))
    ang = inv_freq[:, None].astype(np.float32) * np.arange(L, dtype=np.float32)[None, :]
    a["c_cos"] = np.concatenate([np.cos(ang)] * 2, 0).astype(np.float32)
    a["c_sin"] = np.concatenate([-np.sin(ang), np.sin(ang)], 0).astype(np.float32)
    a["c_swap"] = np.roll(np.eye(ROPE, dtype=np.float32), ROPE // 2, 1)
    return a


def kernel(**inputs):
    import concourse.bacc as bacc
    from concourse.bass_utils import run_bass_kernel_spmd

    nc = bacc.Bacc("TRN2", target_bir_lowering=False, num_devices=1)
    arrays = _layout(inputs)
    t = {n: nc.dram_tensor(f"in_{n}", a.shape, mybir.dt.from_np(a.dtype), kind="ExternalInput").ap()
         for n, a in arrays.items()}
    t["out"] = nc.dram_tensor("out_T", (D_MODEL, SEQ), mybir.dt.float32, kind="ExternalOutput").ap()
    build(nc, t)
    r = run_bass_kernel_spmd(nc, [{f"in_{n}": a for n, a in arrays.items()}], core_ids=[0])
    return np.ascontiguousarray(r.results[0]["out_T"].T)[None]
```

```python
import numpy as np
import concourse.bass as bass
from concourse import mybir
from contextlib import ExitStack

P = 128
D_MODEL, SEQ, DEPTH, N_META = 1024, 512, 2, 16
L = SEQ + N_META
HALF = L // 2
MIX = D_MODEL // 2
HEADS, NOPE, ROPE, VDIM = 8, 64, 32, 64
QKD = NOPE + ROPE
QR, KVR = 3 * D_MODEL // 8, D_MODEL // 4
CONV_K = 3
GROUP, GROUPS, STATE = 16, 32, 64
D_FF = P * ((8 * D_MODEL // 3 + P - 1) // P)
ALPHA = (2.0 * DEPTH) ** 0.25
LN_EPS, RMS_EPS = 1e-5, 1e-6
KD, NF, MT = D_MODEL // P, D_FF // P, MIX // P
TC = 8
NC = L // TC
CL_EARLY = 3
HC = NC // 2
PAIRS = GROUPS // 2
QT = [(i * P, min(P, L - i * P)) for i in range((L + P - 1) // P)]
NQ = len(QT)
VREG = (NQ - 1) * P

C_CKV = QR
C_KR = QR + KVR
C_XBAR = C_KR + ROPE
C_B = C_XBAR + MIX
C_C = C_B + MIX
C_U = C_C + MIX
C_G = C_U + MIX
KR_AT = 64

SLOTS = 4
RAW = 2
TURN_AT = 6
AHEAD = SLOTS - 1
DOWN_CUT = [(0, 6), (6, 6), (12, 5), (17, 5)]
FFN_CH = 2 * NF + 4 * KD
B_FFN1 = 0
B_M1 = B_FFN1 + FFN_CH
N_M1 = 10
B_CONV = B_M1 + N_M1
B_V = B_CONV + 3 * MT
B_GLU = B_V + 2
B_HEAD = B_GLU + MT
B_MERGE = B_HEAD + 2 * HEADS
B_WO = B_MERGE + 6 * KD
B_FFN2 = B_WO + KD
CH = B_FFN2 + FFN_CH
assert CH % SLOTS == 0 and not (B_M1 | B_HEAD | B_MERGE | B_WO | B_FFN2) % SLOTS

ARENA_WORDS = 53100

PC_LN = 0
PC_QG, PC_KG = 48, 51
PC_CW, PC_CB = 53, 65
PC_GB, PC_D = 69, 73
PC_N = 77

TWO_PI_INV = float(np.float32(1 / (2 * np.pi)))
PI_A = 6.28125
PI_B = float(np.float32(np.round((2 * np.pi - PI_A) * 2 ** 20) / 2 ** 20))
PI_C = float(np.float32(2 * np.pi - PI_A - PI_B))
ROUND = 12582912.0
SIN_MAX = 3.1415925


class Steps:

    def __init__(self, eng, sem, layer, per_layer):
        self.eng, self.sem, self.base, self.per_layer = eng, sem, layer * per_layer, per_layer
        self.n, self.it, self.size, self.start = 0, None, 0, 0

    def done(self, ins):
        ins.then_inc(self.sem, 1)
        self.n += 1
        self.wait()

    def wait(self):
        at = self.base + self.n
        if self.it is not None:
            at = at + self.it * self.size
        self.eng.wait_ge(self.sem, at)

    def enter(self, it, size):
        self.it, self.size, self.start = it, size, self.n

    def leave(self, times):
        assert self.n - self.start == self.size, (self.n, self.start, self.size)
        self.n = self.start + self.size * times
        self.it = None

    def close(self):
        assert self.n == self.per_layer, (self.n, self.per_layer)


def build(nc, t):
    f32, f32r = mybir.dt.float32, mybir.dt.float32r
    ALU, ACT, AX = mybir.AluOpType, mybir.ActivationFunctionType, mybir.AxisListType
    ds = bass.ds

    ctx = ExitStack()
    with ctx:
        UNIT = L * 4
        base = (nc.sbuf_base + 31) // 32 * 32
        ctx.enter_context(nc.sbuf_tensor("arena", [P, ARENA_WORDS], f32))
        top = [base]

        def at(name, shape, dt, offset):
            return nc.alloc_sbuf_tensor_at(name, shape, dt, offset=offset)

        def new(name, shape, dt=f32):
            n = 4
            for s in shape[1:]:
                n *= s
            off = top[0]
            top[0] += (n + 31) // 32 * 32
            return at(name, shape, dt, off), off

        xh, _ = new("x_hi", [P, KD, L], f32r)
        xhf = xh.bitcast(f32)
        xl, o = new("x_lo", [P, KD, L], f32r)
        xlf = xl.bitcast(f32)
        w_raw, _ = new("w_raw", [P, RAW, 8 * P])
        w_hi, _ = new("w_hi", [P, SLOTS, 8 * P], f32r)
        w_lo, _ = new("w_lo", [P, SLOTS, 8 * P], f32r)
        M, m0 = new("mixer_region", [P, 52, L])
        U = lambda k: m0 + k * UNIT
        stat, stat_off = new("stat", [P, 5, L])
        ident, _ = new("ident", [P, P])
        ones, _ = new("ones", [P, P])
        mask, _ = new("mask", [P, P])
        rope_cos, _ = new("rope_cos", [P, L])
        rope_sin, _ = new("rope_sin", [P, L])
        swap, _ = new("swap", [P, ROPE])
        par, _ = new("par", [P, PC_N])
        s5lam, _ = new("s5_lambda", [P, 2, PAIRS])
        s5cf, _ = new("s5_coef", [P, 2, PAIRS])
        turn, _ = new("s5_turn", [P, 2, PAIRS])
        decay, _ = new("s5_decay", [P, PAIRS])
        bS, _ = new("s5_bbar_states", [P, 2, PAIRS * 2 * GROUP])
        kr, _ = new("k_rope", [P, L])
        eps_col, _ = new("ln_eps", [P, 1])
        unused_root, _ = new("unused_root", [P, 1])
        small, _ = new("softmax_cols", [P, 4, 2 * NQ])
        assert top[0] <= base + ARENA_WORDS * 4, top[0]

        gh = at("hid_hi", [P, NF, L], f32r, U(0))
        gl = at("hid_lo", [P, NF, L], f32r, U(NF))
        glf = at("hid_rest", [P, NF, L], f32, U(NF))
        silu = at("silu", [P, 2, L], f32, U(44))
        z = at("ln_in", [P, KD, L], f32, U(44))
        cqh = at("cq_hi", [P, 3, L], f32r, U(0))
        cql = at("cq_lo", [P, 3, L], f32r, U(3))
        cqf = at("cq_raw", [P, 3, L], f32, U(3))
        kvh = at("ckv_hi", [P, 2 * L + P], f32r, U(6))
        kvo = U(6) + (2 * L + P) * 4
        kvl = at("ckv_lo", [P, 2 * L + P], f32r, kvo)
        kvf = at("ckv_raw", [P, 2, L], f32, kvo)
        lfS = at("s5_in_states", [P, 2, PAIRS, GROUP, TC], f32, U(44))
        lfT = at("s5_in", [P, 2, PAIRS, P], f32, U(11))
        u8 = at("s5_u_stacked", [P, 8, MT, NC], f32, U(19))
        decays = at("s5_decays", [P, PAIRS, NC], f32, U(23))
        turns = [at(n, [P, PAIRS, NC], f32, U(k)) for n, k in (("s5_turns_re", 0), ("s5_turns_im", 6))]
        cl_tmp = [at(n, [P, 2, 512], f32, U(k)) for n, k in (("s5_tmp_a", 0), ("s5_tmp_b", 6))]
        cl = at("s5_out", [P, TC, 2, 512], f32, U(36))
        braw = at("s5_b_raw", [P, 2, 512], f32, U(31))
        bcomp = at("s5_b_own", [P, 2, PAIRS * GROUP], f32, U(33))
        craw = at("s5_c_raw", [P, 2, 512], f32, U(34))
        ug = at("s5_u", [P, TC, MT, NC], f32, U(27))
        X = at("s5_state", [P, 2, PAIRS, NC], f32, U(31))
        K = at("s5_toeplitz", [P, MT, TC, P], f32, U(19))
        yh = at("s5_y_hi", [P, MT, L], f32r, U(40))
        yl = at("s5_y_lo", [P, MT, L], f32r, U(44))
        zh = at("conv_hi", [P, MT, L], f32r, U(11))
        zl = at("conv_lo", [P, MT, L], f32r, U(15))
        zlf = at("conv_rest", [P, MT, L], f32, U(15))
        sh = at("s5_hi", [P, MT, L], f32r, U(19))
        sl = at("s5_lo", [P, MT, L], f32r, U(23))
        slf = at("s5_rest", [P, MT, L], f32, U(23))
        oh = at("att_hi", [P, MT, L], f32r, U(27))
        ol = at("att_lo", [P, MT, L], f32r, U(31))
        V = at("v", [P, NQ, HEADS * VDIM], f32, U(35))
        PT = at("probs_T", [P, NQ, L], f32, U(40))
        pr = at("probs", [P, 2, L], f32, U(45))
        qT = at("q", [P, 2, L], f32, U(47))
        kT = at("k", [P, 2, L], f32, U(49))
        vb = at("v_head", [P, 2, NQ, VDIM], f32, stat_off + 3 * UNIT)
        conv_u = at("conv_u", [P, L + 2], f32, stat_off + UNIT)
        mh = at("mix_hi", [P, KD, L], f32r, U(0))
        ml = at("mix_lo", [P, KD, L], f32r, U(36))
        mlf = at("mix_rest", [P, KD, L], f32, U(36))
        s5p = at("s5_params", [P, 12, PAIRS], f32, stat_off)
        tmp = at("s5_tmp", [P, 4, 512], f32, stat_off)

        ghf, yhf, ohf, mhf = (v.bitcast(f32) for v in (gh, yh, oh, mh))
        kvh3, kvl3 = (v[:, 0:2 * L].rearrange("p (k t) -> p k t", k=2) for v in (kvh, kvl))

        ps = ctx.enter_context(nc.psum_tensor("ps", [P, 8, 512], f32))
        pair = lambda k: ps[:, 2 * k:2 * k + 2, 0:HALF]
        two = lambda ap: ap.rearrange("p (h t) -> p h t", h=2)

        def sem(name):
            return ctx.enter_context(nc.semaphore(name))

        w_loaded = [sem(f"w_loaded{s}") for s in range(RAW)]
        w_rounded, w_split, chunk_done = sem("w_rounded"), sem("w_split"), sem("chunk_done")
        const_in, out_written, x_ready = sem("const_in"), sem("out_written"), sem("x_ready")
        tile_in = [sem(f"tile_in{k}") for k in range(KD)]
        par_in, s5p_in, b_in, c_in = sem("par_in"), sem("s5p_in"), sem("b_in"), sem("c_in")
        dve_step, act_step, passed = sem("dve_step"), sem("act_step"), sem("passed")
        silu_done, hid_done = sem("silu_done"), sem("hid_done")
        z_taken, ln_sums, ln_stat = sem("z_taken"), sem("ln_sums"), sem("ln_stat")
        ln_square = sem("ln_square")
        ln_var, ln_sd, ln_scaled, ln_hi = sem("ln_var"), sem("ln_sd"), sem("ln_scaled"), sem("ln_hi")
        dt_done, trig_in, trig_done, s5_half = sem("dt_done"), sem("trig_in"), sem("trig_done"), sem("s5_half")
        m1_taken, lf_ready, lf_turned, lf_taken, cl_ready, f_ready = (
            sem("m1_taken"), sem("lf_ready"), sem("lf_turned"), sem("lf_taken"), sem("cl_ready"), sem("f_ready"))
        u_stacked, rms_taken = sem("u_stacked"), sem("rms_taken")
        f_taken, scan_done, conv_taken, conv_hi, conv_done = (sem("f_taken"), sem("scan_done"), sem("conv_taken"),
                                                              sem("conv_hi_done"), sem("conv_done"))
        rms_sums, rms_stat, rms_sd, rms_scaled, rms_hi, lat_ready = (
            sem("rms_sums"), sem("rms_stat"), sem("rms_sd"), sem("rms_scaled"), sem("rms_hi"),
            sem("lat_ready"))
        k_zero, k_ready, k_taken, y_ready, y_taken, gelu_done, yh_done, y_split = (
            sem("k_zero"), sem("k_ready"), sem("k_taken"), sem("y_ready"), sem("y_taken"), sem("gelu_done"),
            sem("yh_done"), sem("y_split"))
        glu_sig, glu_out, glu_hi, glu_done = sem("glu_sig"), sem("glu_out"), sem("glu_hi"), sem("glu_done")
        kr_swap, kr_done, kr_set, v_taken = sem("kr_swap"), sem("kr_done"), sem("kr_set"), sem("v_taken")
        q_copied, k_copied, q_swap, q_ready, vb_done = (sem("q_copied"), sem("k_copied"), sem("q_swap"),
                                                        sem("q_ready"), sem("vb_done"))
        s_done, nb_ready, p_exp, p_ready, t_done, pt_done, pv_done, oh_done, o_done = (
            sem("s_done"), sem("nb_ready"), sem("p_exp"), sem("p_ready"), sem("t_done"), sem("pt_done"),
            sem("pv_done"), sem("oh_done"), sem("o_done"))
        gate_sig, merge_mul, mix_rest, mix_hi_done, mix_done = (sem("gate_sig"), sem("merge_mul"), sem("mix_rest_done"),
                                                                sem("mix_hi_done"), sem("mix_done"))
        ones_set, first_hi, swap_taken = sem("ones_set"), sem("first_hi"), sem("swap_taken")

        block = ctx.enter_context(nc.Block())

        def wait_apart(eng, s, value):
            eng.wait_ge(s, value)
            eng.sem_inc(passed, 1)

        def loop(eng, start, end):
            eng.sem_inc(passed, 1)
            return eng.Fori(start, end)

        def done_at(l, c):
            return l * CH + (c + 1 + SLOTS)

        @block.sync
        def _(sp):
            def load(l, c, it_chunks, ncols, src, k):
                wait_apart(sp, w_split, l * CH + it_chunks + (c + 1))
                dst = w_raw[:, c % RAW, 0:ncols].rearrange("p (k m) -> p k m", k=k)
                sp.dma_start(dst, src).then_inc(w_loaded[c % RAW], 16)

            def rows(w, l, r0, nk, c0, nm):
                return w[ds(l, 1), r0:r0 + nk * P, ds(c0, nm)].rearrange("a (k p) m -> p (a k) m", p=P)

            def ffn(l, b0, wg, wu, wd):
                with sp.Fori(0, NF // 2) as i:
                    for j in range(2):
                        for n, w in enumerate((wg, wu)):
                            load(l, b0 + 2 * j + n, i * 4, 8 * P, rows(w, l, 0, KD, (i * 2 + j) * P, P), KD)
                with sp.Fori(0, KD) as d:
                    for n, (r, nk) in enumerate(DOWN_CUT):
                        load(l, b0 + 2 * NF + n, d * 4, nk * P, rows(wd, l, r * P, nk, d * P, P), nk)

            sp.dma_start(z[:, 0], t["x_T"][0:P, :]).then_inc(tile_in[0], 16)
            with sp.Fori(0, DEPTH) as l:
                ffn(l, B_FFN1, t["ffn1_w_gate"], t["ffn1_w_up"], t["ffn1_w_down"])
                w_in = t["w_in"]
                cols = [C_U + P * k for k in range(MT)] + [P * k for k in range(5)] + [C_KR - KR_AT]
                for m in range(MT):
                    cols += [C_XBAR + P * m, C_C + P * m, C_B + P * m]
                for n, c0 in enumerate(cols):
                    load(l, B_M1 + n, 0, 8 * P, rows(w_in, l, 0, KD, c0, P), KD)
                w_v = t["mla_w_ukv"].rearrange("l r (h s d) -> l r h s d", h=HEADS, s=2)
                for k in range(2):
                    src = w_v[ds(l, 1), k * P:(k + 1) * P, :, 1, :].rearrange("a p h d -> (a p) h d")
                    load(l, B_V + k, 0, HEADS * VDIM, src, HEADS)
                for m in range(MT):
                    load(l, B_GLU + m, 0, MT * P, rows(t["s5_w_glu"], l, 0, MT, m * P, P), MT)
                with sp.Fori(0, HEADS // 2) as i:
                    for b in range(2):
                        h = i * 2 + b
                        load(l, B_HEAD + 2 * b, i * 4, 3 * QKD, rows(t["mla_w_uq"], l, 0, 3, h * QKD, QKD), 3)
                        load(l, B_HEAD + 2 * b + 1, i * 4, 2 * P, rows(t["mla_w_ukv"], l, 0, 2, h * P, P), 2)
                with sp.Fori(0, KD // 2) as i:
                    for b in range(2):
                        for r, w in enumerate(("mla_w_o", "conv_w_out", "s5_w_out")):
                            n = 6 * b + 2 * r
                            load(l, B_MERGE + n, i * 12, 8 * P,
                                 rows(w_in, l, 0, KD, (i * 2 + b) * P + (C_G + r * D_MODEL), P), KD)
                            load(l, B_MERGE + n + 1, i * 12, MT * P, rows(t[w], l, 0, MT, (i * 2 + b) * P, P), MT)
                with sp.Fori(0, KD // 4) as i:
                    for n in range(4):
                        load(l, B_WO + n, i * 4, 8 * P, rows(t["w_o"], l, 0, KD, (i * 4 + n) * P, P), KD)
                ffn(l, B_FFN2, t["ffn2_w_gate"], t["ffn2_w_up"], t["ffn2_w_down"])
            for c in range(AHEAD):
                load(DEPTH, c, 0, 8 * P, rows(t["ffn1_w_gate"], DEPTH - 1, 0, KD, c * P, P), KD)
            for k in range(KD):
                sp.wait_ge(x_ready, 3 * KD * DEPTH + k + 1)
                sp.dma_start(t["out"][k * P:(k + 1) * P, :], z[:, k, N_META:L]).then_inc(out_written, 16)
            sp.wait_ge(out_written, 16 * KD)

        @block.gpsimd
        def _(pool):
            pool.sem_inc(w_split, RAW)
            with pool.Fori(0, DEPTH * CH // SLOTS) as i:
                for s in range(SLOTS):
                    pool.wait_ge(w_rounded, i * SLOTS + (s + 1))
                    pool.tensor_tensor(w_lo[:, s], w_raw[:, s % RAW], w_hi[:, s].bitcast(f32),
                                       ALU.subtract).then_inc(w_split, 1)
            pool.wait_ge(w_rounded, DEPTH * CH + 1)
            pool.tensor_tensor(w_lo[:, 0], w_raw[:, 0], w_hi[:, 0].bitcast(f32), ALU.subtract).then_inc(w_split, 1)

        @block.tensor
        def _(pe):
            pe.sem_inc(chunk_done, SLOTS)
            pe.sem_inc(t_done, 2)

            def split_ready(l, c, it_chunks=0):
                pe.wait_ge(w_split, l * CH + it_chunks + (c + 1 + RAW))

            def product(out, c, k0, hi, lo, n_tiles, first, last, m=P, kp=P, x_wait=None):
                s = c % SLOTS
                for k in range(n_tiles):
                    if x_wait is not None:
                        pe.wait_ge(x_ready, x_wait + (k + 1))
                    cols = slice(k * m, (k + 1) * m)
                    parts = ((w_hi, hi), (w_hi, lo), (w_lo, hi))
                    for n, (w, x) in enumerate(parts):
                        for h in range(2):
                            ins = nc.tensor.matmul(out[0:m, h], w[:, s, cols], x[:, k0 + k, h * HALF:(h + 1) * HALF],
                                                   start=first and k == 0 and n == 0,
                                                   stop=last and k == n_tiles - 1 and n == 2)
                return ins

            def first_products(l, outs, c, hi, lo, ready, n0):
                for k in range(KD):
                    for j, out in enumerate(outs):
                        if k == 0:
                            split_ready(l, c + j)
                        if j == 0:
                            pe.wait_ge(ready, n0 + (k + 1))
                        for n, (w, x) in enumerate(((w_hi, hi), (w_hi, lo), (w_lo, hi))):
                            for h in range(2):
                                ins = nc.tensor.matmul(out[:, h], w[:, (c + j) % SLOTS, k * P:(k + 1) * P],
                                                       x[:, k, h * HALF:(h + 1) * HALF],
                                                       start=k == 0 and n == 0, stop=k == KD - 1 and n == 2)
                        if k == KD - 1:
                            ins.then_inc(chunk_done, 1)

            def sum_over_features(src, out, start=True, stop=True):
                for h in range(2):
                    ins = nc.tensor.matmul(out[:, h], ones[:], src[:, h * HALF:(h + 1) * HALF], start=start, stop=stop)
                return ins

            def layer_norm_middle(l, which):
                pe.wait_ge(ln_sums, (l * 3 + which) * 2 + 1)
                sum_over_features(stat[:, 1], pair(2)).then_inc(ln_stat, 1)

            def layer_norm_end(l, which):
                n = l * 3 + which
                pe.wait_ge(ln_sums, n * 2 + 2)
                sum_over_features(stat[:, 1], pair(2), stop=False)
                sum_over_features(stat[:, 2], pair(3), stop=False)
                pe.wait_ge(z_taken, n * KD + (KD + 2))
                sum_over_features(z[:, KD - 1], pair(2), start=False).then_inc(ln_stat, 1)
                pe.wait_ge(ln_square, n * 5 + 5)
                sum_over_features(stat[:, 4], pair(3), start=False).then_inc(ln_stat, 1)

            def ffn(l, b0, w):
                x0 = l * 24 + w * 16
                n0 = (l * 2 + w) * NF
                pe.wait_ge(silu_done, n0 + 2)
                pe.wait_ge(hid_done, n0 + 2)
                first_products(l, [pair(k) for k in range(3)], b0, xh, xl, x_ready, x0)
                split_ready(l, b0 + 3)
                product(pair(3), b0 + 3, 0, xh, xl, KD, True, True).then_inc(chunk_done, 1)
                with loop(pe, 1, NF // 2) as i:
                    n0 = (l * 2 + w) * NF + i * 2
                    for j in range(2):
                        c = b0 + 2 * j
                        split_ready(l, c, i * 4)
                        pe.wait_ge(silu_done, n0 + (j + 1))
                        product(pair(2 * j), c, 0, xh, xl, KD, True, True).then_inc(chunk_done, 1)
                        split_ready(l, c + 1, i * 4)
                        pe.wait_ge(hid_done, n0 + (j + 1))
                        product(pair(2 * j + 1), c + 1, 0, xh, xl, KD, True, True).then_inc(chunk_done, 1)
                pe.wait_ge(silu_done, (l * 2 + w) * NF + (NF + 1))
                for part in range(2):
                    with loop(pe, 0, 2) as i:
                        for b in range(2):
                            dd = part * 4 + b
                            pe.wait_ge(z_taken, (l * 3 + 2 * w) * KD + i * 2 + (dd + 1))
                            for n, (r, nk) in enumerate(DOWN_CUT):
                                c = b0 + 2 * NF + 4 * dd + n
                                split_ready(l, c, i * 8)
                                if part == 0 and b == 0 and r + nk > NF - 2:
                                    pe.wait_ge(hid_done, (l * 2 + w) * NF + (NF + 2))
                                product(pair(b), c, r, gh, gl, nk, n == 0, n == 3).then_inc(chunk_done, 1)
                    (layer_norm_middle, layer_norm_end)[part](l, 2 * w)

            def m1(l):
                pe.wait_ge(m1_taken, l * N_M1 + 3)
                first_products(l, [pair(k) for k in range(3)], B_M1, xh, xl, x_ready, l * 24 + 8)
                for n in range(3, N_M1):
                    c = B_M1 + n
                    if n == TURN_AT:
                        turn_inputs(l)
                    split_ready(l, c)
                    pe.wait_ge(m1_taken, l * N_M1 + (n + 1))
                    if n >= TURN_AT:
                        pe.wait_ge(lf_taken, l * 8 + 2 * (n - TURN_AT + 1))
                    product(pair(n % 4), c, 0, xh, xl, KD, True, True).then_inc(chunk_done, 1)

            def turn_inputs(l):
                pe.wait_ge(const_in, 16 * 5)
                pe.wait_ge(lf_ready, l + 1)
                for n in range(8):
                    bank = (2 * TURN_AT + n) % 8
                    if n % 2 == 0:
                        pe.wait_ge(m1_taken, l * N_M1 + (n // 2 + TURN_AT + 1))
                    for k in range(4):
                        ins = nc.tensor.transpose(ps[:, bank, k * P:(k + 1) * P],
                                                  lfS[:, n % 2, 4 * (n // 2) + k].rearrange("p h s -> p (h s)"),
                                                  ident[:])
                    ins.then_inc(lf_turned, 1)

            def latent_sums(l):
                for n in range(2):
                    pe.wait_ge(rms_sums, l * 2 + (n + 1))
                    pe.wait_ge(m1_taken, l * N_M1 + (N_M1 + 2 + n))
                    sum_over_features(stat[:, 3 + n], pair(2 + n)).then_inc(rms_stat, 1)
                wait_apart(pe, m1_taken, l * N_M1 + (N_M1 + 4))
                for h in range(2):
                    ins = nc.tensor.matmul(ps[64:96, 2 + h, 0:HALF], swap[64:96, :], kr[64:96, h * HALF:(h + 1) * HALF],
                                           start=True, stop=True)
                ins.then_inc(kr_swap, 1)

            def s5_states_in(l):
                pe.wait_ge(u_stacked, l * 128 + 128)
                for m in range(MT):
                    if m == 1:
                        pe.wait_ge(kr_done, l + 1)
                    if m == 2:
                        pe.wait_ge(rms_taken, l + 1)
                    for ri in range(2):
                        for q in range(4):
                            for g in range(2):
                                p = 4 * m + q
                                ins = nc.tensor.matmul(ps[64 * g:64 * g + 64, 2 * m + ri, q * NC:(q + 1) * NC],
                                                       lfT[:, ri, p, 64 * g:64 * g + 64], u8[:, 2 * q + g, m],
                                                       start=True, stop=True)
                    ins.then_inc(f_ready, 1)

            def conv(l):
                with loop(pe, 0, 3) as i:
                    for k in range(4):
                        split_ready(l, B_CONV + k, i * 4)
                        wait_apart(pe, f_taken, l * MT + (k + 1))
                        pe.wait_ge(conv_taken, l * 12 + i * 4 + (k + 1))
                        product(pair(k), B_CONV + k, 0, xh, xl, KD, True, True).then_inc(chunk_done, 1)

            def s5_toeplitz(l):
                pe.wait_ge(conv_taken, l * 12 + (12 + 4))
                pe.wait_ge(cl_ready, l + 1)
                for m in range(MT):
                    for q in range(4):
                        p = 4 * m + q
                        for ri in range(2):
                            ins = nc.tensor.matmul(ps[32 * q:32 * q + 32, m, 0:TC * 32],
                                                   bS[:, ri, p * 32:(p + 1) * 32],
                                                   cl[:, :, ri, p * 32:(p + 1) * 32],
                                                   start=ri == 0, stop=ri == 1)
                    ins.then_inc(k_ready, 1)

            def s5_outputs(l):
                pe.wait_ge(k_taken, l * PAIRS + PAIRS)
                pe.wait_ge(scan_done, l + 1)
                for m in range(MT):
                    a = 2 * (m % 2)
                    if m >= 2:
                        pe.wait_ge(y_taken, l * MT + (m - 1))
                    for j in range(TC):
                        for bank, (lo, up) in enumerate(((0, 4), (4, 8))):
                            s0 = max(j, lo)
                            if s0 >= up:
                                continue
                            nc.tensor.matmul(ps[:, a + bank, (s0 - lo) * NC:4 * NC], K[:, m, j, :],
                                             ug[:, s0 - j:up - j, m, :], start=j == 0, stop=False,
                                             skip_group_check=True)
                    for s in range(TC):
                        for ri in range(2):
                            for q in range(4):
                                p = 4 * m + q
                                ins = nc.tensor.matmul(
                                    ps[32 * q:32 * q + 32, a + s // 4, (s % 4) * NC:(s % 4 + 1) * NC],
                                    cl[:, s, ri, p * 32:(p + 1) * 32], X[:, ri, p, :],
                                    start=False, stop=ri == 1, skip_group_check=True)
                    ins.then_inc(y_ready, 1)

            def glu(l):
                pe.wait_ge(y_split, l * MT + MT)
                for m in range(MT):
                    c = B_GLU + m
                    split_ready(l, c)
                    if m == 0:
                        pe.wait_ge(v_taken, l * NQ + NQ)
                    product(pair(m), c, 0, yh, yl, MT, True, True).then_inc(chunk_done, 1)

            def values(l):
                pe.wait_ge(lat_ready, l * 5 + 5)
                pe.wait_ge(y_taken, l * MT + MT - 1)
                for k in range(2):
                    c = B_V + k
                    s = c % SLOTS
                    split_ready(l, c)
                    for i in range(NQ):
                        tok = slice(k * L + i * P, k * L + (i + 1) * P)
                        for n, (x, w) in enumerate(((kvh, w_hi), (kvl, w_hi), (kvh, w_lo))):
                            ins = nc.tensor.matmul(ps[:, (4 + i) % 8, :], x[:, tok], w[:, s, 0:HEADS * VDIM],
                                                   start=k == 0 and n == 0, stop=k == 1 and n == 2)
                    ins.then_inc(chunk_done, 1)

            def heads(l):
                def make_q(i, b):
                    c = B_HEAD + 2 * b
                    split_ready(l, c, i * 4)
                    pe.wait_ge(o_done, l * HEADS + i * 2 + (b + 1))
                    product(pair(3), c, 0, cqh, cql, 3, True, True, m=QKD).then_inc(chunk_done, 1)

                def make_k(i, b):
                    c = B_HEAD + 2 * b + 1
                    split_ready(l, c, i * 4)
                    pe.wait_ge(swap_taken, l * HEADS + i * 2 + (b + 1))
                    product(pair(3), c, 0, kvh3, kvl3, 2, True, True).then_inc(chunk_done, 1)

                def swap_q(i, b):
                    wait_apart(pe, q_copied, l * HEADS + i * 2 + (b + 1))
                    for h in range(2):
                        ins = nc.tensor.matmul(ps[64:96, 6 + h, 0:HALF], swap[64:96, :],
                                               qT[64:96, b, h * HALF:(h + 1) * HALF], start=True, stop=True)
                    ins.then_inc(q_swap, 1)

                def scores(h0, b, j):
                    q0, nq = QT[j]
                    if j == 0:
                        pe.wait_ge(q_ready, h0 + (b + 1))
                        pe.wait_ge(k_copied, h0 + (b + 1))
                    if j < NQ - 1:
                        ins = nc.tensor.matmul(ps[:, j, 0:q0 + P], qT[0:QKD, b, q0:q0 + nq],
                                               kT[0:QKD, b, 0:q0 + P], start=True, stop=True)
                    else:
                        for h in range(2):
                            ins = nc.tensor.matmul(ps[0:nq, h, 0:HALF], qT[0:QKD, b, q0:q0 + nq],
                                                   kT[0:QKD, b, h * HALF:(h + 1) * HALF], start=True, stop=True)
                    ins.then_inc(s_done, 1)

                def transposes(h0, b, j):
                    q0, nq = QT[j]
                    buf = (NQ * b + j) % 2
                    wait_apart(pe, p_ready, (h0 + b) * NQ + (j + 1))
                    wait_apart(pe, pt_done, (h0 + b) * NQ + (j + 1))
                    for k in range(j + 1):
                        k0, nk = QT[k]
                        if nk == P:
                            ins = nc.tensor.transpose(ps[:, 4 + buf, k * nq:(k + 1) * nq],
                                                      pr[0:nq, buf, k0:k0 + P], ident[0:nq, 0:nq])
                        else:
                            ins = nc.tensor.matmul(ps[0:nk, 4 + buf, k * nq:(k + 1) * nq],
                                                   pr[0:nq, buf, k0:k0 + nk], ident[0:nq, 0:nq],
                                                   start=True, stop=True)
                    ins.then_inc(t_done, 1)

                def values_sum(h0, b):
                    wait_apart(pe, pt_done, (h0 + b) * NQ + (NQ + 2))
                    wait_apart(pe, vb_done, h0 + (b + 1))
                    for half in range(2):
                        todo = [k for k in range(NQ) if QT[k][0] < (half + 1) * HALF]
                        for k in todo:
                            k0, nk = QT[k]
                            q0 = max(k0, half * HALF)
                            ins = nc.tensor.matmul(
                                ps[64 * b:64 * b + 64, 6 + half, q0 - half * HALF:HALF],
                                vb[0:nk, b, k, :], PT[0:nk, k, q0:(half + 1) * HALF],
                                start=k == 0, stop=k == todo[-1], skip_group_check=True)
                    ins.then_inc(pv_done, 1)

                def head(i, b, i_next, last=False):
                    h0, n0, n = l * HEADS + i * 2, l * HEADS + i_next * 2, 1 - b
                    transposes(h0, b, 0)
                    transposes(h0, b, 1)
                    scores(h0, b, 4)
                    if not last:
                        make_q(i_next, n)
                    transposes(h0, b, 2)
                    if not last:
                        swap_q(i_next, n)
                    transposes(h0, b, 3)
                    if not last:
                        make_k(i_next, n)
                    transposes(h0, b, 4)
                    if not last:
                        for j in range(4):
                            scores(n0, n, j)
                    values_sum(h0, b)

                pe.wait_ge(glu_sig, l * MT + MT)
                make_q(0, 0)
                swap_q(0, 0)
                make_k(0, 0)
                pe.wait_ge(kr_set, l + 1)
                for j in range(4):
                    scores(l * HEADS, 0, j)
                with loop(pe, 0, HEADS // 2 - 1) as i:
                    head(i, 0, i)
                    head(i, 1, i + 1)
                head(HEADS // 2 - 1, 0, HEADS // 2 - 1)
                head(HEADS // 2 - 1, 1, 0, last=True)

            def merge(l):
                pe.wait_ge(o_done, l * HEADS + (HEADS + 2))
                with loop(pe, 0, KD // 2) as i:
                    for b in range(2):
                        for r, (yhi, ylo) in enumerate(((oh, ol), (zh, zl), (sh, sl))):
                            n = 3 * b + r
                            c = B_MERGE + 2 * n
                            split_ready(l, c, i * 12)
                            pe.wait_ge(gate_sig, l * 24 + i * 6 + (n + 1))
                            product(pair(2 * (n % 2)), c, 0, xh, xl, KD, True, True).then_inc(chunk_done, 1)
                            split_ready(l, c + 1, i * 12)
                            pe.wait_ge(merge_mul, l * 24 + i * 6 + (n + 1))
                            product(pair(2 * (n % 2) + 1), c + 1, 0, yhi, ylo, MT, True, True).then_inc(chunk_done, 1)

            def w_o(l):
                pe.wait_ge(merge_mul, l * 24 + (3 * KD + 1))
                first_products(l, [pair(0), pair(1)], B_WO, mh, ml, mix_done, l * KD)
                for part in range(2):
                    for b in range(2 * (1 - part), 4):
                        c = B_WO + part * 4 + b
                        split_ready(l, c)
                        pe.wait_ge(z_taken, (l * 3 + 1) * KD + (part * 4 + b + 1))
                        product(pair(b % 2), c, 0, mh, ml, KD, True, True).then_inc(chunk_done, 1)
                    (layer_norm_middle, layer_norm_end)[part](l, 1)

            pe.wait_ge(ones_set, 1)
            with loop(pe, 0, DEPTH) as l:
                ffn(l, B_FFN1, 0)
                m1(l)
                latent_sums(l)
                s5_states_in(l)
                conv(l)
                s5_toeplitz(l)
                s5_outputs(l)
                values(l)
                glu(l)
                heads(l)
                merge(l)
                w_o(l)
                ffn(l, B_FFN2, 1)

        @block.scalar
        def _(act):
            def ACTV(out, in_, f=ACT.Copy, **kw):
                return nc.scalar.activation(out, in_, f, **kw)

            def round_ahead(l, c, per4=0, i=None):
                c += AHEAD
                v, free = l * (CH // RAW) + (c // RAW + 1), l * CH + (c + 1)
                if i is not None:
                    v, free = v + i * (per4 * SLOTS // RAW), free + i * (per4 * SLOTS)
                act.wait_ge(chunk_done, free)
                act.wait_ge(w_loaded[c % RAW], v * 16)
                ACTV(w_hi[:, c % SLOTS], w_raw[:, c % RAW]).then_inc(w_rounded, 1)

            def square(l, which, k):
                n = l * 3 + which
                act.wait_ge(z_taken, n * KD + (k + 3))
                ACTV(stat[:, 3 + k % 2], z[:, k], ACT.Square).then_inc(ln_square, 1)

            def layer_norm_end(l, which, st):
                n = l * 3 + which
                st.done(ACTV(unused_root[:], eps_col[:], ACT.Sqrt))
                act.wait_ge(ln_var, n + 1)
                ACTV(stat[:, 2], stat[:, 2], ACT.Sqrt, bias=eps_col[:, 0:1]).then_inc(ln_sd, 1)
                for k in range(KD):
                    act.wait_ge(ln_scaled, n * KD + (k + 1))
                    col = PC_LN + which * 16 + k
                    st.done(ACTV(z[:, k], z[:, k], ACT.Identity, scale=par[:, col:col + 1],
                                 bias=par[:, col + 8:col + 9]))
                    ACTV(xh[:, k], z[:, k]).then_inc(ln_hi, 1)

            def ffn(l, b0, w, st):
                with act.Fori(0, NF // 2) as i:
                    n0 = (l * 2 + w) * NF + i * 2
                    for j in range(2):
                        c = b0 + 2 * j
                        round_ahead(l, c, 1, i)
                        act.wait_ge(chunk_done, done_at(l, c) + i * 4)
                        act.wait_ge(hid_done, n0 + (j + 1))
                        ACTV(two(silu[:, j]), pair(2 * j), ACT.Silu).then_inc(silu_done, 1)
                        round_ahead(l, c + 1, 1, i)
                if w == 0:
                    act.wait_ge(s5p_in, l * 16 + 16)
                    ACTV(s5p[:, 2], s5p[:, 2], ACT.Exp).then_inc(dt_done, 1)
                    act.wait_ge(trig_in, l + 1)
                    ACTV(s5p[:, 3], s5p[:, 3], ACT.Exp)
                    ACTV(s5p[:, 6], s5p[:, 4], ACT.Sin)
                    ACTV(s5p[:, 7], s5p[:, 4], ACT.Sin, scale=0.5).then_inc(trig_done, 1)
                    act.wait_ge(par_in, l * 16 + 16)
                b1 = b0 + 2 * NF
                with act.Fori(0, KD // 2) as d:
                    for n in range(4):
                        round_ahead(l, b1 + n, 1, d)
                for k in range(KD // 2, KD):
                    for n in range(4):
                        round_ahead(l, b1 + 4 * k + n)
                        if n == 0:
                            square(l, 2 * w, k - 1)
                square(l, 2 * w, KD - 1)
                layer_norm_end(l, 2 * w, st)

            act.sem_inc(silu_done, 2)
            act.sem_inc(gate_sig, 2)
            act.sem_inc(m1_taken, 4)
            act.sem_inc(pt_done, 2)
            for k in range(1, KD):
                act.dma_start(z[:, k], t["x_T"][k * P:(k + 1) * P, :]).then_inc(tile_in[k], 16)
            for dst, name in ((ident[:], "c_ident"), (mask[:], "c_mask"), (rope_cos[64:96, :], "c_cos"),
                              (rope_sin[64:96, :], "c_sin"), (swap[64:96, :], "c_swap")):
                act.dma_start(dst, t[name]).then_inc(const_in, 16)

            for c in range(AHEAD):
                round_ahead(0, c - AHEAD)
            with act.Fori(0, DEPTH) as l:
                st = Steps(act, act_step, l, ACT_STEPS)
                act.wait_ge(x_ready, l * 24 + 8)
                act.dma_start(par[:], t["par"][ds(l, 1)].rearrange("a p c -> (a p) c")).then_inc(par_in, 16)
                act.dma_start(s5p[:, 0:3], t["s5_par"][ds(l, 1)].rearrange("a p k c -> (a p) k c")).then_inc(s5p_in, 16)
                ffn(l, B_FFN1, 0, st)

                act.wait_ge(x_ready, l * 24 + 16)
                for dst, name, done in ((braw, "s5_b", b_in), (bcomp, "s5_b_own", b_in), (craw, "s5_c", c_in)):
                    act.dma_start(dst[:], t[name][ds(l, 1)].rearrange("a p k c -> (a p) k c")).then_inc(done, 16)
                for n in range(N_M1):
                    c = B_M1 + n
                    if n == MT:
                        wait_apart(act, m1_taken, l * N_M1 + (MT + 4))
                        for qg in range(8):
                            act.dma_start(u8[:, qg].rearrange("p m c -> p (m c)"),
                                          ug[GROUP * qg:GROUP * (qg + 1)].rearrange("h s m c -> h s (m c)")
                                          ).then_inc(u_stacked, 16)
                    if n == TURN_AT:
                        for k in range(8):
                            act.wait_ge(lf_turned, l * 8 + (k + 1))
                            ACTV(lfT[:, k % 2, 4 * (k // 2):4 * (k // 2) + 4],
                                 ps[:, (2 * TURN_AT + k) % 8, :].rearrange("p (q n) -> p q n", q=4)
                                 ).then_inc(lf_taken, 1)
                    round_ahead(l, c)
                    act.wait_ge(chunk_done, done_at(l, c))
                    src = pair(n % 4)
                    if n < MT:
                        for h in range(2):
                            out = ug[:, :, n, h * HC:(h + 1) * HC]
                            ins = ACTV(out, src[:, h].rearrange("p (c s) -> p s c", s=TC))
                        ins.then_inc(m1_taken, 1)
                    elif n < MT + 3:
                        ACTV(two(cqf[:, n - MT]), src).then_inc(m1_taken, 1)
                    elif n < MT + 5:
                        ACTV(two(kvf[:, n - MT - 3]), src).then_inc(m1_taken, 1)
                    else:
                        ACTV(two(kr[64:96]), src[64:96]).then_inc(m1_taken, 1)
                act.wait_ge(rms_taken, l + 1)
                ACTV(stat[:, 3:5], stat[:, 3:5], ACT.Sqrt).then_inc(rms_sd, 1)
                for n in range(3 * MT):
                    round_ahead(l, B_CONV + n)
                wait_apart(act, k_zero, l + 1)
                for m in range(MT):
                    act.wait_ge(k_ready, l * MT + (m + 1))
                    for q in range(4):
                        r = slice(32 * q, 32 * q + 32)
                        ACTV(K[r, m, :, r], ps[r, m, 0:TC * 32].rearrange("p (j o) -> p j o", j=TC)).then_inc(k_taken, 1)
                for m in range(MT):
                    act.wait_ge(y_taken, l * MT + (m + 1))
                    ACTV(ug[:, :, m], ug[:, :, m], ACT.Gelu_apprx_tanh).then_inc(gelu_done, 1)
                for b in range(2):
                    ins = ACTV(kT[64:96, b], kr[64:96])
                ins.then_inc(kr_set, 1)
                for k in range(2):
                    round_ahead(l, B_V + k)
                act.wait_ge(chunk_done, done_at(l, B_V + 1))
                for k in range(NQ):
                    ACTV(V[:, k], ps[:, (4 + k) % 8, :]).then_inc(v_taken, 1)
                for m in range(MT):
                    round_ahead(l, B_GLU + m)
                    act.wait_ge(chunk_done, done_at(l, B_GLU + m))
                    if m >= 2:
                        act.wait_ge(glu_out, l * MT + (m - 1))
                    ACTV(two(stat[:, 2 + m % 2]), pair(m), ACT.Sigmoid,
                         bias=par[:, PC_GB + m:PC_GB + m + 1]).then_inc(glu_sig, 1)
                wait_apart(act, glu_done, l * MT + MT)

                def take_q(i, b):
                    c = B_HEAD + 2 * b
                    act.wait_ge(chunk_done, done_at(l, c) + i * 4)
                    ACTV(two(qT[0:QKD, b]), pair(3)[0:QKD]).then_inc(q_copied, 1)

                def take_k(i, b):
                    c = B_HEAD + 2 * b + 1
                    act.wait_ge(chunk_done, done_at(l, c) + i * 4)
                    ACTV(two(kT[0:NOPE, b]), pair(3)[0:NOPE]).then_inc(k_copied, 1)

                def take_v(i, b):
                    ACTV(vb[:, b], V[:, :, ds((i * 2 + b) * VDIM, VDIM)]).then_inc(vb_done, 1)

                def exps(i, b, j):
                    n, buf = (l * HEADS + i * 2 + b) * NQ + (j + 1), (NQ * b + j) % 2
                    q0, nq = QT[j]
                    act.wait_ge(nb_ready, n)
                    act.wait_ge(t_done, n)
                    col = NQ * b + j
                    src, dst = (ps[:, j, 0:q0 + P], pr[:, buf, 0:q0 + P]) if nq == P else (
                        pair(0)[0:nq], two(pr[0:nq, buf]))
                    ACTV(dst, src, ACT.Exp, scale=QKD ** -0.5, bias=small[0:nq, 1, col:col + 1],
                         accum_out=small[0:nq, 2, col:col + 1]).then_inc(p_exp, 1)

                def copy_t(i, b, j):
                    n, bank = (l * HEADS + i * 2 + b) * NQ + (j + 3), 4 + (NQ * b + j) % 2
                    q0, nq = QT[j]
                    act.wait_ge(t_done, n)
                    if nq == P:
                        ins = ACTV(PT[:, 0:j + 1, q0:q0 + P],
                                   ps[:, bank, 0:(j + 1) * P].rearrange("p (k q) -> p k q", q=P))
                    else:
                        ACTV(PT[:, 0:j, q0:q0 + nq], ps[:, bank, 0:j * nq].rearrange("p (k q) -> p k q", q=nq))
                        ins = ACTV(PT[0:nq, j, q0:q0 + nq], ps[0:nq, bank, j * nq:(j + 1) * nq])
                    ins.then_inc(pt_done, 1)

                def take_o(i, b):
                    wait_apart(act, pv_done, l * HEADS + i * 2 + (b + 1))
                    ACTV(oh[64 * b:64 * b + 64, ds(i, 1)].rearrange("p a (h t) -> p (a h) t", h=2),
                         pair(3)[64 * b:64 * b + 64]).then_inc(oh_done, 1)

                def head(i, b, i_next, i_after=None):
                    copy_t(i, b, 0)
                    exps(i, b, 2)
                    copy_t(i, b, 1)
                    exps(i, b, 3)
                    if i_next is not None:
                        take_q(i_next, 1 - b)
                    exps(i, b, 4)
                    copy_t(i, b, 2)
                    if i_next is not None:
                        round_ahead(l, B_HEAD + 2 * (1 - b) + 1, 1, i_next)
                    copy_t(i, b, 3)
                    if i_next is not None:
                        take_k(i_next, 1 - b)
                    copy_t(i, b, 4)
                    if i_next is not None:
                        take_v(i_next, 1 - b)
                        exps(i_next, 1 - b, 0)
                        exps(i_next, 1 - b, 1)
                    if i_after is not None:
                        round_ahead(l, B_HEAD + 2 * b, 1, i_after)
                    take_o(i, b)

                round_ahead(l, B_HEAD)
                take_q(0, 0)
                round_ahead(l, B_HEAD + 1)
                take_k(0, 0)
                wait_apart(act, v_taken, l * NQ + NQ)
                take_v(0, 0)
                exps(0, 0, 0)
                exps(0, 0, 1)
                round_ahead(l, B_HEAD + 2)
                with act.Fori(0, HEADS // 2 - 1) as i:
                    head(i, 0, i, i + 1)
                    head(i, 1, i + 1, i + 1)
                head(HEADS // 2 - 1, 0, HEADS // 2 - 1)
                head(HEADS // 2 - 1, 1, None)

                with act.Fori(0, KD // 2) as i:
                    for n in range(6):
                        c = B_MERGE + 2 * n
                        round_ahead(l, c, 3, i)
                        act.wait_ge(chunk_done, done_at(l, c) + i * 12)
                        act.wait_ge(merge_mul, l * 24 + i * 6 + (n + 1))
                        ACTV(two(stat[:, n % 2]), pair(2 * (n % 2)), ACT.Sigmoid).then_inc(gate_sig, 1)
                        round_ahead(l, c + 1, 3, i)
                for n in range(KD):
                    round_ahead(l, B_WO + n)
                    if n >= KD // 2:
                        square(l, 1, n - 1)
                square(l, 1, KD - 1)
                layer_norm_end(l, 1, st)
                ffn(l, B_FFN2, 1, st)
                st.close()

        @block.vector
        def _(dve):
            tt, ts, stt = nc.vector.tensor_tensor, nc.vector.tensor_scalar, nc.vector.scalar_tensor_tensor
            MUL, ADD, SUB = ALU.mult, ALU.add, ALU.subtract

            def follow(ins, s, value):
                ins.then_inc(s, 1)
                dve.wait_ge(s, value)

            def split_tile(st, hi, lo, rest, after=None):
                st.done(ts(hi, rest, 1.0, None, MUL))
                return tt(lo, rest, hi.bitcast(f32), SUB)

            def layer_norm(l, which, st, scale, last_chunk):
                n = l * 3 + which

                def take(k):
                    dve.wait_ge(chunk_done, done_at(l, last_chunk(k)))
                    ins = stt(two(z[:, k]), pair(k % 2), scale, two(z[:, k]), MUL, ADD)
                    follow(ins, z_taken, n * KD + (k + 3))

                for k in range(KD):
                    ins = tt(z[:, k], xhf[:, k], xlf[:, k], ADD)
                st.done(ins)
                take(0)
                take(1)
                st.done(tt(stat[:, 1], z[:, 0], z[:, 1], ADD))
                take(2)
                tt(stat[:, 1], stat[:, 1], z[:, 2], ADD).then_inc(ln_sums, 1)
                dve.wait_ge(ln_stat, n * 3 + 1)
                st.done(ts(two(stat[:, 0]), pair(2), 1.0 / (3 * P), None, MUL))
                st.done(tt(z[:, 3], z[:, 3], stat[:, 0], SUB))
                take(3)
                dev = lambda k: tt(z[:, k], z[:, k], stat[:, 0], SUB)
                square_of = lambda k, out: st.done(tt(out, z[:, k], z[:, k], MUL))
                add_sum = lambda k: tt(stat[:, 1], stat[:, 1], z[:, k], ADD)
                for k in (4, 0, 1, 2):
                    dev(k)
                st.done(stt(stat[:, 1], stat[:, 0], -3.0, stat[:, 1], MUL, ADD))
                add_sum(3)
                square_of(0, stat[:, 2])
                for k in range(3, KD - 1):
                    if k > 3:
                        take(k)
                        for j in {4: (5,), 5: (6, 7)}.get(k, ()):
                            dev(j)
                        add_sum(k)
                    dve.wait_ge(ln_square, n * 5 + (k - 2))
                    ins = tt(stat[:, 2], stat[:, 2], stat[:, 3 + k % 2], ADD)
                    if k < KD - 2:
                        st.done(ins)
                    if k in (4, 5):
                        square_of(k - 3, stat[:, 3 + (k + 1) % 2])
                        st.done(tt(stat[:, 2], stat[:, 2], stat[:, 3 + (k + 1) % 2], ADD))
                ins.then_inc(ln_sums, 1)
                take(KD - 1)
                dve.wait_ge(ln_stat, n * 3 + 2)
                st.done(ts(two(stat[:, 0]), pair(2), 1.0 / D_MODEL, None, MUL))
                st.done(tt(stat[:, 3], stat[:, 0], stat[:, 0], MUL))
                dve.wait_ge(ln_stat, n * 3 + 3)
                stt(two(stat[:, 2]), pair(3), 1.0 / D_MODEL, two(stat[:, 3]), MUL, SUB).then_inc(ln_var, 1)
                for k in range(2):
                    dev(k)
                dve.wait_ge(ln_sd, n + 1)
                st.done(nc.vector.reciprocal(stat[:, 1], stat[:, 2]))
                for k in range(KD + 1):
                    if k < KD:
                        tt(z[:, k], z[:, k], stat[:, 1], MUL).then_inc(ln_scaled, 1)
                    if k:
                        dve.wait_ge(ln_hi, n * KD + k)
                        tt(xl[:, k - 1], z[:, k - 1], xhf[:, k - 1], SUB).then_inc(x_ready, 1)
                    if k + 2 < KD:
                        st.done(dev(k + 2))

            def ffn(l, b0, w, st):
                with loop(dve, 0, NF // 2) as i:
                    st.enter(i, 4)
                    n0 = (l * 2 + w) * NF + i * 2
                    for j in range(2):
                        f = ds(i * 2 + j, 1)
                        flat = lambda ap: ap[:, f].rearrange("p a t -> p (a t)")
                        dve.wait_ge(silu_done, n0 + (j + 3))
                        dve.wait_ge(chunk_done, done_at(l, b0 + 2 * j + 1) + i * 4)
                        st.done(tt(glf[:, f].rearrange("p a (h t) -> p (a h) t", h=2), two(silu[:, j]),
                                   pair(2 * j + 1), MUL))
                        st.done(ts(flat(gh), flat(glf), 1.0, None, MUL))
                        tt(flat(gl), flat(glf), flat(ghf), SUB).then_inc(hid_done, 1)
                    st.leave(NF // 2)
                if w == 0:
                    s5_parameters(l, st)
                layer_norm(l, 2 * w, st, 0.5 / ALPHA, lambda k: b0 + 2 * NF + 4 * k + 3)

            def s5_parameters(l, st):
                q = lambda k: s5p[:, k]
                dve.wait_ge(dt_done, l + 1)
                tt(q(3), q(2), q(0), MUL)
                st.done(tt(q(4), q(2), q(1), MUL))
                st.done(ts(q(5), q(4), TWO_PI_INV, ROUND, MUL, ADD))
                st.done(ts(q(5), q(5), ROUND, None, SUB))
                for c in (PI_A, PI_B, PI_C):
                    st.done(stt(q(4), q(5), -c, q(4), MUL, ADD))
                ts(q(4), q(4), SIN_MAX, -SIN_MAX, ALU.min, ALU.max).then_inc(trig_in, 1)
                dve.wait_ge(trig_done, l + 1)
                st.done(tt(q(7), q(7), q(7), MUL))
                st.done(ts(q(7), q(7), -2.0, 1.0, MUL, ADD))
                tt(s5lam[:, 0], q(3), q(7), MUL)
                tt(s5lam[:, 1], q(3), q(6), MUL)
                mag, re, im = q(3), q(7), q(6)
                for k in range(3):
                    tt(q(8), re, re, MUL)
                    tt(q(9), im, im, MUL)
                    st.done(tt(q(10), re, im, MUL))
                    re, im, up = turn[:, 0], turn[:, 1], decay[:]
                    tt(up, mag, mag, MUL)
                    tt(re, q(8), q(9), SUB)
                    st.done(ts(im, q(10), 2.0, None, MUL))
                    mag = up
                tt(q(8), re, re, MUL)
                st.done(tt(q(9), im, im, MUL))
                st.done(tt(q(8), q(8), q(9), ADD))
                st.done(ts(q(8), q(8), -0.5, 1.5, MUL, ADD))
                tt(re, re, q(8), MUL)
                st.done(tt(im, im, q(8), MUL))
                tt(q(5), q(0), q(0), MUL)
                st.done(tt(q(8), q(1), q(1), MUL))
                st.done(tt(q(5), q(5), q(8), ADD))
                nc.vector.reciprocal(q(5), q(5))
                st.done(ts(q(8), s5lam[:, 0], -1.0, None, ADD))
                tt(q(3), q(8), q(0), MUL)
                tt(q(4), s5lam[:, 1], q(1), MUL)
                tt(q(6), s5lam[:, 1], q(0), MUL)
                st.done(tt(q(7), q(8), q(1), MUL))
                tt(q(3), q(3), q(4), ADD)
                st.done(tt(q(6), q(6), q(7), SUB))
                tt(s5cf[:, 0], q(3), q(5), MUL)
                tt(s5cf[:, 1], q(6), q(5), MUL)
                st.done(ts(q(11), q(8), 1.0, None, MUL))

            def s5_tables(l, st):
                def cmul(out, ar, ai, br, bi, op_r, op_i, n):
                    p4 = [tmp[:, k, 0:PAIRS * n].rearrange("p (q h) -> p q h", q=PAIRS) for k in range(4)]
                    tt(p4[0], ar, br, MUL)
                    tt(p4[1], ai, bi, MUL)
                    tt(p4[2], ar, bi, MUL)
                    st.done(tt(p4[3], ai, br, MUL))
                    flat = len(out[0].shape) == 2
                    f = (lambda ap: ap.rearrange("p q h -> p (q h)")) if flat else (lambda ap: ap)
                    tt(out[0], f(p4[0]), f(p4[1]), op_r)
                    st.done(tt(out[1], f(p4[2]), f(p4[3]), op_i))

                def each(ap, n):
                    return ap.unsqueeze(2).to_broadcast([P, PAIRS, n])

                block = ("p (q h) -> p q h", dict(q=PAIRS))
                as_ = lambda ap: ap.rearrange(block[0], **block[1])
                own = lambda ap: ap[:, 0:PAIRS * GROUP].rearrange("p (q h) -> p q h", q=PAIRS)
                dve.wait_ge(b_in, l * 32 + 32)
                cmul([bcomp[:, 0], bcomp[:, 1]], each(s5cf[:, 0], GROUP), each(s5cf[:, 1], GROUP), own(bcomp[:, 0]),
                     own(bcomp[:, 1]), SUB, ADD, GROUP)
                for j in range(TC):
                    br, bi = (own(bcomp[:, n]) if j == 0 else lfS[:, n, :, :, TC - j] for n in range(2))
                    cmul([lfS[:, n, :, :, TC - 1 - j] for n in range(2)], each(s5lam[:, 0], GROUP),
                         each(s5lam[:, 1], GROUP), br, bi, SUB, ADD, GROUP)
                dve.sem_inc(lf_ready, 1)
                cmul([bS[:, 0], bS[:, 1]], each(s5cf[:, 0], 32), each(s5cf[:, 1], 32), as_(braw[:, 0]),
                     as_(braw[:, 1]), SUB, ADD, 32)
                wr, wi = turns
                dve.memset(wr[:, :, 0:1], 1.0)
                dve.memset(wi[:, :, 0:1], 0.0)
                dve.memset(decays[:, :, 0:1], 0.0)
                ts(decays[:, :, 1:NC], decay[:].unsqueeze(2).to_broadcast([P, PAIRS, NC - 1]), 1.0, None, MUL)
                for n in range(2):
                    ins = ts(turns[n][:, :, 1], turn[:, n], 1.0, None, MUL)
                st.done(ins)
                k = 1
                while k < NC - 1:
                    w = min(k, NC - 1 - k)
                    wk = [v[:, :, k:k + 1].to_broadcast([P, PAIRS, w]) for v in turns]
                    cmul([v[:, :, k + 1:k + 1 + w] for v in turns], wk[0], wk[1], wr[:, :, 1:1 + w],
                         wi[:, :, 1:1 + w], SUB, ADD, w)
                    k += w
                dve.wait_ge(c_in, l * 16 + 16)
                dve.wait_ge(lf_turned, l * 8 + 8)
                ts(cl[:, 0, 0], craw[:, 0], 1.0, None, MUL)
                st.done(ts(cl[:, 0, 1], craw[:, 1], -1.0, None, MUL))
                for j in range(1, CL_EARLY):
                    cl_step(j, [tmp[:, k] for k in range(4)], st)

            def cl_step(j, tmps, st):
                as_ = lambda ap: ap.rearrange("p (q h) -> p q h", q=PAIRS)
                lr, li = (s5lam[:, n].unsqueeze(2).to_broadcast([P, PAIRS, 32]) for n in range(2))
                br, bi = (as_(cl[:, j - 1, n]) for n in range(2))
                for dst, a, b in zip(tmps, (lr, li, lr, li), (br, bi, bi, br)):
                    ins = tt(as_(dst), a, b, MUL)
                st.done(ins)
                tt(cl[:, j, 0], tmps[0], tmps[1], ADD)
                st.done(tt(cl[:, j, 1], tmps[2], tmps[3], SUB))

            def conv_tile(l, m, st):
                n0 = 3 * m

                def there(n):
                    dve.wait_ge(chunk_done, done_at(l, B_CONV + n0 + n))
                    return pair((n0 + n) % 4)

                def taken(ins, n):
                    follow(ins, conv_taken, l * 12 + (n0 + n + 5))

                taken(ts(two(stat[:, 0]), there(0), 1.0, None, MUL), 0)
                taken(tt(two(conv_u[:, 2:]), two(stat[:, 0]), there(1), MUL), 1)
                tap = lambda j: par[:, PC_CW + 4 * j + m:PC_CW + 4 * j + m + 1]
                st.done(ts(stat[:, 0], conv_u[:, 2:], tap(2), par[:, PC_CB + m:PC_CB + m + 1], MUL, ADD))
                for j in (1, 0):
                    st.done(stt(stat[:, 0], conv_u[:, j:j + L], tap(j), stat[:, 0], MUL, ADD))
                taken(tt(two(zlf[:, m]), two(stat[:, 0]), there(2), MUL), 2)
                split_tile(st, zh[:, m], zl[:, m], zlf[:, m]).then_inc(conv_done, 1)

            def scan(l, st):
                st.done(dve.memset(X[:, :, :, 0:1].rearrange("p r q c -> p (r q) c"), 0.0))
                N = NC - 1
                t2 = [stat[:, n, 0:4 * N].rearrange("p (q c) -> p q c", q=4) for n in range(2)]
                for m in range(MT):
                    dve.wait_ge(f_ready, l * MT + (m + 1))
                    fr, fi = (ps[:, 2 * m + n, 0:4 * NC].rearrange("p (q c) -> p q c", q=4)[:, :, 0:N] for n in range(2))
                    wr, wi = (v[:, 4 * m:4 * m + 4, 1:NC] for v in turns)
                    gr, gi = (X[:, n, 4 * m:4 * m + 4, 1:NC] for n in range(2))
                    tt(gr, fr, wr, MUL)
                    tt(t2[0], fi, wi, MUL)
                    tt(gi, fi, wr, MUL)
                    follow(tt(t2[1], fr, wi, MUL), f_taken, l * MT + (m + 1))
                    tt(gr, gr, t2[0], ADD)
                    ins = tt(gi, gi, t2[1], SUB)
                    st.done(ins)
                for n in range(2):
                    y = X[:, n].rearrange("p q c -> p (q c)")
                    ins = nc.vector.tensor_tensor_scan(y, decays[:].rearrange("p q c -> p (q c)"), y, 0.0, MUL, ADD)
                st.done(ins)
                for m in range(MT):
                    a, b, c, d = (stat[:, n // 2, n % 2 * HALF:(n % 2 + 1) * HALF] for n in range(4))
                    wr, wi = (v[:, 4 * m:4 * m + 4].rearrange("p q c -> p (q c)") for v in turns)
                    yr, yi = (X[:, n, 4 * m:4 * m + 4].rearrange("p q c -> p (q c)") for n in range(2))
                    tt(a, yr, wr, MUL)
                    tt(b, yi, wi, MUL)
                    tt(c, yr, wi, MUL)
                    st.done(tt(d, yi, wr, MUL))
                    tt(yr, a, b, SUB)
                    ins = tt(yi, c, d, ADD)
                    if m < MT - 1:
                        st.done(ins)
                follow(ins, scan_done, l + 1)
                dve.memset(K[:], 0.0).then_inc(k_zero, 1)

            def latent_sums(l, st):
                for n, (src, k1, m0_) in enumerate(((cqf, 3, MT), (kvf, 2, MT + 3))):
                    for k in range(k1):
                        dve.wait_ge(m1_taken, l * N_M1 + (m0_ + k + 5))
                        dst = stat[:, 3 + n] if k == 0 else stat[:, 0]
                        ins = tt(dst, src[:, k], src[:, k], MUL)
                        if k:
                            st.done(ins)
                            ins = tt(stat[:, 3 + n], stat[:, 3 + n], stat[:, 0], ADD)
                        if k < k1 - 1:
                            st.done(ins)
                    ins.then_inc(rms_sums, 1)
                dve.wait_ge(kr_swap, l + 1)
                tt(two(stat[64:96, 0]), ps[64:96, 2:4, 0:HALF], two(rope_sin[64:96]), MUL)
                st.done(tt(kr[64:96], kr[64:96], rope_cos[64:96], MUL))
                follow(tt(kr[64:96], kr[64:96], stat[64:96, 0], ADD), kr_done, l + 1)
                dve.wait_ge(rms_stat, l * 2 + 2)
                for n, width in enumerate((QR, KVR)):
                    ins = ts(two(stat[:, 3 + n]), pair(2 + n), 1.0 / width, RMS_EPS, MUL, ADD)
                ins.then_inc(rms_taken, 1)

            def latents_begin(l, st):
                for v in (kvh, kvl):
                    dve.memset(v[:, 2 * L:2 * L + P].bitcast(f32), 0.0)
                dve.wait_ge(rms_sd, l + 1)
                for n in range(2):
                    ins = nc.vector.reciprocal(stat[:, 3 + n], stat[:, 3 + n])
                st.done(ins)

            def latent_tiles(l, n, st):
                src, hi, lo, k1, col = ((cqf, cqh, cql, 3, PC_QG), (kvf, kvh3, kvl3, 2, PC_KG))[n]
                for k in range(k1):
                    g = par[:, col + k:col + k + 1]
                    st.done(tt(src[:, k], src[:, k], stat[:, 3 + n], MUL))
                    st.done(ts(hi[:, k], src[:, k], g, None, MUL))
                    stt(lo[:, k], src[:, k], g, hi[:, k].bitcast(f32), MUL, SUB).then_inc(lat_ready, 1)

            def s5_outputs(l, st):
                for m in range(MT):
                    dve.wait_ge(y_ready, l * MT + (m + 1))
                    half = lambda ap: ap.rearrange("p (h s) c -> p h s c", h=2)
                    stt(half(ug[:, :, m]), half(ug[:, :, m]), par[:, PC_D + m:PC_D + m + 1],
                        ps[:, 2 * (m % 2):2 * (m % 2) + 2, 0:HALF].rearrange("p h (s c) -> p h s c", s=TC // 2),
                        MUL, ADD).then_inc(y_taken, 1)
                tok = lambda ap: ap.rearrange("p (c s) -> p c s", s=TC)
                for m in range(MT):
                    dve.wait_ge(gelu_done, l * MT + (m + 1))
                    gelu = ug[:, :, m].rearrange("p s c -> p c s")
                    st.done(ts(tok(yh[:, m]), gelu, 1.0, None, MUL))
                    tt(tok(yl[:, m]), gelu, tok(yhf[:, m]), SUB).then_inc(y_split, 1)
                for m in range(MT):
                    dve.wait_ge(glu_sig, l * MT + (m + 1))
                    gelu = ug[:, :, m].rearrange("p s c -> p c s")
                    follow(tt(tok(slf[:, m]), gelu, tok(stat[:, 2 + m % 2]), MUL), glu_out, l * MT + (m + 1))
                    split_tile(st, sh[:, m], sl[:, m], slf[:, m]).then_inc(glu_done, 1)

            def heads(l, st):
                scale = QKD ** -0.5
                at_head = lambda i, b: l * HEADS + i * 2 + b

                def rope_q(i, b):
                    dve.wait_ge(q_swap, at_head(i, b) + 1)
                    tt(two(stat[64:96, 1 + b]), ps[64:96, 6:8, 0:HALF], two(rope_sin[64:96]),
                       MUL).then_inc(swap_taken, 1)
                    st.done(tt(qT[64:96, b], qT[64:96, b], rope_cos[64:96], MUL))
                    tt(qT[64:96, b], qT[64:96, b], stat[64:96, 1 + b], ADD).then_inc(q_ready, 1)

                def row_max(i, b, j):
                    q0, nq = QT[j]
                    col = NQ * b + j
                    dve.wait_ge(s_done, at_head(i, b) * NQ + (j + 1))
                    if nq == P:
                        diag, row, ax = ps[:, j, q0:q0 + P], ps[:, j, 0:q0 + P], AX.X
                    else:
                        diag, row, ax = ps[0:nq, 1, q0 - HALF:L - HALF], pair(0)[0:nq], AX.XY
                    st.done(tt(diag, diag, mask[0:nq, 0:nq], ADD))
                    st.done(nc.vector.tensor_reduce(small[0:nq, 0, col:col + 1], row, ax, ALU.max))
                    ts(small[0:nq, 1, col:col + 1], small[0:nq, 0, col:col + 1], -scale, None,
                       MUL).then_inc(nb_ready, 1)

                def normalise(i, b, j):
                    q0, nq = QT[j]
                    col, buf = NQ * b + j, (NQ * b + j) % 2
                    dve.wait_ge(p_exp, at_head(i, b) * NQ + (j + 1))
                    st.done(nc.vector.reciprocal(small[0:nq, 3, col:col + 1], small[0:nq, 2, col:col + 1]))
                    n = q0 + nq
                    ts(pr[0:nq, buf, 0:n], pr[0:nq, buf, 0:n], small[0:nq, 3, col:col + 1], None,
                       MUL).then_inc(p_ready, 1)

                def take_o(i, b):
                    dve.wait_ge(oh_done, at_head(i, b) + 1)
                    rows = slice(64 * b, 64 * b + 64)
                    view = lambda ap: ap[rows, ds(i, 1)].rearrange("p a (h t) -> p (a h) t", h=2)
                    tt(view(ol), pair(3)[rows], view(ohf), SUB).then_inc(o_done, 1)

                def begin(i, b):
                    row_max(i, b, 0)
                    row_max(i, b, 1)
                    normalise(i, b, 0)
                    row_max(i, b, 2)
                    normalise(i, b, 1)
                    row_max(i, b, 3)

                def head(i, b, i_next, last=False):
                    normalise(i, b, 2)
                    row_max(i, b, 4)
                    normalise(i, b, 3)
                    if not last:
                        rope_q(i_next, 1 - b)
                    normalise(i, b, 4)
                    if not last:
                        begin(i_next, 1 - b)
                    take_o(i, b)

                rope_q(0, 0)
                begin(0, 0)
                with loop(dve, 0, HEADS // 2 - 1) as i:
                    st.enter(i, 32)
                    head(i, 0, i)
                    head(i, 1, i + 1)
                    st.leave(HEADS // 2 - 1)
                head(HEADS // 2 - 1, 0, HEADS // 2 - 1)
                head(HEADS // 2 - 1, 1, 0, last=True)

            def merge(l, st):
                with loop(dve, 0, KD // 2) as i:
                    st.enter(i, 6)
                    for b in range(2):
                        k = ds(i * 2 + b, 1)
                        flat = lambda ap: ap[:, k].rearrange("p a t -> p (a t)")
                        for r in range(3):
                            n = 3 * b + r
                            dve.wait_ge(gate_sig, l * 24 + i * 6 + (n + 3))
                            dve.wait_ge(chunk_done, done_at(l, B_MERGE + 2 * n + 1) + i * 12)
                            dst = mlf[:, k].rearrange("p a (h t) -> p (a h) t", h=2) if r == 0 else two(stat[:, 2])
                            ins = tt(dst, two(stat[:, n % 2]), pair(2 * (n % 2) + 1), MUL)
                            follow(ins, merge_mul, l * 24 + i * 6 + (n + 3))
                            if r:
                                st.done(tt(flat(mlf), flat(mlf), stat[:, 2], ADD))
                        st.done(ts(flat(mh), flat(mlf), 1.0, None, MUL))
                        tt(flat(ml), flat(mlf), flat(mhf), SUB).then_inc(mix_done, 1)
                    st.leave(KD // 2)

            dve.sem_inc(hid_done, 2)
            dve.sem_inc(z_taken, 2)
            dve.sem_inc(conv_taken, 4)
            dve.sem_inc(merge_mul, 2)
            dve.sem_inc(o_done, 2)
            dve.memset(eps_col[:], LN_EPS / ALPHA ** 2)
            dve.memset(ones[:], 1.0).then_inc(ones_set, 1)
            for k in range(KD):
                dve.wait_ge(tile_in[k], 16)
                ts(xh[:, k], z[:, k], 1.0, None, MUL).then_inc(first_hi, 1)
                dve.wait_ge(first_hi, k + 1)
                tt(xl[:, k], z[:, k], xhf[:, k], SUB).then_inc(x_ready, 1)
            dve.wait_ge(const_in, 16 * 5)
            with loop(dve, 0, DEPTH) as l:
                st = Steps(dve, dve_step, l, DVE_STEPS)
                ffn(l, B_FFN1, 0, st)
                s5_tables(l, st)
                latent_sums(l, st)
                scan(l, st)
                st.done(dve.memset(conv_u[:, 0:2], 0.0))
                late_tmp = [cl_tmp[k // 2][:, k % 2] for k in range(4)]
                for m in range(3):
                    conv_tile(l, m, st)
                    for j in range(CL_EARLY + 2 * m, min(TC, CL_EARLY + 2 * m + 2)):
                        cl_step(j, late_tmp, st)
                dve.sem_inc(cl_ready, 1)
                conv_tile(l, 3, st)
                latents_begin(l, st)
                latent_tiles(l, 0, st)
                latent_tiles(l, 1, st)
                s5_outputs(l, st)
                heads(l, st)
                merge(l, st)
                layer_norm(l, 1, st, 1.0 / ALPHA, lambda k: B_WO + k)
                ffn(l, B_FFN2, 1, st)
                st.close()


ACT_STEPS, DVE_STEPS = 27, 436


_WEIGHTS = ("ffn1_w_gate", "ffn1_w_up", "ffn1_w_down", "w_in", "mla_w_uq", "mla_w_ukv", "mla_w_o", "conv_w_out",
            "s5_w_glu", "s5_w_out", "w_o", "ffn2_w_gate", "ffn2_w_up", "ffn2_w_down")


def _layout(inp):
    a = {n: np.ascontiguousarray(inp[n]) for n in _WEIGHTS}
    a["x_T"] = np.ascontiguousarray(np.concatenate([inp["meta"], inp["x"][0]], 0).T)
    tiles = lambda v: v.reshape(DEPTH, -1, P).transpose(0, 2, 1)
    cols = []
    for n in ("ln1", "ln2", "ln3"):
        cols += [tiles(inp[n + "_g"]), tiles(inp[n + "_b"])]
    cols += [tiles(inp["mla_q_norm_g"]), tiles(inp["mla_kv_norm_g"])]
    cols += [tiles(inp["conv_w"][:, j]) for j in range(CONV_K)] + [tiles(inp["conv_b"])]
    cols += [tiles(inp["s5_b_glu"]), tiles(inp["s5_d"].reshape(DEPTH, MIX))]
    a["par"] = np.ascontiguousarray(np.concatenate(cols, 2))

    def states(v):
        return v.reshape(DEPTH, PAIRS, 2, STATE).transpose(0, 2, 3, 1).reshape(DEPTH, P, PAIRS)

    log_dt = np.broadcast_to(inp["s5_log_dt"][:, :, None], (DEPTH, GROUPS, STATE))
    a["s5_par"] = np.ascontiguousarray(np.stack([states(v) for v in
                                                 (inp["s5_a_re"], inp["s5_a_im"], log_dt)], 2))

    def b_states(v):
        v = v.reshape(DEPTH, PAIRS, 2, STATE, GROUP)
        out = np.zeros((DEPTH, 2, STATE, PAIRS, 2, GROUP), v.dtype)
        for g in range(2):
            out[:, g, :, :, g] = v[:, :, g].transpose(0, 2, 1, 3)
        return out.reshape(DEPTH, P, PAIRS * 2 * GROUP)

    def b_own(v):
        return v.reshape(DEPTH, PAIRS, 2, STATE, GROUP).transpose(0, 2, 3, 1, 4).reshape(DEPTH, P, PAIRS * GROUP)

    for name, lay in (("s5_b", b_states), ("s5_b_own", b_own)):
        a[name] = np.ascontiguousarray(np.stack([lay(inp["s5_b_re"]), lay(inp["s5_b_im"])], 2))
    a["s5_c"] = np.ascontiguousarray(np.stack([b_states(inp[n].transpose(0, 1, 3, 2))
                                               for n in ("s5_c_re", "s5_c_im")], 2))
    a["c_ident"] = np.eye(P, dtype=np.float32)
    a["c_mask"] = np.triu(np.full((P, P), -1e30, np.float32), 1)
    inv_freq = np.float32(10000.0) ** (-np.arange(0, ROPE, 2, dtype=np.float32) / np.float32(ROPE))
    ang = inv_freq[:, None].astype(np.float32) * np.arange(L, dtype=np.float32)[None, :]
    a["c_cos"] = np.concatenate([np.cos(ang)] * 2, 0).astype(np.float32)
    a["c_sin"] = np.concatenate([-np.sin(ang), np.sin(ang)], 0).astype(np.float32)
    a["c_swap"] = np.roll(np.eye(ROPE, dtype=np.float32), ROPE // 2, 1)
    return a


def kernel(**inputs):
    import concourse.bacc as bacc
    from concourse.bass_utils import run_bass_kernel_spmd

    nc = bacc.Bacc("TRN2", target_bir_lowering=False, num_devices=1)
    arrays = _layout(inputs)
    t = {n: nc.dram_tensor(f"in_{n}", a.shape, mybir.dt.from_np(a.dtype), kind="ExternalInput").ap()
         for n, a in arrays.items()}
    t["out"] = nc.dram_tensor("out_T", (D_MODEL, SEQ), mybir.dt.float32, kind="ExternalOutput").ap()
    build(nc, t)
    r = run_bass_kernel_spmd(nc, [{f"in_{n}": a for n, a in arrays.items()}], core_ids=[0])
    return np.ascontiguousarray(r.results[0]["out_T"].T)[None]
```
